# Optimizing a Trainium2 kernel written in Bass

```python
import math
import jax, jax.numpy as jnp
from jax import lax
import numpy as np

D_MODEL = 1024
BATCH = 1
SEQ = 1024
DEPTH = 1

RET_HEADS = 4
RET_DK = 128
RET_DV = 128
RET_CHUNK = 128
ROPE_BASE = 10000.0
GDN_HEADS = 4
GDN_DK = 128
GDN_DV = 128
GDN_CHUNK = 64
CONV_K = 4
NSA_HEADS = 8
NSA_GROUPS = 2
NSA_HPG = NSA_HEADS // NSA_GROUPS
NSA_DK = 64
CMP_LEN = 32
CMP_STRIDE = 16
CMP_HIDDEN = 128
SLC_BLOCK = 64
N_SEL = 8
SLC_Q_CHUNK = 64
WIN = 256
WIN_BLOCK = 128
PLE_DIM = 256
ALPHA = (2 * DEPTH) ** 0.25
BETA_INIT = (8 * DEPTH) ** -0.25
NEG = -1e30
BIG = 1e30
EPS = 1e-6

RET_QK = RET_HEADS * RET_DK
RET_V = RET_HEADS * RET_DV
GDN_QKV = GDN_HEADS * (2 * GDN_DK + GDN_DV)
GDN_V = GDN_HEADS * GDN_DV
NSA_Q = NSA_HEADS * NSA_DK
NSA_KV = NSA_GROUPS * NSA_DK
IN_SPLITS = (RET_QK, RET_QK, RET_V, RET_V,
             GDN_QKV, GDN_HEADS, GDN_HEADS, GDN_V,
             NSA_Q, NSA_KV, NSA_KV, NSA_KV, NSA_KV, NSA_KV, NSA_KV, 3 * NSA_HEADS, NSA_Q,
             3 * D_MODEL)
D_IN = sum(IN_SPLITS)

kernel_name = 'hybrid_retention_gdn_nsa_deepnorm'

def _split(h, sizes):
    idx = np.cumsum(np.array(sizes))[:-1].tolist()
    return jnp.split(h, idx, axis=-1)

def _layer_norm(x, g, b):
    xf = x.astype(jnp.float32)
    mu = xf.mean(-1, keepdims=True)
    var = jnp.square(xf - mu).mean(-1, keepdims=True)
    return ((xf - mu) * lax.rsqrt(var + 1e-5) * g.astype(jnp.float32) + b.astype(jnp.float32)).astype(x.dtype)

def _group_norm(o):
    mu = o.mean(-1, keepdims=True)
    var = jnp.square(o - mu).mean(-1, keepdims=True)
    return (o - mu) * lax.rsqrt(var + 1e-5)

def _rms_norm(o, w):
    return o * lax.rsqrt(jnp.square(o).mean(-1, keepdims=True) + EPS) * w.astype(jnp.float32)

def _l2norm(x):
    return x * lax.rsqrt(jnp.sum(jnp.square(x), -1, keepdims=True) + EPS)

def _rotary(x):
    s, d = x.shape[1], x.shape[-1]
    inv = ROPE_BASE ** (-jnp.arange(0, d, 2, dtype=jnp.float32) / d)
    ang = jnp.arange(s, dtype=jnp.float32)[:, None] * inv[None, :]
    cos = jnp.cos(ang)[None, :, None, :]
    sin = jnp.sin(ang)[None, :, None, :]
    x1, x2 = x[..., 0::2], x[..., 1::2]
    return jnp.stack([x1 * cos - x2 * sin, x1 * sin + x2 * cos], axis=-1).reshape(x.shape)

def _retention(q, k, v):
    B, S, H, dk = q.shape
    dv = v.shape[-1]
    C = RET_CHUNK
    n = S // C
    q = _rotary(q.astype(jnp.float32))
    k = _rotary(k.astype(jnp.float32)) * dk ** -0.5
    v = v.astype(jnp.float32)
    log_g = jnp.log1p(-jnp.exp2(-5.0 - jnp.arange(H, dtype=jnp.float32)))
    qc = q.reshape(B, n, C, H, dk)
    kc = k.reshape(B, n, C, H, dk)
    vc = v.reshape(B, n, C, H, dv)
    pos = jnp.arange(C, dtype=jnp.float32)
    diff = pos[:, None] - pos[None, :]
    causal = diff >= 0
    dmask = jnp.where(causal[None], jnp.exp(jnp.where(causal, diff, 0.0)[None] * log_g[:, None, None]), 0.0)
    scores = jnp.einsum('bnihd,bnjhd->bnhij', qc, kc) * dmask
    o_intra = jnp.einsum('bnhij,bnjhe->bnihe', scores, vc)
    k_dec = kc * jnp.exp((C - 1 - pos)[:, None] * log_g[None, :])[None, None, :, :, None]
    kv = jnp.einsum('bnjhd,bnjhe->nbhde', k_dec, vc)
    chunk_decay = jnp.exp(C * log_g)[None, :, None, None]

    def step(R, kv_c):
        return chunk_decay * R + kv_c, R

    _, R_prev = lax.scan(step, jnp.zeros((B, H, dk, dv), jnp.float32), kv)
    q_dec = qc * jnp.exp((pos + 1.0)[:, None] * log_g[None, :])[None, None, :, :, None]
    o_inter = jnp.einsum('bnihd,nbhde->bnihe', q_dec, R_prev)
    return (o_intra + o_inter).reshape(B, S, H, dv)

def _causal_conv(x, w):
    c = x.shape[-1]
    return lax.conv_general_dilated(x, w[:, None, :], window_strides=(1,), padding=((CONV_K - 1, 0),),
                                    dimension_numbers=('NWC', 'WIO', 'NWC'), feature_group_count=c)

def _gated_delta_net(q, k, v, beta, g):
    B, S, H, dk = q.shape
    dv = v.shape[-1]
    C = GDN_CHUNK
    n = S // C
    q = _l2norm(q.astype(jnp.float32)) * dk ** -0.5
    k = _l2norm(k.astype(jnp.float32))
    v = v.astype(jnp.float32)

    def chunks(t):
        return t.reshape(B, n, C, H, -1).transpose(0, 3, 1, 2, 4)

    qc, kc, vc = chunks(q), chunks(k), chunks(v)
    bc = beta.reshape(B, n, C, H).transpose(0, 3, 1, 2)
    gc = jnp.cumsum(g.reshape(B, n, C, H).transpose(0, 3, 1, 2), axis=-1)
    ii = jnp.arange(C)[:, None]
    jj = jnp.arange(C)[None, :]
    incl = ii >= jj
    strict = ii > jj
    diff = gc[..., :, None] - gc[..., None, :]
    decay = jnp.where(incl, jnp.exp(jnp.where(incl, diff, 0.0)), 0.0)
    kk = jnp.einsum('bhnid,bhnjd->bhnij', kc, kc)
    a_mat = jnp.where(strict, bc[..., :, None] * kk * decay, 0.0) + jnp.eye(C, dtype=jnp.float32)
    rhs = jnp.concatenate([vc * bc[..., None], kc * (bc * jnp.exp(gc))[..., None]], axis=-1)
    sol = lax.linalg.triangular_solve(a_mat, rhs, left_side=True, lower=True, unit_diagonal=True)
    u, w = sol[..., :dv], sol[..., dv:]
    attn = jnp.einsum('bhnid,bhnjd->bhnij', qc, kc) * decay
    q_dec = qc * jnp.exp(gc)[..., None]
    g_last = gc[..., -1]
    k_dec = kc * jnp.exp(g_last[..., None] - gc)[..., None]
    xs = tuple(jnp.moveaxis(t, 2, 0) for t in (u, w, q_dec, k_dec, attn, g_last))

    def step(state, inp):
        u_c, w_c, q_c, k_c, a_c, gl = inp
        v_new = u_c - jnp.einsum('bhcd,bhde->bhce', w_c, state)
        o_c = jnp.einsum('bhcd,bhde->bhce', q_c, state) + jnp.einsum('bhij,bhje->bhie', a_c, v_new)
        state = state * jnp.exp(gl)[..., None, None] + jnp.einsum('bhcd,bhce->bhde', k_c, v_new)
        return state, o_c

    _, o = lax.scan(step, jnp.zeros((B, H, dk, dv), jnp.float32), xs)
    return o.transpose(1, 0, 3, 2, 4).reshape(B, S, H, dv)

def _nsa(q, k_c, v_c, k_s, v_s, k_w, v_w, gate_logits, pe_k, pe_v, w1k, w2k, w1v, w2v):
    B, S = q.shape[:2]
    G, HPG, dk = NSA_GROUPS, NSA_HPG, NSA_DK
    scale = dk ** -0.5
    qg = q.reshape(B, S, G, HPG, dk)
    kv4 = lambda t: t.reshape(B, S, G, dk)
    k_c, v_c, k_s, v_s, k_w, v_w = map(kv4, (k_c, v_c, k_s, v_s, k_w, v_w))
    t_pos = jnp.arange(S)

    n_cmp = (S - CMP_LEN) // CMP_STRIDE + 1
    blk_idx = jnp.arange(n_cmp)[:, None] * CMP_STRIDE + jnp.arange(CMP_LEN)[None, :]

    def compress(t, pe, w1, w2):
        blocks = t[:, blk_idx] + pe[None, None, :, None, :]
        flat = blocks.transpose(0, 1, 3, 2, 4).reshape(B, n_cmp, G, CMP_LEN * dk)
        return jax.nn.gelu(flat @ w1) @ w2

    kc_b = compress(k_c, pe_k, w1k, w2k)
    vc_b = compress(v_c, pe_v, w1v, w2v)
    s_cmp = jnp.einsum('bsghd,bcgd->bghsc', qg, kc_b).astype(jnp.float32) * scale
    cmp_end = jnp.arange(n_cmp) * CMP_STRIDE + CMP_LEN - 1
    cmp_mask = cmp_end[None, :] <= t_pos[:, None]
    p_cmp = jnp.where(cmp_mask, jax.nn.softmax(jnp.where(cmp_mask, s_cmp, NEG), axis=-1), 0.0)
    o_cmp = jnp.einsum('bghsc,bcgd->bsghd', p_cmp.astype(vc_b.dtype), vc_b)

    n_slc = S // SLC_BLOCK
    ci = jnp.arange(n_cmp)[:, None] * CMP_STRIDE
    sj = jnp.arange(n_slc)[None, :] * SLC_BLOCK
    overlap = ((ci < sj + SLC_BLOCK) & (ci + CMP_LEN > sj)).astype(jnp.float32)
    imp = jnp.einsum('bghsc,cj->bgsj', p_cmp, overlap)
    cur = t_pos // SLC_BLOCK
    jb = jnp.arange(n_slc)[None, :]
    forced = (jb == 0) | (jb == cur[:, None]) | (jb == cur[:, None] - 1)
    valid = jb <= cur[:, None]
    rank = jnp.where(valid[None, None], jnp.where(forced[None, None], BIG, imp), -BIG)
    n_sel = min(N_SEL, n_slc)
    _, sel = lax.top_k(rank, n_sel)
    ks_blk = k_s.reshape(B, n_slc, SLC_BLOCK, G, dk).transpose(0, 3, 1, 2, 4)
    vs_blk = v_s.reshape(B, n_slc, SLC_BLOCK, G, dk).transpose(0, 3, 1, 2, 4)
    QC = SLC_Q_CHUNK
    n_qc = S // QC
    bi = jnp.arange(B)[:, None, None, None]
    gi = jnp.arange(G)[None, :, None, None]

    def sel_chunk(args):
        q_c, sel_c, t_c = args
        k_g = ks_blk[bi, gi, sel_c]
        v_g = vs_blk[bi, gi, sel_c]
        s = jnp.einsum('bgqhd,bgqnld->bghqnl', q_c, k_g).astype(jnp.float32) * scale
        pos = sel_c[..., None] * SLC_BLOCK + jnp.arange(SLC_BLOCK)
        m = (pos <= t_c[None, None, :, None, None])[:, :, None]
        s = jnp.where(m, s, NEG).reshape(B, G, HPG, QC, n_sel * SLC_BLOCK)
        pr = jax.nn.softmax(s, axis=-1).reshape(B, G, HPG, QC, n_sel, SLC_BLOCK)
        return jnp.einsum('bghqnl,bgqnld->bqghd', pr.astype(v_g.dtype), v_g)

    q_chunks = qg.reshape(B, n_qc, QC, G, HPG, dk).transpose(1, 0, 3, 2, 4, 5)
    sel_chunks = sel.reshape(B, G, n_qc, QC, n_sel).transpose(2, 0, 1, 3, 4)
    t_chunks = t_pos.reshape(n_qc, QC)
    o_slc = lax.map(sel_chunk, (q_chunks, sel_chunks, t_chunks))
    o_slc = o_slc.transpose(1, 0, 2, 3, 4, 5).reshape(B, S, G, HPG, dk)

    WB = WIN_BLOCK
    nb = S // WB
    nw = WIN // WB

    def windows(t):
        tp = jnp.pad(t, ((0, 0), (WIN, 0), (0, 0), (0, 0)))
        tb = tp.reshape(B, nb + nw, WB, G, dk)
        return jnp.concatenate([tb[:, i:i + nb] for i in range(nw + 1)], axis=2)

    kwin = windows(k_w)
    vwin = windows(v_w)
    qb = qg.reshape(B, nb, WB, G, HPG, dk)
    s_w = jnp.einsum('bnqghd,bnkgd->bnghqk', qb, kwin).astype(jnp.float32) * scale
    qpos = jnp.arange(nb)[:, None] * WB + jnp.arange(WB)[None, :]
    kpos = (jnp.arange(nb)[:, None] - nw) * WB + jnp.arange((nw + 1) * WB)[None, :]
    dq = qpos[:, :, None] - kpos[:, None, :]
    wmask = (dq >= 0) & (dq < WIN) & (kpos[:, None, :] >= 0)
    p_w = jax.nn.softmax(jnp.where(wmask[None, :, None, None], s_w, NEG), axis=-1)
    o_win = jnp.einsum('bnghqk,bnkgd->bnqghd', p_w.astype(vwin.dtype), vwin).reshape(B, S, G, HPG, dk)

    gts = jax.nn.sigmoid(gate_logits).reshape(B, S, G, HPG, 3)
    o = gts[..., 0:1] * o_cmp + gts[..., 1:2] * o_slc + gts[..., 2:3] * o_win
    return o.reshape(B, S, NSA_HEADS * dk)

def _layer(x, p_i, w_in, conv_w, a_log, dt_bias, gdn_norm_w, pe_k, pe_v, w1k, w2k, w1v, w2v,
           w_br_a, w_br_b, w_br_c, w_out, ln_g, ln_b, w_ple, w_ple_gate):
    B, S, _ = x.shape
    h = x @ w_in
    (ra_q, ra_k, ra_v, ra_z, gd_qkv, gd_beta, gd_a, gd_z,
     ns_q, ns_kc, ns_vc, ns_ks, ns_vs, ns_kw, ns_vw, ns_gate, ns_z, merge) = _split(h, IN_SPLITS)

    ret = _retention(ra_q.reshape(B, S, RET_HEADS, RET_DK), ra_k.reshape(B, S, RET_HEADS, RET_DK),
                     ra_v.reshape(B, S, RET_HEADS, RET_DV))
    o_a = _group_norm(ret).reshape(B, S, RET_V).astype(x.dtype) * jax.nn.silu(ra_z)

    qkv = jax.nn.silu(_causal_conv(gd_qkv, conv_w))
    gq, gk, gv = _split(qkv, (GDN_HEADS * GDN_DK, GDN_HEADS * GDN_DK, GDN_V))
    beta = jax.nn.sigmoid(gd_beta.astype(jnp.float32))
    g = -jnp.exp(a_log.astype(jnp.float32)) * jax.nn.softplus((gd_a + dt_bias).astype(jnp.float32))
    gdn = _gated_delta_net(gq.reshape(B, S, GDN_HEADS, GDN_DK), gk.reshape(B, S, GDN_HEADS, GDN_DK),
                           gv.reshape(B, S, GDN_HEADS, GDN_DV), beta, g)
    o_b = _rms_norm(gdn, gdn_norm_w).reshape(B, S, GDN_V).astype(x.dtype) * jax.nn.silu(gd_z)

    o_c = _nsa(ns_q, ns_kc, ns_vc, ns_ks, ns_vs, ns_kw, ns_vw, ns_gate,
               pe_k, pe_v, w1k, w2k, w1v, w2v) * jax.nn.silu(ns_z)

    g_a, g_b, g_c = jnp.split(jax.nn.sigmoid(merge), 3, axis=-1)
    mixed = g_a * (o_a @ w_br_a) + g_b * (o_b @ w_br_b) + g_c * (o_c @ w_br_c)
    sub = mixed @ w_out

    ple = jax.nn.sigmoid(x @ w_ple_gate) * (p_i @ w_ple)
    return _layer_norm(ALPHA * x + sub + ple, ln_g, ln_b)

def setup_inputs(seed: int = 0) -> dict:
    key = jax.random.key(seed)
    ks = jax.random.split(key, 24)
    f32 = jnp.float32

    def nrm(k, shape, s):
        return jax.random.normal(k, shape, f32) * s

    x = nrm(ks[0], (BATCH, SEQ, D_MODEL), 1.0)
    p = nrm(ks[1], (DEPTH, BATCH, SEQ, PLE_DIM), 1.0)
    w_in = nrm(ks[2], (DEPTH, D_MODEL, D_IN), D_MODEL ** -0.5)
    gdn_conv_w = nrm(ks[3], (DEPTH, CONV_K, GDN_QKV), CONV_K ** -0.5)
    gdn_a_log = jnp.log(jax.random.uniform(ks[4], (DEPTH, GDN_HEADS), f32, 1.0, 16.0))
    dt = jnp.exp(jax.random.uniform(ks[5], (DEPTH, GDN_HEADS), f32, math.log(1e-3), math.log(1e-1)))
    gdn_dt_bias = dt + jnp.log(-jnp.expm1(-dt))
    gdn_norm_w = 1.0 + nrm(ks[6], (DEPTH, GDN_DV), 0.02)
    nsa_pe_k = nrm(ks[7], (DEPTH, CMP_LEN, NSA_DK), 0.02)
    nsa_pe_v = nrm(ks[8], (DEPTH, CMP_LEN, NSA_DK), 0.02)
    nsa_cmp_w1k = nrm(ks[9], (DEPTH, CMP_LEN * NSA_DK, CMP_HIDDEN), (CMP_LEN * NSA_DK) ** -0.5)
    nsa_cmp_w2k = nrm(ks[10], (DEPTH, CMP_HIDDEN, NSA_DK), CMP_HIDDEN ** -0.5)
    nsa_cmp_w1v = nrm(ks[11], (DEPTH, CMP_LEN * NSA_DK, CMP_HIDDEN), (CMP_LEN * NSA_DK) ** -0.5)
    nsa_cmp_w2v = nrm(ks[12], (DEPTH, CMP_HIDDEN, NSA_DK), CMP_HIDDEN ** -0.5)
    w_branch_a = nrm(ks[13], (DEPTH, RET_V, D_MODEL), RET_V ** -0.5)
    w_branch_b = nrm(ks[14], (DEPTH, GDN_V, D_MODEL), GDN_V ** -0.5)
    w_branch_c = nrm(ks[15], (DEPTH, NSA_Q, D_MODEL), NSA_Q ** -0.5)
    w_out = nrm(ks[16], (DEPTH, D_MODEL, D_MODEL), D_MODEL ** -0.5 * BETA_INIT)
    ln_g = 1.0 + nrm(ks[17], (DEPTH, D_MODEL), 0.02)
    ln_b = nrm(ks[18], (DEPTH, D_MODEL), 0.02)
    w_ple = nrm(ks[19], (DEPTH, PLE_DIM, D_MODEL), PLE_DIM ** -0.5)
    w_ple_gate = nrm(ks[20], (DEPTH, D_MODEL, D_MODEL), D_MODEL ** -0.5)
    return {'x': x, 'p': p, 'w_in': w_in, 'gdn_conv_w': gdn_conv_w, 'gdn_a_log': gdn_a_log,
            'gdn_dt_bias': gdn_dt_bias, 'gdn_norm_w': gdn_norm_w, 'nsa_pe_k': nsa_pe_k, 'nsa_pe_v': nsa_pe_v,
            'nsa_cmp_w1k': nsa_cmp_w1k, 'nsa_cmp_w2k': nsa_cmp_w2k, 'nsa_cmp_w1v': nsa_cmp_w1v,
            'nsa_cmp_w2v': nsa_cmp_w2v, 'w_branch_a': w_branch_a, 'w_branch_b': w_branch_b,
            'w_branch_c': w_branch_c, 'w_out': w_out, 'ln_g': ln_g, 'ln_b': ln_b, 'w_ple': w_ple,
            'w_ple_gate': w_ple_gate}

def reference(x, p, w_in, gdn_conv_w, gdn_a_log, gdn_dt_bias, gdn_norm_w, nsa_pe_k, nsa_pe_v,
              nsa_cmp_w1k, nsa_cmp_w2k, nsa_cmp_w1v, nsa_cmp_w2v, w_branch_a, w_branch_b, w_branch_c,
              w_out, ln_g, ln_b, w_ple, w_ple_gate):
    for i in range(DEPTH):
        x = _layer(x, p[i], w_in[i], gdn_conv_w[i], gdn_a_log[i], gdn_dt_bias[i], gdn_norm_w[i],
                   nsa_pe_k[i], nsa_pe_v[i], nsa_cmp_w1k[i], nsa_cmp_w2k[i], nsa_cmp_w1v[i], nsa_cmp_w2v[i],
                   w_branch_a[i], w_branch_b[i], w_branch_c[i], w_out[i], ln_g[i], ln_b[i],
                   w_ple[i], w_ple_gate[i])
    return x


_drawn_inputs = setup_inputs


def setup_inputs(seed=0):
    import zlib

    import numpy as np

    out = dict(_drawn_inputs(seed))
    spreads = {}
    factors = {'gdn_a_log': 4.17,
     'gdn_norm_w': 8.0,
     'nsa_pe_k': 8.0,
     'nsa_pe_v': 8.0,
     'nsa_cmp_w1k': 8.0,
     'nsa_cmp_w2k': 8.0,
     'nsa_cmp_w1v': 4.236,
     'ln_g': 2.871,
     'ln_b': 2.903}
    for name, (base, spread) in spreads.items():
        noise = np.random.default_rng([zlib.crc32(name.encode()), seed]).standard_normal(out[name].shape)
        drawn = base * np.exp(spread * noise) if base else spread * noise
        out[name] = __import__('jax').numpy.asarray(drawn.astype(out[name].dtype))
    for name, factor in factors.items():
        out[name] = (out[name] * factor).astype(out[name].dtype)
    return out
```

```python
from contextlib import ExitStack

import numpy as np
import concourse.bass as bass
from concourse import mybir

F32 = mybir.dt.float32
F32R = mybir.dt.float32r
ACT = mybir.ActivationFunctionType
ALU = mybir.AluOpType
AX_X = mybir.AxisListType.X

P = 128
S = 1024
D = 1024
NT = S // P
KD = D // P
HALF = 512
UC = 256
UNIT = KD * UC
HEADS = 4
W4 = HEADS * P
CONV_K = 4
LEVELS = 7
NSMALL = 32
QPARTS = 4

N_FIRST = 6
U_RET = 0
U_VSW = 6
U_SMALL = 7
U_NSA = 8
U_Z = 12
U_GDN = 18
U_MERGE = 24
U_MERGE_RET = 4
U_PLE = 36
U_BR = 40
U_OUT = 48
U_END = 52
KB = 3 * HEADS
UNIT_BR = KB * P
ALPHA = 2.0 ** 0.25


ATANH = tuple(range(19, 0, -2))

PREP_ABS, PREP_LOG, PREP_SS, PREP_DVE = 3, 28, 30, 38


NH = 8
DH = 64
NC = 64
CMP_LEN, CMP_STRIDE = 32, 16
N_SEL = 8
STEPS = NT * NH
SCALE = DH ** -0.5
NEG = -1e30


def place(e):
    return e // NH, e % NH // 4, e % 4


def blocks(n):
    return n + 1, min(n + 1, 3)


def s_uses(e):
    n, h = e // NH, e % NH
    return e + (n + 1) + (1 if h > 2 and n < NT - 1 else 0)


def s_uses_cmp(n):
    return 0 if n == 0 else s_uses(8 * (n - 1) + 2) + 1


def o_uses(e):
    n, h = e // NH, e % NH
    return e + (n + 1) + (1 if h > 5 and n < NT - 1 else 0) + n


def o_uses_cmp(n):
    return 0 if n == 0 else o_uses(8 * (n - 1) + 5) + 1


def o_uses_turn(n):
    return o_uses(8 * n + 7) + 1


def turn_groups():
    at, cmp_at, g = [], [0], 2
    for e in range(STEPS):
        at.append(g)
        g += -(-sum(blocks(e // NH)) // 4)
        if e % NH == 5 and e // NH < NT - 1:
            cmp_at.append(g)
            g += 2
    return at, cmp_at


GROUP_AT, GROUP_AT_CMP = turn_groups()
GROUP_END = GROUP_AT[-1] + -(-sum(blocks(NT - 1)) // 4)


class Steps:

    def __init__(self, eng, sem):
        self.eng, self.sem, self.before, self.here = eng, sem, 0, 0

    def step(self, ins):
        ins.then_inc(self.sem, 1)
        self.here += 1

    def wait(self, back=0):
        self.eng.wait_ge(self.sem, self.before + (self.here - back))

    def value(self):
        return self.before + self.here

    def enter(self, i, per):
        assert not isinstance(self.before, tuple)
        self.start = self.before + self.here
        self.before, self.here = i * per + self.start, 0

    def leave(self, turns, per):
        assert self.here == per, (self.here, per)
        self.before, self.here = self.start + turns * per, 0


def build(nc, io, out):
    with ExitStack() as ctx:
        def sb(name, shape, dt=F32):
            return ctx.enter_context(nc.sbuf_tensor(name + "_sb", shape, dt))

        def sem(name):
            return ctx.enter_context(nc.semaphore(name))

        def scratch(name, shape):
            return nc.dram_tensor(name, shape, F32, kind="Internal").ap()

        ret_dram = scratch("ret_dram", (NT, P, 3 * W4))
        zt_dram = scratch("zt_dram", (12, P, S))
        nsa_dram = scratch("nsa_dram", (8, P, S))
        merge_dram = scratch("merge_dram", (24, P, S))
        oa_dram = scratch("oa_dram", (HEADS, P, S))
        ob_dram = scratch("ob_dram", (HEADS, P, S))
        oc_dram = scratch("oc_dram", (HEADS, P, S))
        pleg_dram = scratch("pleg_dram", (NT, P, D))
        ple_dram = scratch("ple_dram", (NT, P, D))
        gdn_dram = scratch("gdn_dram", (NT, P, 3 * W4))

        acc = ctx.enter_context(nc.psum_tensor("acc", [P, 4, HALF], F32))
        aux = ctx.enter_context(nc.psum_tensor("aux", [P, 4, HALF], F32))

        x_hi = sb("x_hi", [P, KD, S], F32R)
        x_lo = sb("x_lo", [P, KD, S], F32R)
        w_raw = sb("w_raw", [P, 2, UNIT])
        w_hi = sb("w_hi", [P, 2, UNIT], F32R)
        w_lo = sb("w_lo", [P, 2, UNIT], F32R)
        stage = sb("stage", [P, 4, HALF])
        vsw = sb("vsw", [P, NT, UC])
        small = sb("small", [P, NT, NSMALL])
        conv_w = sb("conv_w", [P, 12, CONV_K])
        ident = sb("ident", [P, P])
        ones = sb("ones", [P, 1])
        with ExitStack() as at_start:
            p_hi, p_lo, ple_hi, ple_lo = (at_start.enter_context(nc.sbuf_tensor(n, [P, 2, S], F32R))
                                          for n in ("p_hi", "p_lo", "ple_hi", "ple_lo"))
        gdn_ss = sb("gdn_ss", [P, NT, 12])
        with ExitStack() as in_conv:
            def sb_conv(name, shape):
                return in_conv.enter_context(nc.sbuf_tensor(name + "_sb", shape, F32))

            conv_in = sb_conv("conv_in", [P, 2, CONV_K - 1 + S])
            conv_y = sb_conv("conv_y", [P, 2, S])
            gdn_stage = sb_conv("gdn_stage", [P, NT, UC])
            gdn_sq = sb_conv("gdn_sq", [P, NT, UC])

        with ExitStack() as in_ret:
            def sb_ret(name, shape):
                return in_ret.enter_context(nc.sbuf_tensor(name + "_sb", shape, F32))

            ret_in = sb_ret("ret_in", [P, 2, 3, W4])
            ret_z = sb_ret("ret_z", [P, 2, HEADS, P])
            cos_sin = sb_ret("cos_sin", [P, NT, 2, P // 2])
            ret_decay = sb_ret("ret_decay", [P, HEADS, P])
            q_decay = sb_ret("q_decay", [P, HEADS, P])
            k_decay = sb_ret("k_decay", [P, HEADS])
            rot_tmp = sb_ret("rot_tmp", [P, 4, 2 * HEADS, P // 2])
            rot = sb_ret("rot", [P, 2, HEADS, 2, P // 2])
            k_end = sb_ret("k_end", [P, HEADS, P])
            q_t = sb_ret("q_t", [P, HEADS, P])
            k_t = sb_ret("k_t", [P, HEADS, P])
            q_start_t = sb_ret("q_start_t", [P, HEADS, P])
            ret_s = sb_ret("ret_s", [P, HEADS, P])
            ret_state = sb_ret("ret_state", [P, HEADS, P])
            ret_stats = sb_ret("ret_stats", [P, HEADS, 6])
            ret_mv = sb_ret("ret_mv", [P, HEADS, 2])
            ret_dm = sb_ret("ret_dm", [P, HEADS])
            ret_std = sb_ret("ret_std", [P, HEADS])
            ret_rstd = sb_ret("ret_rstd", [P, HEADS])
            ret_norm = sb_ret("ret_norm", [P, HEADS, P])
            ret_out = sb_ret("ret_out", [P, 2, HEADS, P])

        beta = sb("beta", [P, NT, HEADS])
        gates = sb("gates", [P, NT, 3 * 8])
        with ExitStack() as in_gdn:
            def sb_gdn(name, *shape):
                return in_gdn.enter_context(nc.sbuf_tensor(name + "_sb", [P, *shape], F32))

            g_in = sb_gdn("g_in", 3, HEADS, P)
            g_z = sb_gdn("g_z", HEADS, P)
            tri = sb_gdn("tri", 3, P)
            level_masks = sb_gdn("level_masks", LEVELS, P)
            dt_bias = sb_gdn("dt_bias", HEADS)
            a_log = sb_gdn("a_log", HEADS)
            norm_w = sb_gdn("norm_w", 1)
            (ga, gy, gs, gs2, gpoly, g_log, rn_q, rn_k, s_q, s_q_dec, s_k_beta, s_k_beta_dec,
             s_k_end) = (sb_gdn(n, NT * HEADS) for n in (
                 "ga gy gs gs2 gpoly g_log rn_q rn_k s_q s_q_dec s_k_beta s_k_beta_dec s_k_end".split()))
            ea = sb_gdn("ea", HEADS)
            decays = sb_gdn("decays", 3, NT * HEADS)
            beta_flat = beta[:].rearrange("p t h -> p (t h)")
            k_n, k_b, q_n, q_d, kb_dec, k_e, v_b = (sb_gdn(n, HEADS, P) for n in (
                "k_n k_b q_n q_d kb_dec k_e v_b".split()))
            k_nt = sb_gdn("k_nt", HEADS, P)
            kq_t = sb_gdn("kq_t", HEADS, 2, P)
            q_dt = sb_gdn("q_dt", HEADS, P)
            g_up = sb_gdn("g_up", HEADS, P)
            decay_t = sb_gdn("decay_t", HEADS, P)
            a_t = sb_gdn("a_t", HEADS, 2, P)
            b_t = sb_gdn("b_t", 2, HEADS, P)
            inv = sb_gdn("inv", HEADS, P)
            inv_t = sb_gdn("inv_t", HEADS, P)
            bi = sb_gdn("bi", HEADS, P)
            w_t = sb_gdn("w_t", HEADS, P)
            v_new = sb_gdn("v_new", HEADS, P)
            g_state = sb_gdn("g_state", HEADS, P)
            g_o = sb_gdn("g_o", HEADS, P)
            g_sq = sb_gdn("g_sq", HEADS, P)
            g_ss = sb_gdn("g_ss", HEADS)
            g_std = sb_gdn("g_std", HEADS)
            g_rstd = sb_gdn("g_rstd", HEADS)
            g_on = sb_gdn("g_on", HEADS, P)
            g_out = sb_gdn("g_out", 2, HEADS, P)

        with ExitStack() as in_nsa:
            def sb_nsa(name, *shape):
                return in_nsa.enter_context(nc.sbuf_tensor(name + "_sb", [P, *shape], F32))

            k_sw = sb_nsa("k_sw", 2, S)
            kc_t = sb_nsa("kc_t", NC)
            vc = sb_nsa("vc", 2 * DH)
            cmp_bias = sb_nsa("cmp_bias", 2)
            with ExitStack() as in_cmp:
                def sb_cmp(name, *shape):
                    return in_cmp.enter_context(nc.sbuf_tensor(name + "_sb", [P, *shape], F32))

                kv_c = sb_cmp("kv_c", 2, S)
                w1 = sb_cmp("w1", 2, CMP_LEN, P)
                w2 = sb_cmp("w2", 2, DH)
                pe_t = sb_cmp("pe_t", 2, CMP_LEN)
                hidden = sb_cmp("hidden", 2, 2, NC)
            n_q = sb_nsa("n_q", 2, 4, P)
            n_z = sb_nsa("n_z", 2, 4, P)
            causal_wide = sb_nsa("causal_wide", S)
            win_mask = sb_nsa("win_mask", 3 * P)
            cmp_mask = sb_nsa("cmp_mask", NT, NC)
            row_valid = sb_nsa("row_valid", 1)
            rank_keep = sb_nsa("rank_keep", NT, 16)
            rank_add = sb_nsa("rank_add", NT, 16)
            earlier = sb_nsa("earlier", 16, 16)
            sel_mask = sb_nsa("sel_mask", 2, S)
            scores = sb_nsa("scores", 2, S + 3 * P)
            n_max = sb_nsa("n_max", 2, 2)
            n_nmax = sb_nsa("n_nmax", 2, 2)
            n_sum = sb_nsa("n_sum", 2, 2)
            n_coef = sb_nsa("n_coef", 2, 2)
            p_t = sb_nsa("p_t", 2, 11, P)
            cmp_s = sb_nsa("cmp_s", NH, NC)
            cmp_pt = sb_nsa("cmp_pt", NH, P)
            cmp_max = sb_nsa("cmp_max", NH)
            cmp_rsum = sb_nsa("cmp_rsum", NH)
            cmp_coef = sb_nsa("cmp_coef", NH)
            cmp_pn = sb_nsa("cmp_pn", NH, NC)
            cmp_pg = sb_nsa("cmp_pg", 2, NC)
            imp = sb_nsa("imp", 2, 16)
            beats = cmp_pn[:].rearrange("p h (i j) -> p (h i j)", i=4).rearrange("p (g i j) -> p g i j", g=2, i=16)
            ties = sb_nsa("ties", 2, 16, 16)
            n_beat = sb_nsa("n_beat", 2, 16)
            sel_bias = sb_nsa("sel_bias", 2, 16)
            n_o = sb_nsa("n_o", 2, 4, 2, DH)
            n_out = sb_nsa("n_out", 2, 4, P)

        with ExitStack() as in_br:
            def sb_br(name, shape, dt=F32):
                return in_br.enter_context(nc.sbuf_tensor(name + "_sb", shape, dt))

            mixed = sb_br("mixed", [P, KD, S])
            oc_hi = sb_br("oc_hi", [P, HEADS, S], F32R)
            oc_lo = sb_br("oc_lo", [P, HEADS, S], F32R)
            m_gate = sb_br("m_gate", [P, 2, 3, HALF])
        with ExitStack() as in_fin:
            def sb_fin(name, shape, dt=F32):
                return in_fin.enter_context(nc.sbuf_tensor(name + "_sb", shape, dt))

            resid = sb_fin("resid", [P, NT, D])
            wo_hi = sb_fin("wo_hi", [P, 2, UNIT], F32R)
            wo_lo = sb_fin("wo_lo", [P, 2, UNIT], F32R)
            f_gate = sb_fin("f_gate", [P, 2, HALF])
            f_ple = sb_fin("f_ple", [P, 2, HALF])
            ln_stats = sb_fin("ln_stats", [P, 2, 4, 3])
            ln_sum = sb_fin("ln_sum", [P, 2])
            ln_dev = sb_fin("ln_dev", [P, 2, 4])
            ln_var = sb_fin("ln_var", [P, 2])
            ln_std = sb_fin("ln_std", [P, 2])
            ln_rstd = sb_fin("ln_rstd", [P, 2])
            ln_gb = vsw[:].rearrange("p t n -> p (t n)").rearrange("p (c n) -> p c n", c=2)

        raw_loaded = [sem("raw_loaded0"), sem("raw_loaded1")]
        first_hi = sem("first_hi")
        ple_ready = sem("ple_ready")
        ple_out = sem("ple_out")
        first_split = sem("first_split")
        ones_ready = sem("ones_ready")
        pool_hi = sem("pool_hi")
        w_split = sem("w_split")
        acc_ready = sem("acc_ready")
        acc_freed = sem("acc_freed")
        stored = [sem(f"stored{i}") for i in range(4)]
        const_loaded = sem("const_loaded")
        zeroed = sem("zeroed")
        conv_ready = sem("conv_ready")
        conv_done = sem("conv_done")
        silu_done = sem("silu_done")
        turned = sem("turned")
        turned_freed = sem("turned_freed")
        gdn_staged = sem("gdn_staged")
        gdn_stored = sem("gdn_stored")
        dve_steps = sem("dve_steps")
        ret_const = sem("ret_const")
        ret_loaded = [sem("ret_loaded0"), sem("ret_loaded1")]
        ret_z_loaded = [sem("ret_z_loaded0"), sem("ret_z_loaded1")]
        rot_parts = sem("rot_parts")
        rotated = sem("rotated")
        k_end_ready = sem("k_end_ready")
        qk_turned = sem("qk_turned")
        qk_t_ready = sem("qk_t_ready")
        q_start_ready = sem("q_start_ready")
        ret_s_done = sem("ret_s_done")
        ret_s_ready = sem("ret_s_ready")
        ret_kv_done = sem("ret_kv_done")
        ret_state_ready = sem("ret_state_ready")
        ret_o_done = sem("ret_o_done")
        ret_stats_done = sem("ret_stats_done")
        ret_std_ready = sem("ret_std_ready")
        ret_normed = sem("ret_normed")
        ret_o_turned = sem("ret_o_turned")
        ret_out_ready = sem("ret_out_ready")
        ret_stored = [sem("ret_stored0"), sem("ret_stored1")]
        g_const = sem("g_const")
        prep_act = sem("prep_act")
        prep_dve = sem("prep_dve")
        prep_pe = sem("prep_pe")
        g_loaded = sem("g_loaded")
        g_z_loaded = sem("g_z_loaded")
        g_scaled = sem("g_scaled")
        g_scaled_pool = sem("g_scaled_pool")
        g_turned = sem("g_turned")
        g_t_act = sem("g_t_act")
        g_t_dve = sem("g_t_dve")
        g_decay_done = sem("g_decay_done")
        g_decay_exp = sem("g_decay_exp")
        g_decay_ready = sem("g_decay_ready")
        g_a_done = sem("g_a_done")
        g_a_ready = sem("g_a_ready")
        b_ready = sem("b_ready")
        b_used = sem("b_used")
        bi_ready = sem("bi_ready")
        u_done = sem("u_done")
        inv_steps = sem("inv_steps")
        w_done = sem("w_done")
        w_ready = sem("w_ready")
        v_done = sem("v_done")
        v_ready = sem("v_ready")
        g_o_done = sem("g_o_done")
        g_o_ready = sem("g_o_ready")
        g_s_done = sem("g_s_done")
        g_state_ready = sem("g_state_ready")
        g_ss_ready = sem("g_ss_ready")
        g_std_ready = sem("g_std_ready")
        g_normed = sem("g_normed")
        g_o_turned = sem("g_o_turned")
        g_out_ready = sem("g_out_ready")
        g_stored = [sem("g_stored0"), sem("g_stored1")]
        n_const = sem("n_const")
        cmp_loaded = sem("cmp_loaded")
        cmp_hidden_done = sem("cmp_hidden_done")
        cmp_bias_ready = sem("cmp_bias_ready")
        cmp_hidden_ready = sem("cmp_hidden_ready")
        cmp_kv_done = sem("cmp_kv_done")
        cmp_kv_ready = sem("cmp_kv_ready")
        n_q_loaded = [sem("n_q_loaded0"), sem("n_q_loaded1")]
        n_z_loaded = [sem("n_z_loaded0"), sem("n_z_loaded1")]
        s_done = sem("s_done")
        s_taken = sem("s_taken")
        max_ready = sem("max_ready")
        exp_done = sem("exp_done")
        pt_turned = sem("pt_turned")
        pt_taken_dve = sem("pt_taken_dve")
        pt_taken_act = sem("pt_taken_act")
        o_done = sem("o_done")
        o_taken = sem("o_taken")
        cmp_shifted = sem("cmp_shifted")
        cmp_exp_done = sem("cmp_exp_done")
        sel_ready = sem("sel_ready")
        mask_ready = sem("mask_ready")
        n_stored = [sem("n_stored0"), sem("n_stored1")]
        nsa_steps = sem("nsa_steps")
        o_loaded = [sem(f"o_loaded{c}") for c in range(3)]
        o_hi = sem("o_hi")
        o_split = sem("o_split")
        gate_loaded = [sem("gate_loaded0"), sem("gate_loaded1")]
        gate_ready = sem("gate_ready")
        br_done = sem("br_done")
        br_taken = sem("br_taken")
        mixed_ready = sem("mixed_ready")
        mixed_hi = sem("mixed_hi")
        mixed_split = sem("mixed_split")
        ln_loaded = sem("ln_loaded")
        x_loaded = [sem("x_loaded0"), sem("x_loaded1")]
        f_loaded = [sem("f_loaded0"), sem("f_loaded1")]
        f_sigmoid = sem("f_sigmoid")
        f_prod = sem("f_prod")
        f_used = sem("f_used")
        out_done = sem("out_done")
        out_taken = sem("out_taken")
        ln_var_ready = sem("ln_var_ready")
        ln_std_ready = sem("ln_std_ready")
        ln_scaled = sem("ln_scaled")
        ln_done = sem("ln_done")
        out_stored = sem("out_stored")
        fin_steps = sem("fin_steps")

        block = ctx.enter_context(nc.Block())

        def first_parts(p_part, ple_part, x_part):
            return [p_part[:], ple_part[:]] + [x_part[:, :, q * UC:(q + 1) * UC] for q in range(4)]

        def one(ap):
            return ap.rearrange("o p n -> (o p) n")

        @block.sync
        def _(sp):
            def load(n, src):
                sp.dma_start(w_raw[:, n % 2], src).then_inc(raw_loaded[n % 2], 16)

            def store_ple(g):
                for b in range(4):
                    sp.wait_ge(ple_out, 4 * g + b + 1)
                    sp.dma_start(ple_dram[2 * g + b // 2, :, (b % 2) * HALF:(b % 2 + 1) * HALF],
                                 stage[:, b]).then_inc(stored[b], 16)

            load(0, io["first"][0])
            load(1, io["first"][1])
            sp.dma_start(conv_w[:], io["conv_w"]).then_inc(const_loaded, 16)
            sp.dma_start(ident[:], io["ident"]).then_inc(const_loaded, 16)
            for n in range(2, N_FIRST + 2):
                sp.wait_ge(first_split, n - 1)
                load(n, io["first"][n] if n < N_FIRST else io["weights"][n - N_FIRST])
                if n >= 4:
                    store_ple(n - 4)
            def load_weights(u, slot, n_split):
                sp.wait_ge(w_split, n_split)
                sp.dma_start(w_raw[:, slot], one(io["weights"][bass.ds(u, 1)])).then_inc(raw_loaded[slot], 16)

            def load_branch(ct, slot, n_split):
                sp.wait_ge(w_split, n_split)
                sp.dma_start(w_raw[:, slot, 0:UNIT_BR], one(io["w_branch"][bass.ds(ct, 1)])).then_inc(raw_loaded[slot], 16)

            def load_out(n):
                sp.wait_ge(w_split, U_OUT + n - 1)
                sp.dma_start(w_raw[:, n % 2], io["weights"][U_BR + n]).then_inc(raw_loaded[n % 2], 16)

            with sp.Fori(0, (U_MERGE - 2) // 2) as i:
                for s in range(2):
                    load_weights(2 * i + 2 + s, s, 2 * i + 1 + s)
            for s in range(2):
                load_weights(U_MERGE + s, s, U_MERGE - 1 + s)

            for n, c in enumerate((cos_sin, ret_decay, q_decay, k_decay)):
                if n == 0:
                    sp.wait_ge(gdn_stored, 16 * 7)
                sp.dma_start(c[:], io[("cos_sin", "ret_decay", "q_decay", "k_decay")[n]]).then_inc(ret_const, 16)
            with sp.Fori(0, NT // 4) as i:
                for q in range(4):
                    s = q % 2
                    t = 4 * i + q
                    sp.wait_ge(ret_o_done, t + 1)
                    sp.dma_start(ret_in[:, s].rearrange("p c n -> p (c n)"),
                                 one(ret_dram[bass.ds(t, 1)])).then_inc(ret_loaded[s], 16)
                    sp.wait_ge(ret_out_ready, t + 1)
                    sp.dma_start(ret_z[:, s], zt_dram[0:HEADS, :, bass.ds(P * t, P)].rearrange("h p n -> p h n")
                                 ).then_inc(ret_z_loaded[s], 16)
                    if s == 1:
                        load_weights(2 * i + U_MERGE + 2 + q // 2, q // 2, 2 * i + U_MERGE + 1 + q // 2)
            for q in range(2):
                sp.wait_ge(ret_stored[q], 16 * 5)
            for dst, name in ((tri, "tri"), (level_masks, "level_masks"), (dt_bias, "dt_bias"), (a_log, "a_log"),
                              (norm_w, "norm_w")):
                sp.dma_start(dst[:], io[name]).then_inc(g_const, 16)
            with sp.Fori(0, NT // 2) as i:
                for s in range(2):
                    t = 2 * i + s
                    sp.wait_ge(g_scaled, 3 * t + 3)
                    sp.wait_ge(g_scaled_pool, 5 * t + 5)
                    sp.dma_start(g_in[:].rearrange("p c h n -> p (c h n)"), one(gdn_dram[bass.ds(t, 1)])).then_inc(g_loaded, 16)
                    sp.wait_ge(g_out_ready, t + 1)
                    sp.dma_start(g_z[:], zt_dram[HEADS:2 * HEADS, :, bass.ds(P * t, P)].rearrange("h p n -> p h n")
                                 ).then_inc(g_z_loaded, 16)
                    load_weights(t + U_MERGE + U_MERGE_RET + 2, s, t + U_MERGE + U_MERGE_RET + 1)

            for q in range(2):
                sp.wait_ge(g_stored[q], 16 * 5)
            for dst, src in ((kv_c[:], nsa_dram[4:6].rearrange("c p n -> p c n")), (w1[:], io["w1"]), (w2[:], io["w2"]),
                             (pe_t[:], io["pe_t"]), (k_sw[:], nsa_dram[6:8].rearrange("c p n -> p c n"))):
                sp.dma_start(dst, src).then_inc(cmp_loaded, 16)
            sp.wait_ge(cmp_kv_done, 1)
            for dst, name in ((causal_wide, "causal_wide"), (win_mask, "win_mask"), (cmp_mask, "cmp_mask"),
                              (row_valid, "row_valid"), (rank_keep, "rank_keep"), (rank_add, "rank_add"),
                              (earlier, "earlier")):
                sp.dma_start(dst[:], io[name]).then_inc(n_const, 16)
            for n in range(NT):
                if n >= 2:
                    sp.wait_ge(s_done, s_uses(8 * (n - 2) + 7) + 1)
                sp.dma_start(n_q[:, n % 2], nsa_dram[0:4, :, n * P:(n + 1) * P].rearrange("h p n -> p h n")).then_inc(
                    n_q_loaded[n % 2], 16)
                if n >= 2:
                    sp.wait_ge(o_taken, o_uses_turn(n - 2) + 1)
                sp.dma_start(n_z[:, n % 2], zt_dram[8:12, :, n * P:(n + 1) * P].rearrange("h p n -> p h n")).then_inc(
                    n_z_loaded[n % 2], 16)
                u = U_PLE + 2 + n // 2
                if n % 2 == 0 and u < U_BR:
                    load_weights(u, u % 2, u - 1)
                elif n % 2 == 0:
                    load_branch(u - U_BR, u % 2, u - 1)

            for q in range(2):
                sp.wait_ge(n_stored[q], 16 * 4)
            sp.dma_start(ln_gb, io["ln_gb"]).then_inc(ln_loaded, 16)
            for c, (src, at) in enumerate(((oa_dram, 0), (ob_dram, HEADS), (oc_dram, 0))):
                if c == 2:
                    sp.wait_ge(o_split, HEADS)
                sp.dma_start(mixed[:, at:at + HEADS], src.rearrange("h p n -> p h n")).then_inc(o_loaded[c], 16)

            def load_gates(ct):
                for h in range(2):
                    sp.wait_ge(mixed_ready, 2 * ct + h + 1)
                    sp.dma_start(m_gate[:, h], merge_dram.rearrange("(b c) p n -> c p b n", b=3)[bass.ds(ct, 1), :, :, h * HALF:(h + 1) * HALF]
                                 .rearrange("o p b n -> (o p) b n")).then_inc(gate_loaded[h], 16)

            with sp.Fori(0, (KD - 2) // 2) as i:
                for s in range(2):
                    load_gates(2 * i + s)
                    load_branch(2 * i + s + 2, s, 2 * i + s + 1 + U_BR)
            for s in range(2):
                load_gates(KD - 2 + s)
                load_out(s)

            sp.wait_ge(mixed_split, NT)
            for h in range(2):
                sp.dma_start(resid[:, :, h * HALF:(h + 1) * HALF], io["x_tok"][:, :, h * HALF:(h + 1) * HALF]).then_inc(
                    x_loaded[h], 16)

            def load_ple(t, s, h):
                sp.wait_ge(f_used, NT * h + t + 1)
                for dst, src in ((f_gate, pleg_dram), (f_ple, ple_dram)):
                    sp.dma_start(dst[:, s], one(src[bass.ds(t, 1), :, h * HALF:(h + 1) * HALF])).then_inc(f_loaded[s], 16)

            load_out(2)
            load_out(3)
            for h in range(2):
                with sp.Fori(0, NT // 2) as i:
                    for s in range(2):
                        load_ple(2 * i + s, s, h)
            with sp.Fori(0, NT) as t:
                sp.wait_ge(ln_done, t + 1)
                sp.dma_start(out[0, bass.ds(P * t, P), :], resid[:, bass.ds(t, 1), :].rearrange("p o n -> p (o n)")).then_inc(
                    out_stored, 16)

            sp.wait_ge(out_stored, 16 * NT)
            sp.wait_ge(ln_loaded, 16)
            for q in range(2):
                sp.wait_ge(raw_loaded[q], 16 * ((U_END + 6) // 2))

        @block.gpsimd
        def _(pool):
            def split(u, slot, size=UNIT, parts=None):
                hi, lo = parts or (w_hi[:, slot, 0:size], w_lo[:, slot, 0:size])
                raw = w_raw[:, slot, 0:size]
                pool.tensor_tensor(hi, raw, ones[:].broadcast_to([P, size]), ALU.mult).then_inc(pool_hi, 1)
                pool.wait_ge(pool_hi, u + 1)
                pool.tensor_tensor(lo, raw, hi.bitcast(F32), ALU.subtract).then_inc(w_split, 1)

            pool.memset(ones[:], 1.0).then_inc(ones_ready, 1)
            pool.wait_ge(ones_ready, 1)
            for u in range(2):
                pool.wait_ge(raw_loaded[u], 16 * 4)
                split(u, u)

            def split_next(u, slot, used, loads):
                pool.wait_ge(acc_ready, used)
                pool.wait_ge(raw_loaded[slot], loads)
                split(u, slot)

            with pool.Fori(0, (U_MERGE - 2) // 2) as i:
                for s in range(2):
                    split_next(2 * i + 2 + s, s, 8 * i + 4 * (s + 1), 16 * i + 16 * 5)
            split_next(U_MERGE, 0, 4 * (U_MERGE - 1), 8 * (U_MERGE + 8))

            pool.wait_ge(ret_const, 16 * 4)
            with pool.Fori(0, NT // 4) as i:
                for q in range(4):
                    s = q % 2
                    t = 4 * i + q
                    halves = ret_in[:, s, 0:2].rearrange("p c (h e n) -> p (c h) e n", e=2, n=P // 2)
                    pool.wait_ge(ret_loaded[s], 32 * i + 16 * (q // 2 + 1))
                    pool.wait_ge(rotated, t + 1)
                    for n, (e, f) in enumerate(((0, 0), (1, 1), (0, 1), (1, 0))):
                        table = cos_sin[:, bass.ds(t, 1), f, :].broadcast_to([P, 2 * HEADS, P // 2])
                        pool.tensor_tensor(rot_tmp[:, n], halves[:, :, e], table, ALU.mult).then_inc(rot_parts, 1)
                    if s == 0:
                        split_next(2 * i + U_MERGE + 1 + q // 2, (1 + q // 2) % 2,
                                   8 * i + 4 * (U_MERGE + q // 2), 16 * i + 8 * (U_MERGE + 8) + 16 * (q // 2))
                    pool.wait_ge(rotated, t + 2)
                    pool.wait_ge(ret_kv_done, t + 1)
                    pool.tensor_tensor(k_end[:], rot[:, 1].rearrange("p h e n -> p h (e n)"),
                                       k_decay[:].rearrange("p (h o) -> p h o", o=1).broadcast_to([P, HEADS, P]),
                                       ALU.mult).then_inc(k_end_ready, 1)

            pool.wait_ge(g_const, 16 * 5)
            pool.wait_ge(prep_dve, PREP_DVE)

            def by_head(scalars, t):
                return scalars[:, bass.ds(HEADS * t, HEADS)].rearrange("p (h o) -> p h o", o=1).broadcast_to([P, HEADS, P])

            def over_heads(table):
                return table.rearrange("p (o n) -> p o n", o=1).broadcast_to([P, HEADS, P])

            with pool.Fori(0, NT // 2) as i:
                for s in range(2):
                    t = 2 * i + s
                    pool.wait_ge(g_decay_done, t + 1)
                    pool.tensor_tensor(g_up[:], over_heads(tri[:, 0]), by_head(g_log, t), ALU.mult).then_inc(g_scaled_pool, 1)
                    pool.wait_ge(g_loaded, 16 * (t + 1))
                    pool.wait_ge(g_s_done, t + 1)
                    for dst, c, scalars in ((q_d, 0, s_q_dec), (kb_dec, 1, s_k_beta_dec), (v_b, 2, beta_flat),
                                            (k_e, 1, s_k_end)):
                        pool.tensor_tensor(dst[:], g_in[:, c], by_head(scalars, t), ALU.mult).then_inc(g_scaled_pool, 1)
                    pool.wait_ge(g_decay_exp, t + 1)
                    pool.tensor_tensor(decay_t[:], decay_t[:], over_heads(tri[:, 0]), ALU.mult).then_inc(g_decay_ready, 1)
                    pool.wait_ge(g_a_ready, t + 1)
                    for l in range(LEVELS):
                        if l > 0:
                            pool.wait_ge(b_used, 7 * t + l)
                        if l == 2:
                            pool.wait_ge(inv_steps, 13 * t + 2)
                        pool.tensor_tensor(b_t[:, (l + s) % 2], a_t[:, :, 0], over_heads(level_masks[:, l]),
                                           ALU.mult).then_inc(b_ready, 1)
                        if l == 2:
                            split_next(t + U_MERGE + U_MERGE_RET + 1, 1 - s, 4 * t + 4 * (U_MERGE + U_MERGE_RET),
                                       16 * i + 8 * (U_MERGE + U_MERGE_RET + 8) + 16 * s)

            pool.wait_ge(n_const, 16 * 7)
            for n in range(NT):
                if n % 2 == 0 and n < NT - 2:
                    u = U_PLE + 1 + n // 2
                    split_next(u, u % 2, 4 * (u - 1), 16 * ((u + 8) // 2))
                if n == NT - 2:
                    pool.wait_ge(acc_ready, 4 * (U_BR - 1))
                    pool.wait_ge(raw_loaded[0], 8 * (U_BR + 8))
                    split(U_BR, 0, UNIT_BR)
                if n >= 4:
                    pool.wait_ge(sel_ready, n - 3)
                    for g in range(2):
                        pool.wait_ge(s_taken, s_uses(8 * (n - 1) + 4 * g + 3) + 1)
                        width = (n + 1) * P
                        pool.tensor_tensor(
                            sel_mask[:, g, 0:width].rearrange("p (b n) -> p b n", n=DH),
                            sel_bias[:, g, 0:2 * (n + 1)].rearrange("p (b o) -> p b o", o=1).broadcast_to([P, 2 * (n + 1), DH]),
                            causal_wide[:, S - width:S].rearrange("p (b n) -> p b n", n=DH),
                            ALU.add).then_inc(mask_ready, 1)

            pool.wait_ge(acc_ready, 4 * U_BR)
            pool.wait_ge(raw_loaded[1], 8 * (U_BR + 8))
            split(U_BR + 1, 1, UNIT_BR)
            with pool.Fori(0, (KD - 2) // 2) as i:
                for s in range(2):
                    pool.wait_ge(br_done, 12 * i + 6 * (s + 1))
                    pool.wait_ge(raw_loaded[s], 16 * i + 8 * (U_BR + 8) + 16)
                    split(2 * i + U_BR + 2 + s, s, UNIT_BR)
            for n in range(4):
                pool.wait_ge(br_done, 6 * (KD - 1) if n == 0 else 6 * KD)
                pool.wait_ge(raw_loaded[n % 2], 16 * ((U_OUT + 8) // 2 + n // 2))
                split(U_OUT + n, n % 2, UNIT, None if n < 2 else (wo_hi[:, n % 2], wo_lo[:, n % 2]))
            for h in range(2):
                with pool.Fori(0, NT // 2) as i:
                    for s in range(2):
                        pool.wait_ge(f_sigmoid, 2 * i + s + 1 + NT * h)
                        pool.tensor_tensor(f_gate[:, s], f_gate[:, s], f_ple[:, s], ALU.mult).then_inc(f_prod, 1)
            pool.wait_ge(ln_loaded, 16)
            with pool.Fori(0, NT) as t:
                pool.wait_ge(ln_scaled, t + 1)
                tile = resid[:, bass.ds(t, 1), :].rearrange("p o n -> p (o n)")
                pool.tensor_tensor(tile, tile, ln_gb[:, 1], ALU.add).then_inc(ln_done, 1)

        @block.tensor
        def _(pe):
            mm = nc.tensor.matmul

            def parts(dst, left_hi, left_lo, right_hi, right_lo, first, last):
                mm(dst, left_hi, right_hi, start=first, stop=False, skip_group_check=True)
                mm(dst, left_hi, right_lo, start=False, stop=False, skip_group_check=True)
                return mm(dst, left_lo, right_hi, start=False, stop=last, skip_group_check=True)

            def unit_token_major(bank0, u, slot, cols=UC):
                hi = w_hi[:, slot].rearrange("p (k n) -> p k n", k=KD)
                lo = w_lo[:, slot].rearrange("p (k n) -> p k n", k=KD)
                pe.wait_ge(w_split, u + 1)
                for b in range(4):
                    pe.wait_ge(acc_freed, bank0 + b + 1)
                    for j in range(2):
                        t = 2 * b + j
                        for k in range(KD):
                            last = parts(acc[:, b, j * UC:j * UC + cols], x_hi[:, k, t * P:(t + 1) * P],
                                         x_lo[:, k, t * P:(t + 1) * P], hi[:, k, 0:cols], lo[:, k, 0:cols],
                                         k == 0, k == KD - 1)
                    last.then_inc(acc_ready, 1)

            def unit_channel_major(bank0, u, slot):
                hi = w_hi[:, slot].rearrange("p (k n) -> p k n", k=KD)
                lo = w_lo[:, slot].rearrange("p (k n) -> p k n", k=KD)
                pe.wait_ge(w_split, u + 1)
                for b in range(4):
                    c, h = b // 2, b % 2
                    pe.wait_ge(acc_freed, bank0 + b + 1)
                    for k in range(KD):
                        last = parts(acc[:, b], hi[:, k, c * P:(c + 1) * P], lo[:, k, c * P:(c + 1) * P],
                                     x_hi[:, k, h * HALF:(h + 1) * HALF], x_lo[:, k, h * HALF:(h + 1) * HALF],
                                     k == 0, k == KD - 1)
                    last.then_inc(acc_ready, 1)

            def units(unit, first, count):
                with pe.Fori(0, count // 2) as i:
                    for s in range(2):
                        unit(8 * i + 4 * (first + s), 2 * i + first + s, (first + s) % 2)

            def turn_unit(g, slot_of=None):
                for c in range(2):
                    pe.wait_ge(silu_done, 2 * g + c + 1)
                    for h in range(2):
                        pe.wait_ge(turned_freed, 4 * g + 2 * c + h + 1)
                        for j in range(4):
                            t = 4 * h + j
                            last = nc.tensor.transpose(aux[:, 2 * c + h, j * P:(j + 1) * P],
                                                       conv_y[:, c, t * P:(t + 1) * P], ident[:])
                        last.then_inc(turned, 1)

            pe.wait_ge(first_split, 2)
            for n in range(16):
                t, h = n // 2, n % 2
                if n >= 4:
                    pe.wait_ge(ple_out, n - 3)
                for k in range(2):
                    last = parts(aux[:, n % 4], p_hi[:, k, t * P:(t + 1) * P], p_lo[:, k, t * P:(t + 1) * P],
                                 ple_hi[:, k, h * HALF:(h + 1) * HALF], ple_lo[:, k, h * HALF:(h + 1) * HALF],
                                 k == 0, k == 1)
                last.then_inc(ple_ready, 1)

            pe.wait_ge(first_split, N_FIRST)
            units(unit_token_major, U_RET, 6)
            unit_token_major(4 * U_VSW, U_VSW, U_VSW % 2)
            unit_token_major(4 * U_SMALL, U_SMALL, U_SMALL % 2, NSMALL)
            units(unit_channel_major, U_NSA, 4)
            units(unit_channel_major, U_Z, 6)
            pe.wait_ge(const_loaded, 32)
            unit_channel_major(4 * U_GDN, U_GDN, U_GDN % 2)
            with pe.Fori(0, 2) as i:
                for s in range(2):
                    unit_channel_major(8 * i + 4 * (U_GDN + 1 + s), 2 * i + U_GDN + 1 + s, (U_GDN + 1 + s) % 2)
                    turn_unit(2 * i + s)
            unit_channel_major(4 * (U_GDN + 5), U_GDN + 5, (U_GDN + 5) % 2)
            turn_unit(4)
            turn_unit(5)

            class Filler:

                def __init__(self, u, slot, bank0):
                    self.u, self.bank0, self.n = u, bank0, 0
                    self.hi = w_hi[:, slot].rearrange("p (k n) -> p k n", k=KD)
                    self.lo = w_lo[:, slot].rearrange("p (k n) -> p k n", k=KD)

                def fill(self, steps):
                    for _ in range(steps):
                        b, k = self.n // KD, self.n % KD
                        c, h = b // 2, b % 2
                        if self.n == 0:
                            pe.wait_ge(w_split, self.u + 1)
                        if k == 0:
                            pe.wait_ge(acc_freed, self.bank0 + b + 3)
                        last = parts(acc[:, b % 2], self.hi[:, k, c * P:(c + 1) * P], self.lo[:, k, c * P:(c + 1) * P],
                                     x_hi[:, k, h * HALF:(h + 1) * HALF], x_lo[:, k, h * HALF:(h + 1) * HALF],
                                     k == 0, k == KD - 1)
                        if k == KD - 1:
                            last.then_inc(acc_ready, 1)
                        self.n += 1

            def turn(dst, src, identity):
                for h in range(HEADS):
                    last = nc.tensor.transpose(dst[:, h * P:(h + 1) * P], src[:, h], identity)
                return last

            def ret_tile(t, s, fill):
                v = ret_in[:, s, 2].rearrange("p (h n) -> p h n", h=HEADS)
                pe.wait_ge(rotated, t + 2)
                pe.wait_ge(qk_t_ready, 2 * t + 2)
                for n in range(2):
                    turn(acc[:, 2 + n], rot[:, n].rearrange("p h e n -> p h (e n)"), ident[:]).then_inc(qk_turned, 1)
                fill(5)
                pe.wait_ge(qk_t_ready, 2 * t + 4)
                pe.wait_ge(ret_s_ready, t + 1)
                for h in range(HEADS):
                    last = mm(aux[:, 0, h * P:(h + 1) * P], k_t[:, h], q_t[:, h], start=True, stop=True)
                last.then_inc(ret_s_done, 1)
                pe.wait_ge(k_end_ready, t + 2)
                pe.wait_ge(ret_state_ready, t + 1)
                for h in range(HEADS):
                    last = mm(aux[:, 1, h * P:(h + 1) * P], k_end[:, h], v[:, h], start=True, stop=True)
                last.then_inc(ret_kv_done, 1)
                fill(5)
                pe.wait_ge(ret_s_ready, t + 2)
                pe.wait_ge(q_start_ready, t + 2)
                pe.wait_ge(ret_normed, t + 1)
                for h in range(HEADS):
                    mm(aux[:, 2, h * P:(h + 1) * P], ret_s[:, h], v[:, h], start=True, stop=False)
                    last = mm(aux[:, 2, h * P:(h + 1) * P], q_start_t[:, h], ret_state[:, h], start=False, stop=True)
                last.then_inc(ret_o_done, 1)
                fill(6)
                pe.wait_ge(ret_normed, t + 2)
                pe.wait_ge(ret_out_ready, t + 2)
                turn(aux[:, 3], ret_norm, ident[:]).then_inc(ret_o_turned, 1)

            pe.sem_inc(ret_o_done, 2)
            pe.sem_inc(ret_kv_done, 1)
            pe.sem_inc(qk_turned, 2)
            pe.sem_inc(ret_o_turned, 1)
            pe.wait_ge(acc_freed, 4 * U_MERGE + 4)
            pe.wait_ge(turned_freed, 4 * 6 + 4)
            with pe.Fori(0, NT // 4) as i:
                for q in range(4):
                    if q % 2 == 0:
                        filler = Filler(2 * i + U_MERGE + q // 2, q // 2, 8 * i + 4 * (U_MERGE + q // 2))
                    ret_tile(4 * i + q, q % 2, filler.fill)

            pe.wait_ge(g_const, 16 * 5)
            pe.wait_ge(prep_dve, PREP_LOG)
            for n in range(3):
                last = mm(aux[:, 0, n * 32:(n + 1) * 32], tri[:, n], g_log[:], start=True, stop=True)
            last.then_inc(prep_pe, 1)

            def gdn_tile(t, s, fill):
                pe.wait_ge(g_scaled, 3 * t + 6)
                pe.wait_ge(g_scaled_pool, 5 * t + 7)
                pe.wait_ge(g_out_ready, t + 1)
                pe.wait_ge(v_ready, t + 1)
                pe.wait_ge(g_state_ready, t + 1)
                pe.wait_ge(g_o_ready, t + 1)
                for bank, src in ((acc[:, 2], k_n), (acc[:, 3], k_b), (aux[:, 2], q_n), (aux[:, 3], q_d)):
                    turn(bank, src, ident[:]).then_inc(g_turned, 1)
                fill(2)
                pe.wait_ge(g_t_act, 2 * t + 1)
                mm(acc[:, 2], tri[:, 1], g_up[:].rearrange("p h n -> p (h n)"), start=True, stop=True).then_inc(
                    g_decay_done, 1)
                pe.wait_ge(g_t_dve, 2 * t + 2)
                for h in range(HEADS):
                    last = mm(aux[:, h // 2, (h % 2) * 2 * P:(h % 2 + 1) * 2 * P], k_nt[:, h],
                              kq_t[:, h].rearrange("p c n -> p (c n)"), start=True, stop=True)
                last.then_inc(g_a_done, 1)
                fill(3)
                for l in range(LEVELS):
                    part = b_t[:, (l + s) % 2]
                    pe.wait_ge(b_ready, 7 * t + l + 1)
                    if l == 0:
                        for h in range(HEADS):
                            last = mm(acc[:, 3, h * P:(h + 1) * P], part[:, h], ident[:], start=True, stop=True)
                        last.then_inc(b_used, 1)
                        fill(2)
                        continue
                    pe.wait_ge(inv_steps, 13 * t + 2 * l)
                    for h in range(HEADS):
                        last = mm(aux[:, 2, h * P:(h + 1) * P], part[:, h], inv[:, h], start=True, stop=True)
                    last.then_inc(b_used, 1)
                    fill(1)
                    pe.wait_ge(bi_ready, 6 * t + l)
                    if l < LEVELS - 1:
                        for h in range(HEADS):
                            last = mm(aux[:, 0, h * P:(h + 1) * P], inv_t[:, h], bi[:, h], start=True, stop=True)
                        last.then_inc(u_done, 1)
                    for h in range(HEADS):
                        last = mm(aux[:, 1, h * P:(h + 1) * P], bi[:, h], inv_t[:, h], start=True, stop=True)
                    last.then_inc(u_done, 1)
                    fill(2)
                pe.wait_ge(inv_steps, 13 * t + 13)
                pe.wait_ge(g_decay_exp, t + 1)
                for h in range(HEADS):
                    last = mm(acc[:, 2, h * P:(h + 1) * P], kb_dec[:, h], inv_t[:, h], start=True, stop=True)
                last.then_inc(w_done, 1)
                fill(2)
                pe.wait_ge(w_ready, t + 1)
                pe.wait_ge(g_state_ready, t + 1)
                for h in range(HEADS):
                    mm(acc[:, 3, h * P:(h + 1) * P], inv_t[:, h], v_b[:, h], start=True, stop=False)
                    last = mm(acc[:, 3, h * P:(h + 1) * P], w_t[:, h], g_state[:, h], start=False, stop=True)
                last.then_inc(v_done, 1)
                fill(2)
                pe.wait_ge(v_ready, t + 2)
                for h in range(HEADS):
                    mm(aux[:, 3, h * P:(h + 1) * P], q_dt[:, h], g_state[:, h], start=True, stop=False)
                    last = mm(aux[:, 3, h * P:(h + 1) * P], a_t[:, h, 1], v_new[:, h], start=False, stop=True)
                last.then_inc(g_o_done, 1)
                for h in range(HEADS):
                    last = mm(aux[:, 2, h * P:(h + 1) * P], k_e[:, h], v_new[:, h], start=True, stop=True)
                last.then_inc(g_s_done, 1)
                fill(3)
                pe.wait_ge(g_normed, t + 1)
                turn(acc[:, 2], g_on, ident[:]).then_inc(g_o_turned, 1)

            pe.sem_inc(g_decay_done, 1)
            pe.sem_inc(g_turned, 4)
            pe.sem_inc(g_s_done, 1)
            pe.sem_inc(b_used, 1)
            with pe.Fori(0, NT // 2) as i:
                for s in range(2):
                    u = U_MERGE + U_MERGE_RET + s
                    gdn_tile(2 * i + s, s, Filler(2 * i + u, u % 2, 8 * i + 4 * u).fill)

            pe.wait_ge(cmp_loaded, 16 * 5)
            pe.wait_ge(g_out_ready, NT + 1)
            for c in range(2):
                for g in range(2):
                    rows = slice(64 * g, 64 * g + 64)
                    for l in range(CMP_LEN):
                        mm(aux[:, 2 * c + g, 0:NC - 1], w1[rows, c, l], kv_c[rows, c, l:l + CMP_STRIDE * (NC - 2) + 1:CMP_STRIDE],
                           start=(l == 0), stop=(l == CMP_LEN - 1))
                for l in range(CMP_LEN):
                    last = mm(acc[:, 2 + c, 0:1], w1[0:64, c, l], pe_t[0:64, c, l:l + 1],
                              start=(l == 0), stop=(l == CMP_LEN - 1))
                last.then_inc(cmp_hidden_done, 1)
            pe.wait_ge(cmp_hidden_ready, 4)
            for g in range(2):
                mm(acc[64 * g:64 * g + 64, 2, 0:NC - 1], w2[:, 0], hidden[:, 0, g, 0:NC - 1], start=True, stop=True)
                last = mm(acc[0:NC - 1, 3, g * DH:(g + 1) * DH], hidden[:, 1, g, 0:NC - 1], w2[:, 1], start=True, stop=True)
            last.then_inc(cmp_kv_done, 1)

            def bank_of(group):
                if group >= 2:
                    pe.wait_ge(pt_taken_act if group % 2 else pt_taken_dve, group // 2)
                return acc[:, 2 + group % 2]

            def taken(group):
                pe.wait_ge(pt_taken_act if group % 2 else pt_taken_dve, group // 2 + 1)

            def scores_cmp(n):
                pe.wait_ge(n_q_loaded[n % 2], 16 * (n // 2 + 1))
                pe.wait_ge(cmp_kv_ready, 1)
                if n > 0:
                    pe.wait_ge(s_taken, s_uses_cmp(n))
                for g in range(2):
                    rows = slice(64 * g, 64 * g + 64)
                    for h in range(4):
                        last = mm(aux[:, g, h * NC:(h + 1) * NC], n_q[rows, n % 2, h], kc_t[rows, :], start=True, stop=True)
                last.then_inc(s_done, 1)

            def scores_of(e):
                n, g, h = place(e)
                rows = slice(64 * g, 64 * g + 64)
                q = n_q[rows, n % 2, h]
                pe.wait_ge(s_taken, s_uses(e))
                sel, win = blocks(n)
                for at in range(0, sel * P, HALF):
                    end = min(at + HALF, sel * P)
                    mm(aux[:, at // HALF, 0:end - at], q, k_sw[rows, 0, at:end], start=True, stop=True)
                mm(aux[:, 2, 0:win * P], q, k_sw[rows, 1, (n + 1 - win) * P:(n + 1) * P], start=True,
                   stop=True).then_inc(s_done, 1)

            def outputs_cmp(n):
                pe.wait_ge(cmp_exp_done, n + 1)
                first = GROUP_AT_CMP[n]
                for g in range(2):
                    bank = bank_of(first + g)
                    for h in range(4):
                        last = nc.tensor.transpose(bank[0:NC, h * P:(h + 1) * P], cmp_s[:, 4 * g + h], ident[:])
                    last.then_inc(pt_turned, 1)
                for g in range(2):
                    taken(first + g)
                if n > 0:
                    pe.wait_ge(o_taken, o_uses_cmp(n))
                for h in range(NH):
                    last = mm(aux[:, 3, h * DH:(h + 1) * DH], cmp_pt[0:NC, h], vc[0:NC, (h // 4) * DH:(h // 4 + 1) * DH],
                              start=True, stop=True)
                last.then_inc(o_done, 1)

            def turn_tile(n):
                pe.wait_ge(o_taken, o_uses_turn(n))
                turn(aux[:, 3], n_o[:, n % 2].rearrange("p h g d -> p h (g d)"), ident[:]).then_inc(o_done, 1)

            def outputs_of(e, fill):
                n, g, h = place(e)
                sel, win = blocks(n)
                total = sel + win
                pe.wait_ge(exp_done, 2 * (e + 1))
                groups = range(0, total, 4)
                for at in groups:
                    bank = bank_of(GROUP_AT[e] + at // 4)
                    for j in range(at, min(at + 4, total)):
                        col = j * P if j < sel else S + (j - sel) * P
                        last = nc.tensor.transpose(bank[:, (j - at) * P:(j - at + 1) * P], scores[:, e % 2, col:col + P], ident[:])
                    last.then_inc(pt_turned, 1)
                    if at == 0:
                        fill(2)
                fill(2)
                if e % NH == 0 and n > 0:
                    turn_tile(n - 1)
                pe.wait_ge(o_taken, o_uses(e))
                for j in range(total):
                    if j % 4 == 0:
                        taken(GROUP_AT[e] + j // 4)
                    b, i, k = (0, j, j) if j < sel else (1, j - sel, n + 1 - win + j - sel)
                    last = mm(aux[:, 3, b * DH:(b + 1) * DH], p_t[:, e % 2, j],
                              vsw[:, k, b * P + g * DH:b * P + (g + 1) * DH], start=(i == 0),
                              stop=(i == (sel, win)[b] - 1))
                last.then_inc(o_done, 1)

            class PleFiller:

                def __init__(self):
                    self.n = 0

                def fill(self, steps):
                    for _ in range(steps):
                        k, j, b, u = self.n % KD, self.n // KD % 2, self.n // 16 % 4, U_PLE + self.n // 64
                        if self.n % 64 == 0:
                            pe.wait_ge(w_split, u + 1)
                        if j == 0 and k == 0:
                            pe.wait_ge(acc_freed, 4 * u + b + 3)
                        t = 2 * b + j
                        hi = w_hi[:, u % 2, k * UC:(k + 1) * UC]
                        lo = w_lo[:, u % 2, k * UC:(k + 1) * UC]
                        last = parts(acc[:, b % 2, j * UC:(j + 1) * UC], x_hi[:, k, t * P:(t + 1) * P],
                                     x_lo[:, k, t * P:(t + 1) * P], hi, lo, k == 0, k == KD - 1)
                        if j == 1 and k == KD - 1:
                            last.then_inc(acc_ready, 1)
                        self.n += 1

            ple = PleFiller()
            scores_cmp(0)
            outputs_cmp(0)
            scores_of(0)
            for e in range(STEPS):
                n, h = e // NH, e % NH
                if e + 1 < STEPS:
                    scores_of(e + 1)
                outputs_of(e, ple.fill)
                if n < NT - 1 and h == 1:
                    scores_cmp(n + 1)
                if n < NT - 1 and h == 5:
                    outputs_cmp(n + 1)
            turn_tile(NT - 1)

            bank = [acc[:, b] for b in range(4)] + [aux[:, b] for b in range(4)]
            pe.wait_ge(acc_freed, 4 * U_BR + 4)
            pe.wait_ge(s_taken, s_uses(STEPS - 1) + 1)
            pe.wait_ge(pt_taken_dve, GROUP_END // 2)
            pe.wait_ge(pt_taken_act, GROUP_END // 2)
            with pe.Fori(0, KD // 2) as i:
                for s in range(2):
                    ct = 2 * i + s
                    hi = w_hi[:, s].rearrange("p (k n) -> p k n", n=P)
                    lo = w_lo[:, s].rearrange("p (k n) -> p k n", n=P)
                    pe.wait_ge(w_split, ct + U_BR + 1)
                    for h in range(2):
                        cols = slice(h * HALF, (h + 1) * HALF)
                        for b in range(3):
                            pe.wait_ge(br_taken, 6 * ct + 3 * h + b + 1)
                            for k in range(HEADS):
                                o_h, o_l, j = (x_hi, x_lo, HEADS * b + k) if b < 2 else (oc_hi, oc_lo, k)
                                if s == 0 and h == 0:
                                    pe.wait_ge(o_split, HEADS * b + k + 1)
                                last = parts(bank[3 * h + b], hi[:, HEADS * b + k], lo[:, HEADS * b + k],
                                             o_h[:, j, cols], o_l[:, j, cols], k == 0, k == HEADS - 1)
                            last.then_inc(br_done, 1)

            pe.wait_ge(br_taken, 6 * KD + 6)
            pe.wait_ge(o_taken, o_uses_turn(NT - 1) + 1)

            def out_product(n, t):
                part_hi, part_lo = (w_hi, w_lo) if n < 2 else (wo_hi, wo_lo)
                for k in range(KD):
                    last = parts(bank[t][:, (n % 2) * UC:(n % 2 + 1) * UC], x_hi[:, k, t * P:(t + 1) * P],
                                 x_lo[:, k, t * P:(t + 1) * P], part_hi[:, n % 2, k * UC:(k + 1) * UC],
                                 part_lo[:, n % 2, k * UC:(k + 1) * UC], k == 0, k == KD - 1)
                return last

            for n in range(2):
                pe.wait_ge(w_split, U_OUT + n + 1)
                for t in range(NT):
                    pe.wait_ge(mixed_split, t + 1)
                    last = out_product(n, t)
                    if n == 1:
                        last.then_inc(out_done, 1)
            pe.wait_ge(w_split, U_OUT + 4)
            for t in range(NT):
                pe.wait_ge(out_taken, t + 1)
                out_product(2, t)
                out_product(3, t).then_inc(out_done, 1)

        @block.scalar
        def _(act):
            act.sem_inc(acc_freed, 4)
            act.sem_inc(turned_freed, 4)

            for n, dst in enumerate(first_parts(p_hi, ple_hi, x_hi)):
                act.wait_ge(raw_loaded[n % 2], 16 * (n // 2 + 1))
                act.activation(dst, w_raw[:, n % 2].rearrange("p (k n) -> p k n", n=dst.shape[2]),
                               ACT.Copy).then_inc(first_hi, 1)

            def to_stage(bank0, b, func, stores, dst):
                act.wait_ge(acc_ready, bank0 + b + 1)
                act.wait_ge(stored[b], stores)
                act.activation(stage[:, b], acc[:, b], func).then_inc(acc_freed, 1)
                act.wait_ge(acc_freed, bank0 + b + 5)
                act.dma_start(dst, stage[:, b].rearrange("p (j n) -> p j n", j=2)).then_inc(stored[b], 16)

            with act.Fori(0, 3) as i:
                for s in range(2):
                    for b in range(4):
                        cols = ret_dram[2 * b:2 * b + 2, :, bass.ds(2 * UC * i + UC * s, UC)]
                        to_stage(8 * i + 4 * s, b, ACT.Copy, 32 * i + 16 * (s + 4), cols.rearrange("t p n -> p t n"))
            for u, dst in ((U_VSW, vsw), (U_SMALL, small)):
                for b in range(4):
                    act.wait_ge(acc_ready, 4 * u + b + 1)
                    width = dst.shape[2]
                    act.activation(dst[:, 2 * b:2 * b + 2, :],
                                   acc[:, b].rearrange("p (j n) -> p j n", j=2)[:, :, 0:width],
                                   ACT.Copy).then_inc(acc_freed, 1)
            with act.Fori(0, 2) as i:
                for s in range(2):
                    for b in range(4):
                        half = nsa_dram[bass.ds(4 * i + 2 * s + b // 2, 1), :, (b % 2) * HALF:(b % 2 + 1) * HALF]
                        to_stage(8 * i + 4 * (U_NSA + s), b, ACT.Copy, 32 * i + 16 * (10 + s),
                                 half.rearrange("o p (j n) -> (o p) j n", j=2))
            with act.Fori(0, 3) as i:
                for s in range(2):
                    for b in range(4):
                        half = zt_dram[bass.ds(4 * i + 2 * s + b // 2, 1), :, (b % 2) * HALF:(b % 2 + 1) * HALF]
                        to_stage(8 * i + 4 * (U_Z + s), b, ACT.Silu, 32 * i + 16 * (14 + s),
                                 half.rearrange("o p (j n) -> (o p) j n", j=2))

            act.wait_ge(zeroed, 1)

            def conv_unit(g):
                for b in range(4):
                    c, h = b // 2, b % 2
                    act.wait_ge(acc_ready, 4 * g + 4 * U_GDN + b + 1)
                    act.wait_ge(conv_done, 2 * g + c + 1)
                    act.activation(conv_in[:, c, CONV_K - 1 + h * HALF:CONV_K - 1 + (h + 1) * HALF],
                                   acc[:, b], ACT.Copy).then_inc(acc_freed, 1)

            def silu_unit(g):
                for c in range(2):
                    act.wait_ge(conv_done, 2 * g + c + 3)
                    act.activation(conv_y[:, c], conv_y[:, c], ACT.Silu).then_inc(silu_done, 1)

            def store_unit(g):
                act.wait_ge(gdn_staged, g + 1)
                act.dma_start(gdn_dram[:, :, bass.ds(UC * g, UC)].rearrange("t p n -> p t n"),
                              gdn_stage[:]).then_inc(gdn_stored, 16)

            act.sem_inc(conv_done, 2)
            act.sem_inc(gdn_stored, 16)
            conv_unit(0)
            silu_unit(0)
            with act.Fori(0, 5) as g:
                conv_unit(g + 1)
                silu_unit(g + 1)
                store_unit(g)
            store_unit(5)

            def merge_bank(u, b, bank0, stores):
                act.wait_ge(acc_ready, bank0 + b + 1)
                act.wait_ge(stored[b], stores)
                act.activation(stage[:, b], acc[:, b % 2], ACT.Copy).then_inc(acc_freed, 1)
                act.wait_ge(acc_freed, bank0 + b + 5)
                act.dma_start(merge_dram[bass.ds(2 * u + b // 2, 1), :, (b % 2) * HALF:(b % 2 + 1) * HALF]
                              .rearrange("o p n -> (o p) n"), stage[:, b]).then_inc(stored[b], 16)

            act.sem_inc(qk_t_ready, 2)
            with act.Fori(0, NT // 4) as i:
                for q in range(4):
                    s = q % 2
                    t = 4 * i + q
                    for n, dst in enumerate((q_t, k_t)):
                        act.wait_ge(qk_turned, 2 * t + n + 3)
                        act.wait_ge(ret_s_done, t + 1)
                        act.wait_ge(q_start_ready, t + 1)
                        act.activation(dst[:].rearrange("p h n -> p (h n)"), acc[:, 2 + n],
                                       ACT.Copy).then_inc(qk_t_ready, 1)
                    merge_bank(2 * i + q // 2, 2 * s, 8 * i + 4 * (U_MERGE + q // 2), 32 * i + 16 * (20 + q // 2))
                    act.wait_ge(ret_stats_done, t + 1)
                    act.activation(ret_std[:], ret_mv[:, :, 1], ACT.Sqrt).then_inc(ret_std_ready, 1)
                    merge_bank(2 * i + q // 2, 2 * s + 1, 8 * i + 4 * (U_MERGE + q // 2), 32 * i + 16 * (20 + q // 2))
                    act.wait_ge(ret_out_ready, t + 3)
                    act.dma_start(oa_dram[:, :, bass.ds(P * t, P)].rearrange("h p n -> p h n"),
                                  ret_out[:, s]).then_inc(ret_stored[s], 16)
            for s in range(2):
                act.wait_ge(ret_stored[s], 16 * 5)

            act.activation(beta[:], small[:, :, 0:4], ACT.Sigmoid).then_inc(prep_act, 1)
            act.activation(gates[:], small[:, :, 8:32], ACT.Sigmoid).then_inc(prep_act, 1)
            act.wait_ge(prep_dve, PREP_ABS)
            act.activation(gy[:], gy[:], ACT.Exp, scale=-1.0).then_inc(prep_act, 1)
            act.wait_ge(g_const, 16 * 5)
            act.activation(ea[:], a_log[:], ACT.Exp).then_inc(prep_act, 1)
            act.wait_ge(prep_pe, 1)
            act.activation(decays[:].rearrange("p c n -> p (c n)"), aux[:, 0, 0:96], ACT.Exp).then_inc(prep_act, 1)
            act.wait_ge(prep_dve, PREP_SS)
            act.activation(rn_q[:], rn_q[:], ACT.Sqrt).then_inc(prep_act, 1)
            act.activation(rn_k[:], rn_k[:], ACT.Sqrt).then_inc(prep_act, 1)

            act.sem_inc(v_ready, 1)
            act.sem_inc(g_o_ready, 1)
            with act.Fori(0, NT // 2) as i:
                for s in range(2):
                    t = 2 * i + s
                    u = U_MERGE_RET + s

                    def merge(b):
                        merge_bank(2 * i + u, b, 8 * i + 4 * (U_MERGE + u), 32 * i + 16 * (20 + u))

                    def flat(x):
                        return x.rearrange("p h n -> p (h n)")

                    act.wait_ge(g_turned, 4 * t + 5)
                    act.activation(flat(k_nt[:]), acc[:, 2], ACT.Copy).then_inc(g_t_act, 1)
                    act.wait_ge(g_turned, 4 * t + 8)
                    act.activation(flat(q_dt[:]), aux[:, 3], ACT.Copy).then_inc(g_t_act, 1)
                    act.wait_ge(g_decay_done, t + 2)
                    act.activation(flat(decay_t[:]), acc[:, 2], ACT.Exp).then_inc(g_decay_exp, 1)
                    for l in range(1, LEVELS):
                        act.wait_ge(b_used, 7 * t + l + 2)
                        if l > 1:
                            act.wait_ge(u_done, 11 * t + 2 * l - 2)
                        act.activation(flat(bi[:]), aux[:, 2], ACT.Copy).then_inc(bi_ready, 1)
                        if l in (1, 3, 6):
                            merge((1, 3, 6).index(l))
                    act.wait_ge(w_done, t + 1)
                    act.activation(flat(w_t[:]), acc[:, 2], ACT.Copy, scale=-1.0).then_inc(w_ready, 1)
                    act.wait_ge(v_done, t + 1)
                    act.activation(flat(v_new[:]), acc[:, 3], ACT.Copy).then_inc(v_ready, 1)
                    act.wait_ge(g_o_done, t + 1)
                    act.activation(flat(g_o[:]), aux[:, 3], ACT.Copy).then_inc(g_o_ready, 1)
                    merge(3)
                    act.wait_ge(g_ss_ready, t + 1)
                    act.activation(g_std[:], g_ss[:], ACT.Sqrt).then_inc(g_std_ready, 1)
                    act.wait_ge(g_out_ready, t + 2)
                    act.dma_start(ob_dram[:, :, bass.ds(P * t, P)].rearrange("h p n -> p h n"),
                                  g_out[:, s]).then_inc(g_stored[s], 16)

            act.wait_ge(prep_act, 7)
            for c in range(2):
                act.wait_ge(cmp_hidden_done, c + 1)
                act.activation(cmp_bias[:, c:c + 1], acc[:, 2 + c, 0:1], ACT.Copy).then_inc(cmp_bias_ready, 1)
            act.wait_ge(cmp_bias_ready, 2)
            for c in range(2):
                for g in range(2):
                    act.activation(hidden[:, c, g, 0:NC - 1], aux[:, 2 * c + g, 0:NC - 1], ACT.Gelu_apprx_tanh,
                                   bias=cmp_bias[:, c:c + 1]).then_inc(cmp_hidden_ready, 1)

            def exp_of(e):
                n = e // NH
                act.wait_ge(max_ready, e + 1)
                for b, (at, width) in enumerate(zip((0, S), (w * P for w in blocks(n)))):
                    part = scores[:, e % 2, at:at + width]
                    act.activation(part, part, ACT.Exp, bias=n_nmax[:, e % 2, b:b + 1], scale=SCALE,
                                   accum_out=n_sum[:, e % 2, b:b + 1]).then_inc(exp_done, 1)

            def exp_cmp(n):
                act.wait_ge(cmp_shifted, n + 1)
                act.activation(cmp_s[:], cmp_s[:], ACT.Exp, scale=SCALE).then_inc(cmp_exp_done, 1)

            def take_groups_cmp(n):
                for g in range(2):
                    group = GROUP_AT_CMP[n] + g
                    if group % 2:
                        act.wait_ge(pt_turned, group + 1)
                        act.activation(cmp_pt[0:NC, 4 * g:4 * g + 4].rearrange("p h n -> p (h n)"),
                                       acc[0:NC, 3], ACT.Copy).then_inc(pt_taken_act, 1)

            def take_groups(e):
                total = sum(blocks(e // NH))
                for at in range(0, total, 4):
                    group = GROUP_AT[e] + at // 4
                    if group % 2:
                        width = min(4, total - at) * P
                        act.wait_ge(pt_turned, group + 1)
                        if e >= 2:
                            act.wait_ge(o_done, o_uses(e - 2) + 1)
                        act.activation(p_t[:, e % 2, at:at + width // P].rearrange("p j n -> p (j n)"),
                                       acc[:, 3, 0:width], ACT.Copy).then_inc(pt_taken_act, 1)

            def store_tile(n):
                act.wait_ge(o_taken, o_uses_turn(n) + 1)
                act.dma_start(oc_dram[:, :, n * P:(n + 1) * P].rearrange("h p n -> p h n"),
                              n_out[:, n % 2]).then_inc(n_stored[n % 2], 16)

            def ple_bank(u, b):
                act.wait_ge(acc_ready, 4 * u + b + 1)
                act.wait_ge(stored[b], 16 * (20 + u - U_MERGE))
                act.activation(stage[:, b], acc[:, b % 2], ACT.Copy).then_inc(acc_freed, 1)
                act.wait_ge(acc_freed, 4 * u + b + 5)
                cols = pleg_dram[2 * b:2 * b + 2, :, (u - U_PLE) * UC:(u - U_PLE + 1) * UC]
                act.dma_start(cols.rearrange("t p n -> p t n"),
                              stage[:, b].rearrange("p (j n) -> p j n", j=2)).then_inc(stored[b], 16)

            exp_cmp(0)
            take_groups_cmp(0)
            exp_of(0)
            for e in range(STEPS):
                n, h = e // NH, e % NH
                take_groups(e)
                if e + 1 < STEPS:
                    exp_of(e + 1)
                if n < NT - 1 and h == 2:
                    exp_cmp(n + 1)
                if n < NT - 1 and h == 5:
                    take_groups_cmp(n + 1)
                if h % 4 == 3:
                    ple_bank(U_PLE + n // 2, 2 * (n % 2) + h // 4)
                if h == 0 and n > 0:
                    store_tile(n - 1)
            store_tile(NT - 1)

            act.wait_ge(acc_ready, 4 * U_BR)
            for j in range(KB):
                if j % HEADS == 0:
                    act.wait_ge(o_loaded[j // HEADS], 16)
                hi = x_hi[:, j] if j < 2 * HEADS else oc_hi[:, j - 2 * HEADS]
                act.activation(hi, mixed[:, j % (2 * HEADS)], ACT.Copy).then_inc(o_hi, 1)
            with act.Fori(0, KD) as ct:
                for h in range(2):
                    act.wait_ge(gate_loaded[h], 16 * (ct + 1))
                    act.activation(m_gate[:, h], m_gate[:, h], ACT.Sigmoid).then_inc(gate_ready, 1)
            act.wait_ge(br_done, 6 * KD)
            act.wait_ge(mixed_ready, 2 * KD + 2)
            with act.Fori(0, NT) as t:
                act.activation(x_hi[:, :, bass.ds(P * t, P)], mixed[:, :, bass.ds(P * t, P)], ACT.Copy).then_inc(mixed_hi, 1)
            for h in range(2):
                with act.Fori(0, NT // 2) as i:
                    for s in range(2):
                        act.wait_ge(f_loaded[s], 32 * i + 32 * (h * NT // 2 + 1))
                        act.activation(f_gate[:, s], f_gate[:, s], ACT.Sigmoid).then_inc(f_sigmoid, 1)
            with act.Fori(0, NT // 2) as i:
                for s in range(2):
                    act.wait_ge(ln_var_ready, 2 * i + s + 1)
                    act.activation(ln_std[:, s:s + 1], ln_var[:, s:s + 1], ACT.Sqrt).then_inc(ln_std_ready, 1)

            for b in range(4):
                act.wait_ge(stored[b], 16 * 36)
            for s in range(2):
                act.wait_ge(n_stored[s], 16 * 4)

        @block.vector
        def _(dve):
            his = first_parts(p_hi, ple_hi, x_hi)
            for n, lo in enumerate(first_parts(p_lo, ple_lo, x_lo)):
                dve.wait_ge(first_hi, n + 1)
                dve.tensor_tensor(lo, w_raw[:, n % 2].rearrange("p (k n) -> p k n", n=lo.shape[2]),
                                  his[n].bitcast(F32), ALU.subtract).then_inc(first_split, 1)
                for m in range(4 * (n - 2), 4 * (n - 1)) if n >= 2 else ():
                    dve.wait_ge(ple_ready, m + 1)
                    if m >= 4:
                        dve.wait_ge(stored[m % 4], 16 * (m // 4))
                    dve.tensor_copy(stage[:, m % 4], aux[:, m % 4]).then_inc(ple_out, 1)
            dve.memset(conv_in[:, :, 0:CONV_K - 1], 0.0).then_inc(zeroed, 1)
            dve.wait_ge(zeroed, 1)
            dve.wait_ge(const_loaded, 32)
            st = Steps(dve, dve_steps)

            def conv(g, c):
                dve.wait_ge(acc_freed, 4 * g + 4 * U_GDN + 4 + 2 * (c + 1))
                dve.wait_ge(turned, 4 * g + 2 * (c + 1))
                w = conv_w[:, bass.ds(2 * g + c, 1), :]
                for k in range(CONV_K):
                    src, tap = conv_in[:, c, k:k + S], w[:, 0, k:k + 1]
                    if k == 0:
                        st.step(dve.tensor_scalar(conv_y[:, c], src, tap, None, ALU.mult))
                    else:
                        st.wait()
                        ins = dve.scalar_tensor_tensor(conv_y[:, c], src, tap, conv_y[:, c], ALU.mult, ALU.add)
                        if k < CONV_K - 1:
                            st.step(ins)
                        else:
                            ins.then_inc(conv_done, 1)

            def stage_unit(g):
                dve.wait_ge(gdn_stored, 16 * g + 16)
                for b in range(4):
                    c, h = b // 2, b % 2
                    dve.wait_ge(turned, 4 * g + b + 5)
                    dve.tensor_copy(gdn_stage[:, 4 * h:4 * h + 4, c * P:(c + 1) * P],
                                    aux[:, b].rearrange("p (j n) -> p j n", j=4)).then_inc(turned_freed, 1)
                dve.wait_ge(turned_freed, 4 * g + 8)
                dve.tensor_tensor(gdn_sq[:], gdn_stage[:], gdn_stage[:], ALU.mult).then_inc(gdn_staged, 1)
                dve.wait_ge(gdn_staged, g + 1)
                st.step(dve.tensor_reduce(gdn_ss[:, :, bass.ds(2 * g, 2)],
                                  gdn_sq[:].rearrange("p t (h n) -> p t h n", h=2), AX_X, ALU.add))
                st.wait()

            dve.sem_inc(turned, 4)
            for c in range(2):
                conv(0, c)
            with dve.Fori(0, 5) as g:
                st.enter(g, 7)
                for c in range(2):
                    conv(g + 1, c)
                stage_unit(g)
                st.leave(5, 7)
            stage_unit(5)

            dve.memset(ret_state[:], 0.0).then_inc(ret_state_ready, 1)
            dve.sem_inc(rotated, 1)
            dve.sem_inc(q_start_ready, 1)
            dve.sem_inc(k_end_ready, 1)
            dve.sem_inc(ret_s_ready, 1)
            dve.sem_inc(ret_normed, 1)
            dve.sem_inc(ret_out_ready, 2)
            dve.sem_inc(ret_s_done, 1)
            for q in ret_stored:
                dve.sem_inc(q, 16)
            dve.wait_ge(ret_const, 16 * 4)
            with dve.Fori(0, NT // 4) as i:
                st.enter(i, 4 * 12)
                for q in range(4):
                    s = q % 2
                    t = 4 * i + q
                    dve.wait_ge(rot_parts, 4 * t + 4)
                    dve.wait_ge(qk_turned, 2 * t + 2)
                    dve.wait_ge(k_end_ready, t + 1)
                    out_qk = rot[:].rearrange("p c h e n -> p (c h) e n")
                    st.step(dve.tensor_tensor(out_qk[:, :, 0], rot_tmp[:, 0], rot_tmp[:, 1], ALU.subtract))
                    st.wait()
                    dve.tensor_tensor(out_qk[:, :, 1], rot_tmp[:, 2], rot_tmp[:, 3], ALU.add).then_inc(rotated, 1)
                    dve.wait_ge(qk_t_ready, 2 * t + 3)
                    dve.wait_ge(ret_o_done, t + 2)
                    dve.tensor_tensor(q_start_t[:], q_t[:], q_decay[:], ALU.mult).then_inc(q_start_ready, 1)
                    dve.wait_ge(ret_s_done, t + 2)
                    dve.tensor_tensor(ret_s[:].rearrange("p h n -> p (h n)"), aux[:, 0],
                                      ret_decay[:].rearrange("p h n -> p (h n)"), ALU.mult).then_inc(ret_s_ready, 1)
                    dve.wait_ge(ret_o_done, t + 3)
                    for h in range(HEADS):
                        st.step(dve.bn_stats(ret_stats[:, h], aux[:, 2, h * P:(h + 1) * P]))
                    st.wait()
                    mean, var = ret_mv[:, :, 0], ret_mv[:, :, 1]
                    st.step(dve.tensor_tensor(mean, ret_stats[:, :, 1], ret_stats[:, :, 4], ALU.add))
                    st.step(dve.tensor_tensor(ret_dm[:], ret_stats[:, :, 1], ret_stats[:, :, 4], ALU.subtract))
                    st.step(dve.tensor_tensor(var, ret_stats[:, :, 2], ret_stats[:, :, 5], ALU.add))
                    st.wait()
                    st.step(dve.tensor_scalar(mean, mean, 0.5, None, ALU.mult))
                    st.step(dve.scalar_tensor_tensor(ret_dm[:], ret_dm[:], P / 4, ret_dm[:], ALU.mult, ALU.mult))
                    st.wait()
                    st.step(dve.tensor_tensor(var, var, ret_dm[:], ALU.add))
                    st.wait()
                    dve.tensor_scalar(var, var, 1.0 / P, 1e-5, ALU.mult, ALU.add).then_inc(ret_stats_done, 1)
                    dve.wait_ge(ret_kv_done, t + 2)
                    for h in range(HEADS):
                        ins = dve.scalar_tensor_tensor(ret_state[:, h], ret_state[:, h], chunk_decay(h),
                                                       aux[:, 1, h * P:(h + 1) * P], ALU.mult, ALU.add)
                    ins.then_inc(ret_state_ready, 1)
                    dve.wait_ge(ret_std_ready, t + 1)
                    st.step(dve.reciprocal(ret_rstd[:], ret_std[:]))
                    st.wait()
                    dve.wait_ge(ret_o_turned, t + 1)
                    for h in range(HEADS):
                        ins = dve.tensor_scalar(ret_norm[:, h], aux[:, 2, h * P:(h + 1) * P], ret_mv[:, h, 0:1],
                                                ret_rstd[:, h:h + 1], ALU.subtract, ALU.mult)
                    ins.then_inc(ret_normed, 1)
                    dve.wait_ge(ret_o_turned, t + 2)
                    dve.wait_ge(ret_z_loaded[s], 32 * i + 16 * (q // 2 + 1))
                    dve.wait_ge(ret_stored[s], 32 * i + 16 * (q // 2 + 1))
                    dve.tensor_tensor(ret_out[:, s].rearrange("p h n -> p (h n)"), aux[:, 3],
                                      ret_z[:, s].rearrange("p h n -> p (h n)"), ALU.mult).then_inc(ret_out_ready, 1)
                st.leave(NT // 4, 4 * 12)

            prep = Steps(dve, prep_dve)

            def small_step(ins):
                prep.step(ins)
                prep.wait()

            def tiles(x):
                return x.rearrange("p (t h) -> p t h", h=HEADS)

            def over_tiles(x):
                return x.rearrange("p (o h) -> p o h", o=1).broadcast_to([P, NT, HEADS])

            for q in range(2):
                dve.wait_ge(ret_stored[q], 16 * 5)
            dve.wait_ge(g_const, 16 * 5)
            small_step(dve.tensor_tensor(tiles(ga[:]), small[:, :, 4:8], over_tiles(dt_bias[:]), ALU.add))
            small_step(dve.tensor_scalar(gs[:], ga[:], -1.0, None, ALU.mult))
            small_step(dve.tensor_tensor(gy[:], ga[:], gs[:], ALU.max))
            assert prep.here == PREP_ABS
            dve.wait_ge(prep_act, 3)
            small_step(dve.tensor_scalar(gs[:], gy[:], 2.0, None, ALU.add))
            small_step(dve.reciprocal(gs[:], gs[:]))
            small_step(dve.tensor_tensor(gs[:], gs[:], gy[:], ALU.mult))
            small_step(dve.tensor_tensor(gs2[:], gs[:], gs[:], ALU.mult))
            small_step(dve.tensor_scalar(gpoly[:], gs2[:], 1.0 / ATANH[0], 1.0 / ATANH[1], ALU.mult, ALU.add))
            for n in ATANH[2:]:
                small_step(dve.tensor_tensor(gpoly[:], gpoly[:], gs2[:], ALU.mult))
                small_step(dve.tensor_scalar(gpoly[:], gpoly[:], 1.0 / n, None, ALU.add))
            small_step(dve.scalar_tensor_tensor(gpoly[:], gpoly[:], 2.0, gs[:], ALU.mult, ALU.mult))
            small_step(dve.scalar_tensor_tensor(gpoly[:], ga[:], 0.0, gpoly[:], ALU.max, ALU.add))
            dve.wait_ge(prep_act, 4)
            small_step(dve.tensor_scalar(ea[:], ea[:], -1.0, None, ALU.mult))
            small_step(dve.tensor_tensor(tiles(g_log[:]), tiles(gpoly[:]), over_tiles(ea[:]), ALU.mult))
            assert prep.here == PREP_LOG, prep.here
            small_step(dve.tensor_scalar(tiles(rn_q[:]), gdn_ss[:, :, 0:4], 1e-6, None, ALU.add))
            small_step(dve.tensor_scalar(tiles(rn_k[:]), gdn_ss[:, :, 4:8], 1e-6, None, ALU.add))
            assert prep.here == PREP_SS, prep.here
            dve.wait_ge(prep_act, 7)
            small_step(dve.reciprocal(rn_q[:], rn_q[:]))
            small_step(dve.reciprocal(rn_k[:], rn_k[:]))
            small_step(dve.tensor_scalar(s_q[:], rn_q[:], float(P) ** -0.5, None, ALU.mult))
            small_step(dve.tensor_tensor(s_q_dec[:], s_q[:], decays[:, 0], ALU.mult))
            small_step(dve.tensor_tensor(s_k_beta[:], rn_k[:], beta_flat, ALU.mult))
            small_step(dve.tensor_tensor(s_k_beta_dec[:], s_k_beta[:], decays[:, 0], ALU.mult))
            small_step(dve.memset(g_state[:], 0.0))
            small_step(dve.tensor_tensor(s_k_end[:], rn_k[:], decays[:, 1], ALU.mult))
            assert prep.here == PREP_DVE, prep.here

            dve.sem_inc(g_state_ready, 1)
            dve.sem_inc(g_scaled, 3)
            dve.sem_inc(g_scaled_pool, 5)
            dve.sem_inc(g_out_ready, 1)
            for q in g_stored:
                dve.sem_inc(q, 16)

            def by_head(scalars, t):
                return scalars[:, bass.ds(HEADS * t, HEADS)].rearrange("p (h o) -> p h o", o=1).broadcast_to([P, HEADS, P])

            def heads(bank):
                return bank.rearrange("p (h n) -> p h n", h=HEADS)

            eye = ident[:].rearrange("p (o n) -> p o n", o=1).broadcast_to([P, HEADS, P])
            with dve.Fori(0, NT // 2) as i:
                st.enter(i, 2 * 3)
                for s in range(2):
                    t = 2 * i + s
                    dve.wait_ge(g_loaded, 16 * (t + 1))
                    dve.wait_ge(g_turned, 4 * t + 4)
                    for dst, c, scalars in ((k_n, 1, rn_k), (k_b, 1, s_k_beta), (q_n, 0, s_q)):
                        dve.tensor_tensor(dst[:], g_in[:, c], by_head(scalars, t), ALU.mult).then_inc(g_scaled, 1)
                    dve.wait_ge(g_turned, 4 * t + 7)
                    dve.tensor_copy(kq_t[:, :, 0], heads(acc[:, 3])).then_inc(g_t_dve, 1)
                    dve.tensor_copy(kq_t[:, :, 1], heads(aux[:, 2])).then_inc(g_t_dve, 1)
                    dve.wait_ge(g_a_done, t + 1)
                    dve.wait_ge(g_decay_ready, t + 1)
                    for h in range(HEADS):
                        ins = dve.tensor_tensor(
                            a_t[:, h], aux[:, h // 2, (h % 2) * 2 * P:(h % 2 + 1) * 2 * P].rearrange("p (c n) -> p c n", c=2),
                            decay_t[:, h:h + 1].broadcast_to([P, 2, P]), ALU.mult)
                    ins.then_inc(g_a_ready, 1)
                    dve.wait_ge(b_used, 7 * t + 2)
                    dve.tensor_tensor(inv[:], eye, heads(acc[:, 3]), ALU.subtract).then_inc(inv_steps, 1)
                    dve.tensor_tensor(inv_t[:], eye, b_t[:, s], ALU.subtract).then_inc(inv_steps, 1)
                    for l in range(1, LEVELS):
                        dve.wait_ge(inv_steps, 13 * t + 2 * l)
                        if l < LEVELS - 1:
                            dve.wait_ge(u_done, 11 * t + 2 * l - 1)
                            dve.tensor_tensor(inv[:], inv[:], heads(aux[:, 0]), ALU.subtract).then_inc(inv_steps, 1)
                            dve.wait_ge(u_done, 11 * t + 2 * l)
                            dve.tensor_tensor(inv_t[:], inv_t[:], heads(aux[:, 1]), ALU.subtract).then_inc(inv_steps, 1)
                        else:
                            dve.wait_ge(u_done, 11 * t + 11)
                            dve.tensor_tensor(inv_t[:], inv_t[:], heads(aux[:, 1]), ALU.subtract).then_inc(inv_steps, 1)
                    dve.wait_ge(g_s_done, t + 2)
                    for h in range(HEADS):
                        ins = dve.scalar_tensor_tensor(g_state[:, h], g_state[:, h], decays[:, 2, bass.ds(HEADS * t + h, 1)],
                                                       aux[:, 2, h * P:(h + 1) * P], ALU.mult, ALU.add)
                    ins.then_inc(g_state_ready, 1)
                    dve.wait_ge(g_o_ready, t + 2)
                    st.step(dve.tensor_tensor(g_sq[:], g_o[:], g_o[:], ALU.mult))
                    st.wait()
                    st.step(dve.tensor_reduce(g_ss[:], g_sq[:], AX_X, ALU.add))
                    st.wait()
                    dve.tensor_scalar(g_ss[:], g_ss[:], 1.0 / P, 1e-6, ALU.mult, ALU.add).then_inc(g_ss_ready, 1)
                    dve.wait_ge(g_std_ready, t + 1)
                    st.step(dve.reciprocal(g_rstd[:], g_std[:]))
                    st.wait()
                    dve.tensor_tensor(g_on[:], g_o[:], g_rstd[:].rearrange("p (h o) -> p h o", o=1).broadcast_to([P, HEADS, P]),
                                      ALU.mult).then_inc(g_normed, 1)
                    dve.wait_ge(g_o_turned, t + 1)
                    dve.wait_ge(g_z_loaded, 16 * (t + 1))
                    dve.wait_ge(g_stored[s], 16 * i + 16)
                    dve.scalar_tensor_tensor(g_out[:, s].rearrange("p h n -> p (h n)"), acc[:, 2], norm_w[:, 0:1],
                                             g_z[:].rearrange("p h n -> p (h n)"), ALU.mult, ALU.mult).then_inc(g_out_ready, 1)
                st.leave(NT // 2, 2 * 3)

            ns = Steps(dve, nsa_steps)

            def chained(ins):
                ns.step(ins)
                ns.wait()

            for q in range(2):
                dve.wait_ge(g_stored[q], 16 * 5)
            ns.step(dve.memset(kc_t[:], 0.0))
            chained(dve.memset(vc[:], 0.0))
            dve.wait_ge(cmp_kv_done, 1)
            ns.step(dve.tensor_copy(kc_t[:, 0:NC - 1], acc[:, 2, 0:NC - 1]))
            chained(dve.tensor_copy(vc[0:NC - 1, :], acc[0:NC - 1, 3, 0:2 * DH]))
            dve.sem_inc(cmp_kv_ready, 1)
            dve.wait_ge(n_const, 16 * 7)

            def take_cmp(n):
                dve.wait_ge(s_done, s_uses_cmp(n) + 1)
                if n > 0:
                    dve.wait_ge(o_done, o_uses_cmp(n - 1) + 1)
                mask = cmp_mask[:, n:n + 1, :].broadcast_to([P, 4, NC])
                for g in range(2):
                    ins = dve.tensor_tensor(cmp_s[:, 4 * g:4 * g + 4], aux[:, g, 0:4 * NC].rearrange("p (h c) -> p h c", h=4),
                                            mask, ALU.add)
                    ins.then_inc(s_taken, 1) if g else ns.step(ins)
                ns.wait()
                dve.wait_ge(s_taken, s_uses_cmp(n) + 1)
                chained(dve.tensor_reduce(cmp_max[:], cmp_s[:], AX_X, ALU.max))
                dve.tensor_tensor(cmp_s[:], cmp_s[:], cmp_max[:].rearrange("p (h o) -> p h o", o=1).broadcast_to([P, NH, NC]),
                                  ALU.subtract).then_inc(cmp_shifted, 1)

            def select(n):
                dve.wait_ge(cmp_exp_done, n + 1)
                chained(dve.tensor_reduce(cmp_rsum[:], cmp_s[:], AX_X, ALU.add))
                chained(dve.reciprocal(cmp_rsum[:], cmp_rsum[:]))
                gate = gates[:, n].rearrange("p (h b) -> p h b", b=3)[:, :, 0]
                ns.step(dve.tensor_tensor(cmp_coef[:], cmp_rsum[:], gate, ALU.mult))
                if n == 0:
                    ns.wait()
                    ns.step(dve.tensor_scalar(cmp_coef[:], cmp_coef[:], row_valid[:, 0:1], None, ALU.mult))
                if n < N_SEL * DH // P:
                    return
                chained(dve.tensor_tensor(cmp_pn[:], cmp_s[:], cmp_rsum[:].rearrange("p (h o) -> p h o", o=1)
                                          .broadcast_to([P, NH, NC]), ALU.mult))
                chained(dve.tensor_reduce(cmp_pg[:], cmp_pn[:].rearrange("p (g h) c -> p g c h", g=2), AX_X, ALU.add))
                chained(dve.tensor_reduce(imp[:], cmp_pg[:].rearrange("p g (j c) -> p g j c", c=4), AX_X, ALU.add))
                chained(dve.tensor_tensor(imp[:, :, 1:16], imp[:, :, 1:16],
                                          cmp_pg[:].rearrange("p g (j c) -> p g j c", c=4)[:, :, 0:15, 3], ALU.add))
                chained(dve.tensor_tensor(imp[:], imp[:], rank_keep[:, n:n + 1, :].broadcast_to([P, 2, 16]), ALU.mult))
                chained(dve.tensor_tensor(imp[:], imp[:], rank_add[:, n:n + 1, :].broadcast_to([P, 2, 16]), ALU.add))
                for g in range(2):
                    other = imp[:, g:g + 1, :].broadcast_to([P, 16, 16])
                    own = imp[:, g].rearrange("p (j o) -> p j o", o=1).broadcast_to([P, 16, 16])
                    ns.step(dve.tensor_tensor(beats[:, g], other, own, ALU.is_gt))
                    ns.step(dve.tensor_tensor(ties[:, g], other, own, ALU.is_equal))
                ns.wait()
                for g in range(2):
                    ns.step(dve.tensor_tensor(ties[:, g], ties[:, g], earlier[:], ALU.mult))
                ns.wait()
                chained(dve.tensor_tensor(beats, beats, ties[:], ALU.add))
                chained(dve.tensor_reduce(n_beat[:], beats, AX_X, ALU.add))
                dve.wait_ge(mask_ready, 2 * (n - 4)) if n > 4 else None
                dve.tensor_scalar(sel_bias[:], n_beat[:], N_SEL - 0.5, NEG, ALU.is_ge, ALU.mult).then_inc(sel_ready, 1)

            def take(e):
                n, g, h = place(e)
                sel, win = blocks(n)
                dve.wait_ge(s_done, s_uses(e) + 1)
                if e >= 2:
                    dve.wait_ge(pt_turned, GROUP_AT[e - 2] + -(-sum(blocks((e - 2) // NH)) // 4))
                if n >= 4:
                    dve.wait_ge(mask_ready, 2 * (n - 4) + g + 1)
                    mask = sel_mask[:, g, 0:sel * P]
                else:
                    mask = causal_wide[:, S - sel * P:S]
                raw = aux[:, 0:2].rearrange("p b n -> p (b n)")[:, 0:sel * P]
                ns.step(dve.tensor_tensor_reduce(scores[:, e % 2, 0:sel * P], raw, mask, 1.0, -3e38, ALU.add, ALU.max,
                                                 n_max[:, e % 2, 0:1]))
                dve.tensor_tensor_reduce(scores[:, e % 2, S:S + win * P], aux[:, 2, 0:win * P],
                                         win_mask[:, (3 - win) * P:3 * P], 1.0, -3e38, ALU.add, ALU.max,
                                         n_max[:, e % 2, 1:2]).then_inc(s_taken, 1)
                ns.wait()
                dve.wait_ge(s_taken, s_uses(e) + 1)
                dve.tensor_scalar(n_nmax[:, e % 2], n_max[:, e % 2], -SCALE, None, ALU.mult).then_inc(max_ready, 1)

            def take_groups_cmp(n):
                for g in range(2):
                    group = GROUP_AT_CMP[n] + g
                    if group % 2 == 0:
                        dve.wait_ge(pt_turned, group + 1)
                        dve.tensor_copy(cmp_pt[0:NC, 4 * g:4 * g + 4].rearrange("p h n -> p (h n)"),
                                        acc[0:NC, 2]).then_inc(pt_taken_dve, 1)

            def take_groups(e):
                total = sum(blocks(e // NH))
                for at in range(0, total, 4):
                    group = GROUP_AT[e] + at // 4
                    if group % 2 == 0:
                        width = min(4, total - at) * P
                        dve.wait_ge(pt_turned, group + 1)
                        dve.tensor_copy(p_t[:, e % 2, at:at + width // P].rearrange("p j n -> p (j n)"),
                                        acc[:, 2, 0:width]).then_inc(pt_taken_dve, 1)

            def gate_cmp(n):
                dve.wait_ge(o_done, o_uses_cmp(n) + 1)
                if n >= 2:
                    dve.wait_ge(o_done, o_uses_turn(n - 2) + 1)
                ns.wait()
                dve.tensor_tensor(n_o[:, n % 2].rearrange("p h g d -> p g h d"),
                                  aux[:, 3].rearrange("p (g h d) -> p g h d", g=2, h=4),
                                  cmp_coef[:].rearrange("p (g h o) -> p g h o", g=2, o=1).broadcast_to([P, 2, 4, DH]),
                                  ALU.mult).then_inc(o_taken, 1)

            def gate(e):
                n, g, h = place(e)
                head = 4 * g + h
                dve.wait_ge(exp_done, 2 * (e + 1))
                chained(dve.reciprocal(n_coef[:, e % 2], n_sum[:, e % 2]))
                chained(dve.tensor_tensor(n_coef[:, e % 2], n_coef[:, e % 2], gates[:, n, 3 * head + 1:3 * head + 3], ALU.mult))
                dve.wait_ge(o_done, o_uses(e) + 1)
                dst = n_o[:, n % 2, h, g]
                if head == 0:
                    dve.wait_ge(o_taken, o_uses_cmp(n) + 1)
                chained(dve.scalar_tensor_tensor(dst, aux[:, 3, 0:DH], n_coef[:, e % 2, 0:1], dst, ALU.mult, ALU.add))
                dve.scalar_tensor_tensor(dst, aux[:, 3, DH:2 * DH], n_coef[:, e % 2, 1:2], dst, ALU.mult,
                                         ALU.add).then_inc(o_taken, 1)

            def gate_tile(n):
                dve.wait_ge(o_done, o_uses_turn(n) + 1)
                dve.wait_ge(n_z_loaded[n % 2], 16 * (n // 2 + 1))
                if n >= 2:
                    dve.wait_ge(n_stored[n % 2], 16 * (n // 2))
                dve.tensor_tensor(n_out[:, n % 2].rearrange("p h n -> p (h n)"), aux[:, 3],
                                  n_z[:, n % 2].rearrange("p h n -> p (h n)"), ALU.mult).then_inc(o_taken, 1)

            take_cmp(0)
            select(0)
            take_groups_cmp(0)
            gate_cmp(0)
            take(0)
            for e in range(STEPS):
                n, h = e // NH, e % NH
                if e + 1 < STEPS:
                    take(e + 1)
                take_groups(e)
                if h == 0 and n > 0:
                    gate_tile(n - 1)
                gate(e)
                if n < NT - 1 and h == 1:
                    take_cmp(n + 1)
                if n < NT - 1 and h == 3:
                    select(n + 1)
                if n < NT - 1 and h == 5:
                    take_groups_cmp(n + 1)
                    gate_cmp(n + 1)
            gate_tile(NT - 1)

            for j in range(KB):
                dve.wait_ge(o_hi, j + 1)
                hi, lo = (x_hi[:, j], x_lo[:, j]) if j < 2 * HEADS else (oc_hi[:, j - 2 * HEADS], oc_lo[:, j - 2 * HEADS])
                dve.tensor_tensor(lo, mixed[:, j % (2 * HEADS)], hi.bitcast(F32), ALU.subtract).then_inc(o_split, 1)
            dve.sem_inc(mixed_ready, 2)
            dve.sem_inc(br_taken, 6)
            dve.wait_ge(o_split, KB)
            fs = Steps(dve, fin_steps)
            with dve.Fori(0, KD) as ct:
                fs.enter(ct, 2)
                for h in range(2):
                    dve.wait_ge(gate_ready, 2 * ct + h + 1)
                    for b in range(3):
                        dve.wait_ge(br_done, 6 * ct + 3 * h + b + 1)
                        src = (acc if 3 * h + b < 4 else aux)[:, (3 * h + b) % 4]
                        dve.tensor_tensor(m_gate[:, h, b], m_gate[:, h, b], src, ALU.mult).then_inc(br_taken, 1)
                    dst = mixed[:, bass.ds(ct, 1), h * HALF:(h + 1) * HALF].rearrange("p o n -> p (o n)")
                    dve.wait_ge(br_taken, 6 * ct + 3 * h + 3 + 6)
                    fs.step(dve.tensor_tensor(dst, m_gate[:, h, 0], m_gate[:, h, 1], ALU.add))
                    fs.wait()
                    dve.tensor_tensor(dst, dst, m_gate[:, h, 2], ALU.add).then_inc(mixed_ready, 1)
                fs.leave(KD, 2)
            with dve.Fori(0, NT) as t:
                dve.wait_ge(mixed_hi, t + 1)
                tokens = bass.ds(P * t, P)
                dve.tensor_tensor(x_lo[:, :, tokens], mixed[:, :, tokens], x_hi[:, :, tokens].bitcast(F32),
                                  ALU.subtract).then_inc(mixed_split, 1)

            def half_tile(t, h):
                return resid[:, bass.ds(t, 1), h * HALF:(h + 1) * HALF].rearrange("p o n -> p (o n)")

            def residual(t, s, h):
                dve.wait_ge(f_prod, t + 1 + NT * h)
                dve.scalar_tensor_tensor(half_tile(t, h), half_tile(t, h), ALPHA, f_gate[:, s], ALU.mult,
                                         ALU.add).then_inc(f_used, 1)

            dve.sem_inc(f_used, 2)
            dve.wait_ge(x_loaded[0], 16)
            with dve.Fori(0, NT // 2) as i:
                for s in range(2):
                    residual(2 * i + s, s, 0)
            dve.wait_ge(x_loaded[1], 16)
            for t in range(NT):
                dve.wait_ge(f_used, NT + 2)
                residual(t, t % 2, 1)
                dve.wait_ge(out_done, t + 1)
                bank = (acc if t < 4 else aux)[:, t % 4]
                dve.tensor_tensor(half_tile(t, 0), half_tile(t, 0), bank, ALU.add).then_inc(out_taken, 1)
            dve.wait_ge(f_used, 2 * NT + 2)
            dve.wait_ge(out_taken, NT)
            dve.wait_ge(ln_loaded, 16)
            for t in range(NT):
                s = t % 2
                dve.wait_ge(out_done, NT + t + 1)
                bank = (acc if t < 4 else aux)[:, t % 4]
                dve.tensor_tensor(half_tile(t, 1), half_tile(t, 1), bank, ALU.add).then_inc(out_taken, 1)
                fs.step(dve.bn_stats(ln_stats[:, s, 0:2].rearrange("p e c -> p (e c)"), half_tile(t, 0)))
                dve.wait_ge(out_taken, NT + t + 1)
                fs.step(dve.bn_stats(ln_stats[:, s, 2:4].rearrange("p e c -> p (e c)"), half_tile(t, 1)))
                fs.wait()
                fs.step(dve.tensor_reduce(ln_sum[:, s:s + 1], ln_stats[:, s, :, 1], AX_X, ALU.add))
                fs.wait()
                fs.step(dve.tensor_scalar(ln_sum[:, s:s + 1], ln_sum[:, s:s + 1], 0.25, None, ALU.mult))
                fs.wait()
                fs.step(dve.tensor_scalar(ln_dev[:, s], ln_stats[:, s, :, 1], ln_sum[:, s:s + 1], None, ALU.subtract))
                fs.wait()
                fs.step(dve.scalar_tensor_tensor(ln_dev[:, s], ln_dev[:, s], D / 4, ln_dev[:, s], ALU.mult, ALU.mult))
                fs.wait()
                fs.step(dve.tensor_tensor(ln_dev[:, s], ln_dev[:, s], ln_stats[:, s, :, 2], ALU.add))
                fs.wait()
                fs.step(dve.tensor_reduce(ln_var[:, s:s + 1], ln_dev[:, s], AX_X, ALU.add))
                fs.wait()
                dve.tensor_scalar(ln_var[:, s:s + 1], ln_var[:, s:s + 1], 1.0 / D, 1e-5, ALU.mult, ALU.add).then_inc(ln_var_ready, 1)
                dve.wait_ge(ln_std_ready, t + 1)
                fs.step(dve.reciprocal(ln_rstd[:, s:s + 1], ln_std[:, s:s + 1]))
                fs.wait()
                tile = resid[:, t]
                fs.step(dve.tensor_scalar(tile, tile, ln_sum[:, s:s + 1], ln_rstd[:, s:s + 1], ALU.subtract, ALU.mult))
                fs.wait()
                dve.tensor_tensor(tile, tile, ln_gb[:, 0], ALU.mult).then_inc(ln_scaled, 1)


def nsa_tables():
    q, k = np.arange(P)[:, None], np.arange(P)[None, :]
    later = np.where(k > q, NEG, 0)
    causal_wide = np.concatenate([np.zeros((P, S - P)), later], 1)
    win_mask = np.concatenate([np.where(k > q, 0, NEG), np.zeros((P, P)), later], 1)
    t = np.arange(S).reshape(NT, P).T[:, :, None]
    c = np.arange(NC)[None, None, :]
    cmp_mask = np.where((c * CMP_STRIDE + CMP_LEN - 1 <= t) & (c < NC - 1), 0, NEG)
    j, cur = np.arange(S // DH)[None, None, :], t // DH
    forced, valid = (j == 0) | (j == cur) | (j == cur - 1), j <= cur
    i = np.arange(16)
    tables = {
        "causal_wide": causal_wide, "win_mask": win_mask, "cmp_mask": cmp_mask,
        "row_valid": (np.arange(P) >= CMP_LEN - 1)[:, None],
        "rank_keep": valid & ~forced, "rank_add": np.where(valid, np.where(forced, -NEG, 0), NEG),
        "earlier": np.broadcast_to(i[None, :] < i[:, None], (P, 16, 16)),
    }
    return {n: a.astype(np.float32) for n, a in tables.items()}


def gdn_tables():
    k, i = np.arange(P)[:, None], np.arange(P)[None, :]
    masks = [(k // (1 << l) == i // (1 << l) - 1) & (k // (2 << l) == i // (2 << l)) for l in range(LEVELS)]
    return {
        "tri": np.stack([k <= i, k > i, k == k + 0 * i], 1).astype(np.float32),
        "level_masks": np.stack(masks, 1).astype(np.float32),
    }


def log_decay(h):
    return np.log1p(-np.exp2(np.float32(-5.0 - h)), dtype=np.float32)


def chunk_decay(h):
    return float(np.exp(np.float32(P) * log_decay(h)))


def ret_tables():
    pos = np.arange(P, dtype=np.float32)
    lg = np.array([log_decay(h) for h in range(HEADS)], np.float32)
    scale = np.float32(P ** -0.5)
    diff = pos[None, :] - pos[:, None]
    decay = np.where(diff[:, None] >= 0, np.exp(np.maximum(diff, 0)[:, None] * lg[None, :, None]), 0) * scale
    inv = np.float32(10000.0) ** (-np.arange(0, P, 2, dtype=np.float32) / np.float32(P))
    ang = np.arange(S, dtype=np.float32)[:, None] * inv[None, :]
    cs = np.stack([np.cos(ang), np.sin(ang)], 1).reshape(NT, P, 2, P // 2).transpose(1, 0, 2, 3)
    return {
        "cos_sin": cs.astype(np.float32),
        "ret_decay": decay.astype(np.float32),
        "q_decay": np.broadcast_to(np.exp((pos + 1)[None, :] * lg[:, None]), (P, HEADS, P)).astype(np.float32),
        "k_decay": (np.exp((P - 1 - pos)[:, None] * lg[None, :]) * scale).astype(np.float32),
    }


def weight_units(w):
    n = w.shape[1] // UC
    return w.reshape(KD, P, n, UC).transpose(2, 1, 0, 3).reshape(n, P, UNIT)


def twice(a):
    return np.concatenate([a, a])


def weight_rows(w):
    return w.reshape(2, P, S).transpose(1, 0, 2).reshape(1, P, UNIT)


def layout(x, p, w_in, gdn_conv_w, w_ple, gdn_a_log, gdn_dt_bias, gdn_norm_w, w_ple_gate,
           nsa_pe_k, nsa_pe_v, nsa_cmp_w1k, nsa_cmp_w2k, nsa_cmp_w1v, nsa_cmp_w2v,
           w_branch_a, w_branch_b, w_branch_c, w_out, ln_g, ln_b):
    w = w_in[0]
    sizes = (512, 512, 512, 512, 1536, 4, 4, 512, 512, 128, 128, 128, 128, 128, 128, 24, 512, 3072)
    names = "rq rk rv rz gqkv gb ga gz nq nkc nvc nks nvs nkw nvw ng nz merge".split()
    ends = np.cumsum(sizes)
    col = {n: w[:, e - z:e] for n, e, z in zip(names, ends, sizes)}
    halves = np.arange(W4).reshape(HEADS, P // 2, 2).transpose(0, 2, 1).reshape(-1)
    pairs = np.arange(W4).reshape(2, 4, 64).transpose(1, 0, 2).reshape(-1)
    small = np.zeros((D, UC), w.dtype)
    small[:, 0:4], small[:, 4:8], small[:, 8:32] = col["gb"], col["ga"], col["ng"]
    units = [
        col["rq"][:, halves], col["rk"][:, halves], col["rv"],
        col["nvs"], col["nvw"], small,
        col["nq"][:, pairs], col["nkc"], col["nvc"], col["nks"], col["nkw"],
        col["rz"], col["gz"], col["nz"][:, pairs],
        col["gqkv"], col["merge"], w_ple_gate[0],
        w_out[0],
    ]
    weights = weight_units(np.concatenate(units, axis=1))
    w_branch = np.concatenate([w_branch_a[0], w_branch_b[0], w_branch_c[0][pairs]])
    first = np.concatenate([weight_rows(p[0, 0].T), weight_rows(w_ple[0]), weight_units(x[0].T)])
    return {
        "first": first, "weights": weights,
        "w_branch": w_branch.reshape(KB, P, KD, P).transpose(2, 1, 0, 3).reshape(KD, P, UNIT_BR),
        "x_tok": x[0].reshape(NT, P, D).transpose(1, 0, 2),
        "ln_gb": np.broadcast_to(np.stack([ln_g[0], ln_b[0]]), (P, 2, D)),
        "conv_w": gdn_conv_w[0].reshape(CONV_K, 12, P).transpose(2, 1, 0),
        "ident": np.eye(P, dtype=np.float32),
        **ret_tables(), **gdn_tables(), **nsa_tables(),
        "w1": twice(np.stack([w[0].reshape(CMP_LEN, DH, P).transpose(1, 0, 2) for w in (nsa_cmp_w1k, nsa_cmp_w1v)], 1)),
        "w2": np.stack([nsa_cmp_w2k[0], nsa_cmp_w2v[0]], 1),
        "pe_t": twice(np.stack([nsa_pe_k[0].T, nsa_pe_v[0].T], 1)),
        "dt_bias": np.broadcast_to(gdn_dt_bias, (P, HEADS)), "a_log": np.broadcast_to(gdn_a_log, (P, HEADS)),
        "norm_w": gdn_norm_w.reshape(P, 1),
    }


def kernel(**inputs):
    import concourse.bacc as bacc
    from concourse.bass_utils import run_bass_kernel_spmd

    nc = bacc.Bacc("TRN2", target_bir_lowering=False, num_devices=1)
    arrays = {n: np.ascontiguousarray(a) for n, a in layout(**{n: np.asarray(a) for n, a in inputs.items()}).items()}
    io = {n: nc.dram_tensor(n, a.shape, mybir.dt.from_np(a.dtype), kind="ExternalInput").ap() for n, a in arrays.items()}
    out = nc.dram_tensor("out", (1, S, D), F32, kind="ExternalOutput").ap()
    build(nc, io, out)
    r = run_bass_kernel_spmd(nc, [arrays], core_ids=[0])
    return r.results[0]["out"]
```

```python
from contextlib import ExitStack

import numpy as np
import concourse.bass as bass
from concourse import mybir

F32 = mybir.dt.float32
F32R = mybir.dt.float32r
ACT = mybir.ActivationFunctionType
ALU = mybir.AluOpType
AX_X = mybir.AxisListType.X

P = 128
S = 1024
D = 1024
NT = S // P
KD = D // P
HALF = 512
UC = 256
UNIT = KD * UC
HEADS = 4
W4 = HEADS * P
CONV_K = 4
LEVELS = 7
NSMALL = 32

N_FIRST = 6
U_RET = 0
U_VSW = 6
U_SMALL = 7
U_NSA = 8
U_Z = 12
U_GDN = 18
U_PLE0 = 24
U_MERGE = 26
U_MERGE_RET = 4
U_PLE = 38
U_BR = 40
U_OUT = 48
U_END = 52
KB = 3 * HEADS
UNIT_BR = KB * P
ALPHA = 2.0 ** 0.25


ATANH = tuple(range(19, 0, -2))

PREP_ABS, PREP_LOG, PREP_SS, PREP_DVE = 3, 28, 30, 37


NH = 8
DH = 64
NC = 64
CMP_LEN, CMP_STRIDE = 32, 16
N_SEL = 8
AHEAD = 3
STEPS = NT * NH
SCALE = DH ** -0.5
CMP_LOADS = 8
NEG = -1e30


def place(e):
    return e // NH, e % NH // 4, e % 4


def blocks(n):
    return n + 1, min(n + 1, 3)


def orders():
    s_at, s_cmp, at, cmp_at, uses, group = {e: e + 1 for e in range(AHEAD)}, {0: 0}, {}, {0: 0}, AHEAD + 1, 2
    for e in range(STEPS):
        at[e] = group
        group += -(-sum(blocks(e // NH)) // 4)
        if e + AHEAD < STEPS:
            s_at[e + AHEAD] = uses
            uses += 1
        if e % NH == 0 and e // NH < NT - 1:
            s_cmp[e // NH + 1] = uses
            uses += 1
        if e % NH == 5 and e // NH < NT - 1:
            cmp_at[e // NH + 1] = group
            group += 2
    return s_at, s_cmp, at, cmp_at, uses, group


S_AT, S_AT_CMP, GROUP_AT, GROUP_AT_CMP, S_END, GROUP_END = orders()


def by_dve(group):
    return group % 5 == 0


def dve_before(group):
    return -(-group // 5)


def act_before(group):
    return group - dve_before(group)


class Steps:

    def __init__(self, eng, sem):
        self.eng, self.sem, self.before, self.here = eng, sem, 0, 0

    def step(self, ins):
        ins.then_inc(self.sem, 1)
        self.here += 1

    def wait(self, back=0):
        self.eng.wait_ge(self.sem, self.before + (self.here - back))

    def value(self):
        return self.before + self.here

    def enter(self, i, per):
        assert not isinstance(self.before, tuple)
        self.start = self.before + self.here
        self.before, self.here = i * per + self.start, 0

    def leave(self, turns, per):
        assert self.here == per, (self.here, per)
        self.before, self.here = self.start + turns * per, 0


def build(nc, io, out):
    with ExitStack() as ctx:
        def sb(name, shape, dt=F32):
            return ctx.enter_context(nc.sbuf_tensor(name + "_sb", shape, dt))

        def sem(name):
            return ctx.enter_context(nc.semaphore(name))

        def scratch(name, shape):
            return nc.dram_tensor(name, shape, F32, kind="Internal").ap()

        ret_dram = scratch("ret_dram", (NT, P, 3 * W4))
        zt_dram = scratch("zt_dram", (12, P, S))
        nsa_dram = scratch("nsa_dram", (8, P, S))
        merge_dram = scratch("merge_dram", (24, P, S))
        oa_dram = scratch("oa_dram", (HEADS, P, S))
        ob_dram = scratch("ob_dram", (HEADS, P, P + S))
        oc_dram = scratch("oc_dram", (HEADS, P, S))
        pleg_dram = scratch("pleg_dram", (NT, P, D))
        ple_dram = scratch("ple_dram", (NT, P, D))
        gdn_dram = scratch("gdn_dram", (NT, P, 3 * W4))

        acc = ctx.enter_context(nc.psum_tensor("acc", [P, 4, HALF], F32))
        aux = ctx.enter_context(nc.psum_tensor("aux", [P, 4, HALF], F32))

        x_hi = sb("x_hi", [P, KD, S], F32R)
        x_lo = sb("x_lo", [P, KD, S], F32R)
        w_raw = sb("w_raw", [P, 2, UNIT])
        w_hi = sb("w_hi", [P, 2, UNIT], F32R)
        w_lo = sb("w_lo", [P, 2, UNIT], F32R)
        stage = sb("stage", [P, 4, HALF])
        vsw = sb("vsw", [P, NT, UC])
        small = sb("small", [P, NT, NSMALL])
        conv_w = sb("conv_w", [P, 12, CONV_K])
        ident = sb("ident", [P, P])
        ones = sb("ones", [P, 1])
        with ExitStack() as at_start:
            p_hi, p_lo, ple_hi, ple_lo = (at_start.enter_context(nc.sbuf_tensor(n, [P, 2, S], F32R))
                                          for n in ("p_hi", "p_lo", "ple_hi", "ple_lo"))
        gdn_ss = sb("gdn_ss", [P, NT, 12])
        beta = sb("beta", [P, NT, HEADS])
        gates = sb("gates", [P, NT, 3 * 8])
        with ExitStack() as in_conv:
            def sb_conv(name, shape):
                return in_conv.enter_context(nc.sbuf_tensor(name + "_sb", shape, F32))

            conv_in = sb_conv("conv_in", [P, 2, CONV_K - 1 + S])
            conv_y = sb_conv("conv_y", [P, 2, S])
            gdn_stage = sb_conv("gdn_stage", [P, NT, UC])
            gdn_sq = sb_conv("gdn_sq", [P, NT, UC])

        with ExitStack() as in_ret:
            def sb_ret(name, shape):
                return in_ret.enter_context(nc.sbuf_tensor(name + "_sb", shape, F32))

            ret_in = sb_ret("ret_in", [P, 2, 3, W4])
            ret_z = sb_ret("ret_z", [P, 2, HEADS, P])
            cos_sin = sb_ret("cos_sin", [P, NT, 2, P // 2])
            ret_decay = sb_ret("ret_decay", [P, HEADS, P])
            q_decay = sb_ret("q_decay", [P, HEADS, P])
            k_decay = sb_ret("k_decay", [P, HEADS])
            rot_tmp = sb_ret("rot_tmp", [P, 4, 2 * HEADS, P // 2])
            rot = sb_ret("rot", [P, 2, HEADS, 2, P // 2])
            k_end = sb_ret("k_end", [P, HEADS, P])
            q_t = sb_ret("q_t", [P, HEADS, P])
            k_t = sb_ret("k_t", [P, HEADS, P])
            q_start_t = sb_ret("q_start_t", [P, HEADS, P])
            ret_s = sb_ret("ret_s", [P, HEADS, P])
            ret_state = sb_ret("ret_state", [P, HEADS, P])
            ret_stats = sb_ret("ret_stats", [P, HEADS, 6])
            ret_mv = sb_ret("ret_mv", [P, HEADS, 2])
            ret_dm = sb_ret("ret_dm", [P, HEADS])
            ret_std = sb_ret("ret_std", [P, HEADS])
            ret_rstd = sb_ret("ret_rstd", [P, HEADS])
            ret_norm = sb_ret("ret_norm", [P, HEADS, P])
            ret_out = sb_ret("ret_out", [P, 2, HEADS, P])

        with ExitStack() as in_gdn:
            def sb_gdn(name, *shape):
                return in_gdn.enter_context(nc.sbuf_tensor(name + "_sb", [P, *shape], F32))

            g_in = sb_gdn("g_in", 3, HEADS, P)
            g_z = sb_gdn("g_z", HEADS, P)
            k_n, k_b, q_n, q_d, kb_dec, k_e, v_b = (sb_gdn(n, HEADS, P) for n in (
                "k_n k_b q_n q_d kb_dec k_e v_b".split()))
            k_nt = sb_gdn("k_nt", HEADS, P)
            kq_t = sb_gdn("kq_t", HEADS, 2, P)
            q_dt = sb_gdn("q_dt", HEADS, P)
            g_up = sb_gdn("g_up", HEADS, P)
            decay_t = sb_gdn("decay_t", HEADS, P)
            a_t = sb_gdn("a_t", HEADS, 2, P)
            b_t = sb_gdn("b_t", 2, HEADS, P)
            inv = sb_gdn("inv", HEADS, P)
            inv_t = sb_gdn("inv_t", HEADS, P)
            bi = sb_gdn("bi", HEADS, P)
            w_t = sb_gdn("w_t", HEADS, P)
            v_new = sb_gdn("v_new", HEADS, P)
            g_state = sb_gdn("g_state", HEADS, P)
            g_o = sb_gdn("g_o", HEADS, P)
            g_sq = sb_gdn("g_sq", HEADS, P)
            g_ss = sb_gdn("g_ss", HEADS)
            g_std = sb_gdn("g_std", HEADS)
            g_rstd = sb_gdn("g_rstd", HEADS)
            g_on = sb_gdn("g_on", HEADS, P)
            g_out = sb_gdn("g_out", 2, HEADS, P)
            tri = sb_gdn("tri", 3, P)
            level_masks = sb_gdn("level_masks", LEVELS, P)
            dt_bias = sb_gdn("dt_bias", HEADS)
            a_log = sb_gdn("a_log", HEADS)
            norm_w = sb_gdn("norm_w", 1)
            (ga, gy, gs, gs2, gpoly, g_log, rn_q, rn_k, s_q, s_q_dec, s_k_beta, s_k_beta_dec,
             s_k_end) = (sb_gdn(n, NT * HEADS) for n in (
                 "ga gy gs gs2 gpoly g_log rn_q rn_k s_q s_q_dec s_k_beta s_k_beta_dec s_k_end".split()))
            ea = sb_gdn("ea", HEADS)
            decays = sb_gdn("decays", 3, NT * HEADS)
            beta_flat = beta[:].rearrange("p t h -> p (t h)")

        with ExitStack() as in_nsa:
            def sb_nsa(name, *shape):
                return in_nsa.enter_context(nc.sbuf_tensor(name + "_sb", [P, *shape], F32))

            k_sw = sb_nsa("k_sw", 2, S)
            kc_t = sb_nsa("kc_t", NC)
            vc = sb_nsa("vc", 2 * DH)
            cmp_bias = sb_nsa("cmp_bias", 2)
            with ExitStack() as in_cmp:
                def sb_cmp(name, *shape):
                    return in_cmp.enter_context(nc.sbuf_tensor(name + "_sb", [P, *shape], F32))

                kv_c = sb_cmp("kv_c", 2, 2, S)
                w1 = sb_cmp("w1", 2, CMP_LEN // 2, P)
                w2 = sb_cmp("w2", 2, DH)
                pe_t = sb_cmp("pe_t", 2, CMP_LEN // 2)
                hidden = sb_cmp("hidden", 2, 2, NC)
            n_q = sb_nsa("n_q", 2, 4, P)
            n_z = sb_nsa("n_z", 2, 4, P)
            causal_wide = sb_nsa("causal_wide", S)
            win_mask = sb_nsa("win_mask", 3 * P)
            cmp_mask = sb_nsa("cmp_mask", NT, NC)
            row_valid = sb_nsa("row_valid", 1)
            rank_keep = sb_nsa("rank_keep", NT, 16)
            rank_add = sb_nsa("rank_add", NT, 16)
            earlier = sb_nsa("earlier", 16, 16)
            sel_mask = sb_nsa("sel_mask", 2, S)
            scores = sb_nsa("scores", AHEAD, S + 3 * P)
            n_max = sb_nsa("n_max", AHEAD, 2)
            n_nmax = sb_nsa("n_nmax", AHEAD, 2)
            n_sum = sb_nsa("n_sum", AHEAD, 2)
            n_coef = sb_nsa("n_coef", AHEAD, 2)
            p_t = sb_nsa("p_t", 2, 11, P)
            cmp_s = sb_nsa("cmp_s", NH, NC)
            cmp_pt = sb_nsa("cmp_pt", NH, P)
            cmp_rsum = sb_nsa("cmp_rsum", NH)
            cmp_coef = sb_nsa("cmp_coef", NH)
            cmp_max = cmp_coef
            cmp_pn = sb_nsa("cmp_pn", NH, NC)
            cmp_pg = sb_nsa("cmp_pg", 2, NC)
            imp = sb_nsa("imp", 2, 16)
            beats = cmp_pn[:].rearrange("p h (i j) -> p (h i j)", i=4).rearrange("p (g i j) -> p g i j", g=2, i=16)
            ties = sb_nsa("ties", 2, 16, 16)
            n_beat = sb_nsa("n_beat", 2, 16)
            sel_bias = sb_nsa("sel_bias", 2, 16)
            n_out = sb_nsa("n_out", 2, 4, P)

        with ExitStack() as in_br:
            def sb_br(name, shape, dt=F32):
                return in_br.enter_context(nc.sbuf_tensor(name + "_sb", shape, dt))

            mixed = sb_br("mixed", [P, KD, S])
            oc_hi = sb_br("oc_hi", [P, HEADS, S], F32R)
            oc_lo = sb_br("oc_lo", [P, HEADS, S], F32R)
            m_gate = sb_br("m_gate", [P, 2, 3, HALF])
        with ExitStack() as in_fin:
            def sb_fin(name, shape, dt=F32):
                return in_fin.enter_context(nc.sbuf_tensor(name + "_sb", shape, dt))

            resid = sb_fin("resid", [P, NT, D])
            wo_hi = sb_fin("wo_hi", [P, 2, UNIT], F32R)
            wo_lo = sb_fin("wo_lo", [P, 2, UNIT], F32R)
            f_gate = sb_fin("f_gate", [P, 4, HALF])
            f_ple = stage
            ln_stats = sb_fin("ln_stats", [P, NT, 2, 6])
            ln_mv = sb_fin("ln_mv", [P, 2, 2])
            ln_var = sb_fin("ln_var", [P, 2])
            ln_std = sb_fin("ln_std", [P, 2])
            ln_rstd = sb_fin("ln_rstd", [P, 2])
            ln_gb = vsw[:].rearrange("p t n -> p (t n)").rearrange("p (c n) -> p c n", c=2)

        raw_loaded = [sem("raw_loaded0"), sem("raw_loaded1")]
        first_hi = sem("first_hi")
        ple_ready = sem("ple_ready")
        ple_out = sem("ple_out")
        first_split = sem("first_split")
        ones_ready = sem("ones_ready")
        pool_hi = sem("pool_hi")
        w_split = sem("w_split")
        acc_ready = sem("acc_ready")
        acc_freed = sem("acc_freed")
        stored = [sem(f"stored{i}") for i in range(4)]
        const_loaded = sem("const_loaded")
        zeroed = sem("zeroed")
        small_turned = sem("small_turned")
        small_ready = sem("small_ready")
        conv_done = sem("conv_done")
        silu_done = sem("silu_done")
        turned = sem("turned")
        turned_freed = sem("turned_freed")
        gdn_staged = sem("gdn_staged")
        gdn_stored = sem("gdn_stored")
        dve_steps = sem("dve_steps")
        ret_const = sem("ret_const")
        ret_loaded = [sem("ret_loaded0"), sem("ret_loaded1")]
        ret_z_loaded = [sem("ret_z_loaded0"), sem("ret_z_loaded1")]
        rot_parts = sem("rot_parts")
        rotated = sem("rotated")
        k_end_ready = sem("k_end_ready")
        qk_turned = sem("qk_turned")
        qk_t_ready = sem("qk_t_ready")
        q_start_ready = sem("q_start_ready")
        ret_s_done = sem("ret_s_done")
        ret_s_ready = sem("ret_s_ready")
        ret_kv_done = sem("ret_kv_done")
        ret_state_ready = sem("ret_state_ready")
        ret_o_done = sem("ret_o_done")
        ret_stats_done = sem("ret_stats_done")
        ret_std_ready = sem("ret_std_ready")
        ret_normed = sem("ret_normed")
        ret_o_turned = sem("ret_o_turned")
        ret_out_ready = sem("ret_out_ready")
        ret_stored = [sem("ret_stored0"), sem("ret_stored1")]
        g_const = sem("g_const")
        prep_act = sem("prep_act")
        prep_dve = sem("prep_dve")
        prep_pe = sem("prep_pe")
        g_zeroed = sem("g_zeroed")
        g_loaded = sem("g_loaded")
        g_z_loaded = sem("g_z_loaded")
        g_scaled = sem("g_scaled")
        g_scaled_pool = sem("g_scaled_pool")
        g_turned = sem("g_turned")
        g_t_act = sem("g_t_act")
        g_t_dve = sem("g_t_dve")
        g_decay_done = sem("g_decay_done")
        g_decay_exp = sem("g_decay_exp")
        g_decay_ready = sem("g_decay_ready")
        g_a_done = sem("g_a_done")
        g_a_ready = sem("g_a_ready")
        b_ready = sem("b_ready")
        b_used = sem("b_used")
        bi_ready = sem("bi_ready")
        u_done = sem("u_done")
        inv_steps = sem("inv_steps")
        w_done = sem("w_done")
        w_ready = sem("w_ready")
        v_done = sem("v_done")
        v_ready = sem("v_ready")
        g_o_done = sem("g_o_done")
        g_o_ready = sem("g_o_ready")
        g_s_done = sem("g_s_done")
        g_state_ready = sem("g_state_ready")
        g_ss_ready = sem("g_ss_ready")
        g_std_ready = sem("g_std_ready")
        g_normed = sem("g_normed")
        g_o_turned = sem("g_o_turned")
        g_out_ready = sem("g_out_ready")
        g_stored = [sem("g_stored0"), sem("g_stored1")]
        n_const = sem("n_const")
        cmp_loaded = sem("cmp_loaded")
        cmp_hidden_done = sem("cmp_hidden_done")
        cmp_bias_ready = sem("cmp_bias_ready")
        cmp_hidden_ready = sem("cmp_hidden_ready")
        cmp_kv_done = sem("cmp_kv_done")
        cmp_kv_ready = sem("cmp_kv_ready")
        n_q_loaded = [sem("n_q_loaded0"), sem("n_q_loaded1")]
        n_z_loaded = [sem("n_z_loaded0"), sem("n_z_loaded1")]
        s_done = sem("s_done")
        s_taken = sem("s_taken")
        max_ready = sem("max_ready")
        exp_done = sem("exp_done")
        pt_turned = sem("pt_turned")
        pt_taken_dve = sem("pt_taken_dve")
        pt_taken_act = sem("pt_taken_act")
        scaled = sem("scaled")
        cmp_scaled = sem("cmp_scaled")
        o_done = sem("o_done")
        o_taken = sem("o_taken")
        cmp_shifted = sem("cmp_shifted")
        cmp_exp_done = sem("cmp_exp_done")
        sel_ready = sem("sel_ready")
        mask_ready = sem("mask_ready")
        n_stored = [sem("n_stored0"), sem("n_stored1")]
        nsa_steps = sem("nsa_steps")
        o_loaded = [sem(f"o_loaded{c}") for c in range(3)]
        o_hi = sem("o_hi")
        o_split = sem("o_split")
        gate_loaded = [sem("gate_loaded0"), sem("gate_loaded1")]
        gate_ready = sem("gate_ready")
        br_done = sem("br_done")
        br_taken = sem("br_taken")
        mixed_ready = sem("mixed_ready")
        mixed_hi = sem("mixed_hi")
        mixed_split = sem("mixed_split")
        wo_part = sem("wo_part")
        wo_split = sem("wo_split")
        ln_loaded = sem("ln_loaded")
        x_loaded = [sem("x_loaded0"), sem("x_loaded1")]
        f_loaded = [sem(f"f_loaded{i}") for i in range(4)]
        f_sigmoid = sem("f_sigmoid")
        f_prod = sem("f_prod")
        f_used = sem("f_used")
        out_done = sem("out_done")
        out_taken = sem("out_taken")
        ln_var_ready = sem("ln_var_ready")
        ln_std_ready = sem("ln_std_ready")
        ln_done = sem("ln_done")
        out_stored = sem("out_stored")
        fin_steps = sem("fin_steps")

        block = ctx.enter_context(nc.Block())

        def first_parts(p_part, ple_part, x_part):
            return [p_part[:], ple_part[:]] + [x_part[:, :, q * UC:(q + 1) * UC] for q in range(4)]

        def mixer_part(j, in_x, in_oc):
            return in_oc[:, j] if j < HEADS else in_x[:, (HEADS if j < 2 * HEADS else 0) + j % HEADS]

        def one(ap):
            return ap.rearrange("o p n -> (o p) n")

        @block.sync
        def _(sp):
            def load(n, src):
                sp.dma_start(w_raw[:, n % 2], src).then_inc(raw_loaded[n % 2], 16)

            def store_ple(g):
                for b in range(4):
                    sp.wait_ge(ple_out, 4 * g + b + 1)
                    sp.dma_start(ple_dram[2 * g + b // 2, :, (b % 2) * HALF:(b % 2 + 1) * HALF],
                                 stage[:, b]).then_inc(stored[b], 16)

            load(0, io["first"][0])
            load(1, io["first"][1])
            sp.dma_start(conv_w[:], io["conv_w"]).then_inc(const_loaded, 16)
            sp.dma_start(ident[:], io["ident"]).then_inc(const_loaded, 16)
            for n in range(2, N_FIRST + 2):
                sp.wait_ge(first_split, n - 1)
                load(n, io["first"][n] if n < N_FIRST else io["weights"][n - N_FIRST])
                if n >= 4:
                    store_ple(n - 4)
            def load_weights(u, slot, n_split):
                sp.wait_ge(w_split, n_split)
                sp.dma_start(w_raw[:, slot], one(io["weights"][bass.ds(u, 1)])).then_inc(raw_loaded[slot], 16)

            def load_branch(ct, slot, n_split):
                sp.wait_ge(w_split, n_split)
                sp.dma_start(w_raw[:, slot, 0:UNIT_BR], one(io["w_branch"][bass.ds(ct, 1)])).then_inc(raw_loaded[slot], 16)

            def load_out(n):
                sp.wait_ge(w_split, U_OUT + n - 1)
                sp.dma_start(w_raw[:, n % 2], io["weights"][U_BR + n]).then_inc(raw_loaded[n % 2], 16)

            with sp.Fori(0, (U_MERGE - 2) // 2) as i:
                for s in range(2):
                    load_weights(2 * i + 2 + s, s, 2 * i + 1 + s)
            for s in range(2):
                load_weights(U_MERGE + s, s, U_MERGE - 1 + s)

            for n, c in enumerate((cos_sin, ret_decay, q_decay, k_decay)):
                if n == 0:
                    sp.wait_ge(gdn_stored, 16 * 7)
                sp.dma_start(c[:], io[("cos_sin", "ret_decay", "q_decay", "k_decay")[n]]).then_inc(ret_const, 16)
            for dst, name in ((dt_bias, "dt_bias"), (a_log, "a_log"), (tri, "tri"), (level_masks, "level_masks"),
                              (norm_w, "norm_w")):
                sp.dma_start(dst[:], io[name]).then_inc(g_const, 16)
            with sp.Fori(0, NT // 4) as i:
                for q in range(4):
                    s = q % 2
                    t = 4 * i + q
                    sp.wait_ge(ret_o_done, t + 1)
                    sp.dma_start(ret_in[:, s].rearrange("p c n -> p (c n)"),
                                 one(ret_dram[bass.ds(t, 1)])).then_inc(ret_loaded[s], 16)
                    sp.wait_ge(ret_out_ready, t + 1)
                    sp.dma_start(ret_z[:, s], zt_dram[0:HEADS, :, bass.ds(P * t, P)].rearrange("h p n -> p h n")
                                 ).then_inc(ret_z_loaded[s], 16)
                    if s == 1:
                        load_weights(2 * i + U_MERGE + 2 + q // 2, q // 2, 2 * i + U_MERGE + 1 + q // 2)
            for q in range(2):
                sp.wait_ge(ret_stored[q], 16 * 5)
            with sp.Fori(0, NT // 2) as i:
                for s in range(2):
                    t = 2 * i + s
                    sp.wait_ge(g_scaled, 3 * t + 3)
                    sp.wait_ge(g_scaled_pool, 5 * t + 5)
                    sp.dma_start(g_in[:].rearrange("p c h n -> p (c h n)"), one(gdn_dram[bass.ds(t, 1)])).then_inc(g_loaded, 16)
                    sp.wait_ge(g_out_ready, t + 2)
                    sp.dma_start(g_z[:], zt_dram[HEADS:2 * HEADS, :, bass.ds(P * t, P)].rearrange("h p n -> p h n")
                                 ).then_inc(g_z_loaded, 16)
                    load_weights(t + U_MERGE + U_MERGE_RET + 2, s, t + U_MERGE + U_MERGE_RET + 1)

            for q in range(2):
                sp.wait_ge(g_stored[q], 16 * (6 - q))
            for g in range(2):
                for odd in range(2):
                    sp.dma_start(kv_c[64 * odd:64 * odd + 64, :, g, 0:S - odd],
                                 nsa_dram[4:6, 64 * g:64 * g + 64, odd:S].rearrange("c p n -> p c n")).then_inc(cmp_loaded, 16)
            for dst, src in ((w1[:], io["w1"]), (w2[:], io["w2"]),
                             (pe_t[:], io["pe_t"]), (k_sw[:], nsa_dram[6:8].rearrange("c p n -> p c n"))):
                sp.dma_start(dst, src).then_inc(cmp_loaded, 16)
            sp.wait_ge(cmp_kv_done, 1)
            for dst, name in ((causal_wide, "causal_wide"), (win_mask, "win_mask"), (cmp_mask, "cmp_mask"),
                              (row_valid, "row_valid"), (rank_keep, "rank_keep"), (rank_add, "rank_add"),
                              (earlier, "earlier")):
                sp.dma_start(dst[:], io[name]).then_inc(n_const, 16)
            for n in range(NT):
                if n >= 2:
                    sp.wait_ge(s_done, S_AT[NH * (n - 1) - 1] + 1)
                sp.dma_start(n_q[:, n % 2], nsa_dram[0:4, :, n * P:(n + 1) * P].rearrange("h p n -> p h n")).then_inc(
                    n_q_loaded[n % 2], 16)
                if n >= 2:
                    sp.wait_ge(o_taken, n - 1)
                sp.dma_start(n_z[:, n % 2], zt_dram[8:12, :, n * P:(n + 1) * P].rearrange("h p n -> p h n")).then_inc(
                    n_z_loaded[n % 2], 16)
                if n < 2:
                    load_branch(n, n, U_BR + n - 1)

            for q in range(2):
                sp.wait_ge(n_stored[q], 16 * 4)
            sp.dma_start(ln_gb, io["ln_gb"]).then_inc(ln_loaded, 16)
            for c, (src, at) in enumerate(((oc_dram, 0), (ob_dram[:, :, P:], HEADS), (oa_dram, 0))):
                if c == 2:
                    sp.wait_ge(o_split, HEADS)
                sp.dma_start(mixed[:, at:at + HEADS], src.rearrange("h p n -> p h n")).then_inc(o_loaded[c], 16)

            def load_gates(ct):
                for h in range(2):
                    sp.wait_ge(mixed_ready, 2 * ct + h + 1)
                    sp.dma_start(m_gate[:, h], merge_dram.rearrange("(b c) p n -> c p b n", b=3)[bass.ds(ct, 1), :, :, h * HALF:(h + 1) * HALF]
                                 .rearrange("o p b n -> (o p) b n")).then_inc(gate_loaded[h], 16)

            with sp.Fori(0, (KD - 2) // 2) as i:
                for s in range(2):
                    load_gates(2 * i + s)
                    load_branch(2 * i + s + 2, s, 2 * i + s + 1 + U_BR)
            for s in range(2):
                load_gates(KD - 2 + s)
                load_out(s)

            sp.wait_ge(mixed_split, NT)
            for h in range(2):
                load_out(2 + h)
                sp.dma_start(resid[:, :, h * HALF:(h + 1) * HALF], io["x_tok"][:, :, h * HALF:(h + 1) * HALF]).then_inc(
                    x_loaded[h], 16)

            for b in range(4):
                sp.wait_ge(stored[b], 16 * 36)

            def load_ple(t, s, h):
                sp.wait_ge(f_used, NT * h + t + 1)
                for dst, src in ((f_gate, pleg_dram), (f_ple, ple_dram)):
                    sp.dma_start(dst[:, s], one(src[bass.ds(t, 1), :, h * HALF:(h + 1) * HALF])).then_inc(f_loaded[s], 16)

            for h in range(2):
                with sp.Fori(0, NT // 4) as i:
                    for s in range(4):
                        load_ple(4 * i + s, s, h)
            with sp.Fori(0, NT) as t:
                sp.wait_ge(ln_done, t + 1)
                sp.dma_start(out[0, bass.ds(P * t, P), :], resid[:, bass.ds(t, 1), :].rearrange("p o n -> p (o n)")).then_inc(
                    out_stored, 16)

            sp.wait_ge(out_stored, 16 * NT)
            sp.wait_ge(ln_loaded, 16)
            for q in range(2):
                sp.wait_ge(raw_loaded[q], 16 * ((U_END + 6) // 2))

        @block.gpsimd
        def _(pool):
            def split(u, slot, size=UNIT):
                hi, lo = w_hi[:, slot, 0:size], w_lo[:, slot, 0:size]
                raw = w_raw[:, slot, 0:size]
                pool.tensor_tensor(hi, raw, ones[:].broadcast_to([P, size]), ALU.mult).then_inc(pool_hi, 1)
                pool.wait_ge(pool_hi, u + 1)
                pool.tensor_tensor(lo, raw, hi.bitcast(F32), ALU.subtract).then_inc(w_split, 1)

            pool.memset(ones[:], 1.0).then_inc(ones_ready, 1)
            pool.wait_ge(ones_ready, 1)
            for u in range(2):
                pool.wait_ge(raw_loaded[u], 16 * 4)
                split(u, u)

            def split_next(u, slot, used, loads):
                pool.wait_ge(acc_ready, used)
                pool.wait_ge(raw_loaded[slot], loads)
                split(u, slot)

            with pool.Fori(0, (U_MERGE - 2) // 2) as i:
                for s in range(2):
                    split_next(2 * i + 2 + s, s, 8 * i + 4 * (s + 1), 16 * i + 16 * 5)
            split_next(U_MERGE, 0, 4 * (U_MERGE - 1), 8 * (U_MERGE + 8))

            pool.wait_ge(ret_const, 16 * 4)
            with pool.Fori(0, NT // 4) as i:
                for q in range(4):
                    s = q % 2
                    t = 4 * i + q
                    halves = ret_in[:, s, 0:2].rearrange("p c (h e n) -> p (c h) e n", e=2, n=P // 2)
                    pool.wait_ge(ret_loaded[s], 32 * i + 16 * (q // 2 + 1))
                    pool.wait_ge(rotated, t + 1)
                    for n, (e, f) in enumerate(((0, 0), (1, 1), (0, 1), (1, 0))):
                        table = cos_sin[:, bass.ds(t, 1), f, :].broadcast_to([P, 2 * HEADS, P // 2])
                        pool.tensor_tensor(rot_tmp[:, n], halves[:, :, e], table, ALU.mult).then_inc(rot_parts, 1)
                    if s == 0:
                        split_next(2 * i + U_MERGE + 1 + q // 2, (1 + q // 2) % 2,
                                   8 * i + 4 * (U_MERGE + q // 2), 16 * i + 8 * (U_MERGE + 8) + 16 * (q // 2))
                    pool.wait_ge(rotated, t + 2)
                    pool.wait_ge(ret_kv_done, t + 1)
                    pool.tensor_tensor(k_end[:], rot[:, 1].rearrange("p h e n -> p h (e n)"),
                                       k_decay[:].rearrange("p (h o) -> p h o", o=1).broadcast_to([P, HEADS, P]),
                                       ALU.mult).then_inc(k_end_ready, 1)

            for q in range(2):
                pool.wait_ge(ret_stored[q], 16 * 5)
            pool.memset(g_o[:], 0.0).then_inc(g_zeroed, 1)
            pool.memset(g_z[:], 0.0).then_inc(g_zeroed, 1)
            pool.memset(g_state[:], 0.0).then_inc(g_state_ready, 1)
            pool.wait_ge(g_const, 16 * 5)
            pool.wait_ge(prep_dve, PREP_DVE)

            def by_head(scalars, t):
                return scalars[:, bass.ds(HEADS * t, HEADS)].rearrange("p (h o) -> p h o", o=1).broadcast_to([P, HEADS, P])

            def over_heads(table):
                return table.rearrange("p (o n) -> p o n", o=1).broadcast_to([P, HEADS, P])

            with pool.Fori(0, NT // 2) as i:
                for s in range(2):
                    t = 2 * i + s
                    pool.wait_ge(g_decay_done, t + 1)
                    pool.tensor_tensor(g_up[:], over_heads(tri[:, 0]), by_head(g_log, t), ALU.mult).then_inc(g_scaled_pool, 1)
                    pool.wait_ge(g_loaded, 16 * (t + 1))
                    pool.wait_ge(g_s_done, t + 1)
                    for dst, c, scalars in ((q_d, 0, s_q_dec), (kb_dec, 1, s_k_beta_dec), (v_b, 2, beta_flat),
                                            (k_e, 1, s_k_end)):
                        pool.tensor_tensor(dst[:], g_in[:, c], by_head(scalars, t), ALU.mult).then_inc(g_scaled_pool, 1)
                    pool.wait_ge(g_decay_exp, t + 1)
                    pool.tensor_tensor(decay_t[:], decay_t[:], over_heads(tri[:, 0]), ALU.mult).then_inc(g_decay_ready, 1)
                    pool.wait_ge(g_a_ready, t + 1)
                    for l in range(LEVELS):
                        if l > 0:
                            pool.wait_ge(b_used, 7 * t + l)
                        if l == 2:
                            pool.wait_ge(inv_steps, 13 * t + 2)
                        pool.tensor_tensor(b_t[:, (l + s) % 2], a_t[:, :, 0], over_heads(level_masks[:, l]),
                                           ALU.mult).then_inc(b_ready, 1)
                        if l == 2:
                            split_next(t + U_MERGE + U_MERGE_RET + 1, 1 - s, 4 * t + 4 * (U_MERGE + U_MERGE_RET),
                                       16 * i + 8 * (U_MERGE + U_MERGE_RET + 8) + 16 * s)

            split_next(U_PLE + 1, 1, 4 * U_PLE, 8 * (U_PLE + 8))
            pool.wait_ge(acc_ready, 4 * (U_PLE + 1))
            pool.wait_ge(raw_loaded[0], 8 * (U_BR + 8))
            split(U_BR, 0, UNIT_BR)
            pool.wait_ge(n_const, 16 * 7)
            for n in range(NT):
                if n >= 4:
                    for g in range(2):
                        pool.wait_ge(sel_ready, 2 * (n - 4) + g + 1)
                        pool.wait_ge(s_taken, S_AT[NH * (n - 1) + 4 * g + 3] + 1)
                        width = (n + 1) * P
                        pool.tensor_tensor(
                            sel_mask[:, g, 0:width].rearrange("p (b n) -> p b n", n=DH),
                            sel_bias[:, g, 0:2 * (n + 1)].rearrange("p (b o) -> p b o", o=1).broadcast_to([P, 2 * (n + 1), DH]),
                            causal_wide[:, S - width:S].rearrange("p (b n) -> p b n", n=DH),
                            ALU.add).then_inc(mask_ready, 1)

            pool.wait_ge(acc_ready, 4 * U_BR)
            pool.wait_ge(raw_loaded[1], 8 * (U_BR + 8))
            split(U_BR + 1, 1, UNIT_BR)
            with pool.Fori(0, (KD - 2) // 2) as i:
                for s in range(2):
                    pool.wait_ge(br_done, 12 * i + 6 * (s + 1))
                    pool.wait_ge(raw_loaded[s], 16 * i + 8 * (U_BR + 8) + 16)
                    split(2 * i + U_BR + 2 + s, s, UNIT_BR)
            for n in range(2):
                pool.wait_ge(br_done, 6 * (KD - 1 + n))
                pool.wait_ge(raw_loaded[n], 8 * (U_OUT + 8))
                split(U_OUT + n, n)
            for h in range(2):
                with pool.Fori(0, NT // 4) as i:
                    for s in range(4):
                        pool.wait_ge(f_sigmoid, 4 * i + s + 1 + NT * h)
                        pool.tensor_tensor(f_gate[:, s], f_gate[:, s], f_ple[:, s], ALU.mult).then_inc(f_prod, 1)

        @block.tensor
        def _(pe):
            mm = nc.tensor.matmul

            def parts(dst, left_hi, left_lo, right_hi, right_lo, first, last):
                mm(dst, left_hi, right_hi, start=first, stop=False, skip_group_check=True)
                mm(dst, left_hi, right_lo, start=False, stop=False, skip_group_check=True)
                return mm(dst, left_lo, right_hi, start=False, stop=last, skip_group_check=True)

            def unit_token_major(bank0, u, slot, cols=UC):
                hi = w_hi[:, slot].rearrange("p (k n) -> p k n", k=KD)
                lo = w_lo[:, slot].rearrange("p (k n) -> p k n", k=KD)
                pe.wait_ge(w_split, u + 1)
                for b in range(4):
                    pe.wait_ge(acc_freed, bank0 + b + 1)
                    for j in range(2):
                        t = 2 * b + j
                        for k in range(KD):
                            last = parts(acc[:, b, j * UC:j * UC + cols], x_hi[:, k, t * P:(t + 1) * P],
                                         x_lo[:, k, t * P:(t + 1) * P], hi[:, k, 0:cols], lo[:, k, 0:cols],
                                         k == 0, k == KD - 1)
                    last.then_inc(acc_ready, 1)

            def unit_channel_major(bank0, u, slot):
                hi = w_hi[:, slot].rearrange("p (k n) -> p k n", k=KD)
                lo = w_lo[:, slot].rearrange("p (k n) -> p k n", k=KD)
                pe.wait_ge(w_split, u + 1)
                for b in range(4):
                    c, h = b // 2, b % 2
                    pe.wait_ge(acc_freed, bank0 + b + 1)
                    for k in range(KD):
                        last = parts(acc[:, b], hi[:, k, c * P:(c + 1) * P], lo[:, k, c * P:(c + 1) * P],
                                     x_hi[:, k, h * HALF:(h + 1) * HALF], x_lo[:, k, h * HALF:(h + 1) * HALF],
                                     k == 0, k == KD - 1)
                    last.then_inc(acc_ready, 1)

            def units(unit, first, count):
                with pe.Fori(0, count // 2) as i:
                    for s in range(2):
                        unit(8 * i + 4 * (first + s), 2 * i + first + s, (first + s) % 2)

            def turn_unit(g):
                for c in range(2):
                    pe.wait_ge(silu_done, 2 * g + c + 1)
                    for h in range(2):
                        pe.wait_ge(turned_freed, 4 * g + 2 * c + h + 1)
                        for j in range(4):
                            t = 4 * h + j
                            last = nc.tensor.transpose(aux[:, 2 * c + h, j * P:(j + 1) * P],
                                                       conv_y[:, c, t * P:(t + 1) * P], ident[:])
                        last.then_inc(turned, 1)

            pe.wait_ge(first_split, 2)
            for n in range(16):
                t, h = n // 2, n % 2
                if n >= 4:
                    pe.wait_ge(ple_out, n - 3)
                for k in range(2):
                    last = parts(aux[:, n % 4], p_hi[:, k, t * P:(t + 1) * P], p_lo[:, k, t * P:(t + 1) * P],
                                 ple_hi[:, k, h * HALF:(h + 1) * HALF], ple_lo[:, k, h * HALF:(h + 1) * HALF],
                                 k == 0, k == 1)
                last.then_inc(ple_ready, 1)

            pe.wait_ge(first_split, N_FIRST)
            units(unit_token_major, U_RET, 6)
            unit_token_major(4 * U_VSW, U_VSW, U_VSW % 2)
            s = U_SMALL % 2
            pe.wait_ge(w_split, U_SMALL + 1)
            for b in range(4):
                pe.wait_ge(acc_freed, 4 * U_SMALL + b + 1)
                for k in range(KD):
                    cols = slice(k * UC, k * UC + NSMALL)
                    last = parts(acc[0:NSMALL, b, 0:UC], w_hi[:, s, cols], w_lo[:, s, cols],
                                 x_hi[:, k, b * UC:(b + 1) * UC], x_lo[:, k, b * UC:(b + 1) * UC], k == 0, k == KD - 1)
                last.then_inc(acc_ready, 1)
            pe.wait_ge(const_loaded, 32)
            pe.wait_ge(ple_out, 16)
            for t in range(NT):
                if t % 2 == 0:
                    pe.wait_ge(acc_freed, 4 * U_SMALL + 4 + t // 2 + 1)
                last = nc.tensor.transpose(aux[:, 0, t * NSMALL:(t + 1) * NSMALL],
                                           stage[0:NSMALL, t // 2, (t % 2) * P:(t % 2 + 1) * P], ident[0:NSMALL, 0:NSMALL])
            last.then_inc(small_turned, 1)
            units(unit_channel_major, U_NSA, 4)
            units(unit_channel_major, U_Z, 6)
            pe.wait_ge(const_loaded, 32)
            unit_channel_major(4 * U_GDN, U_GDN, U_GDN % 2)
            with pe.Fori(0, 2) as i:
                for s in range(2):
                    unit_channel_major(8 * i + 4 * (U_GDN + 1 + s), 2 * i + U_GDN + 1 + s, (U_GDN + 1 + s) % 2)
                    turn_unit(2 * i + s)
            unit_channel_major(4 * (U_GDN + 5), U_GDN + 5, (U_GDN + 5) % 2)
            for s in range(2):
                turn_unit(4 + s)
                unit_token_major(4 * (U_PLE0 + s), U_PLE0 + s, s)

            class Filler:

                def __init__(self, u, slot, bank0):
                    self.u, self.bank0, self.n = u, bank0, 0
                    self.hi = w_hi[:, slot].rearrange("p (k n) -> p k n", k=KD)
                    self.lo = w_lo[:, slot].rearrange("p (k n) -> p k n", k=KD)

                def fill(self, steps):
                    for _ in range(steps):
                        b, k = self.n // KD, self.n % KD
                        c, h = b // 2, b % 2
                        if self.n == 0:
                            pe.wait_ge(w_split, self.u + 1)
                        if k == 0:
                            pe.wait_ge(acc_freed, self.bank0 + b + 3)
                        last = parts(acc[:, b % 2], self.hi[:, k, c * P:(c + 1) * P], self.lo[:, k, c * P:(c + 1) * P],
                                     x_hi[:, k, h * HALF:(h + 1) * HALF], x_lo[:, k, h * HALF:(h + 1) * HALF],
                                     k == 0, k == KD - 1)
                        if k == KD - 1:
                            last.then_inc(acc_ready, 1)
                        self.n += 1

            def turn(dst, src, identity):
                for h in range(HEADS):
                    last = nc.tensor.transpose(dst[:, h * P:(h + 1) * P], src[:, h], identity)
                return last

            def ret_tile(t, s, fill):
                v = ret_in[:, s, 2].rearrange("p (h n) -> p h n", h=HEADS)
                pe.wait_ge(rotated, t + 2)
                pe.wait_ge(qk_t_ready, 2 * t + 2)
                for n in range(2):
                    turn(acc[:, 2 + n], rot[:, n].rearrange("p h e n -> p h (e n)"), ident[:]).then_inc(qk_turned, 1)
                fill(4)
                pe.wait_ge(qk_t_ready, 2 * t + 4)
                pe.wait_ge(ret_s_ready, t + 1)
                for h in range(HEADS):
                    last = mm(aux[:, 0, h * P:(h + 1) * P], k_t[:, h], q_t[:, h], start=True, stop=True)
                last.then_inc(ret_s_done, 1)
                pe.wait_ge(k_end_ready, t + 2)
                pe.wait_ge(ret_state_ready, t + 1)
                for h in range(HEADS):
                    last = mm(aux[:, 1, h * P:(h + 1) * P], k_end[:, h], v[:, h], start=True, stop=True)
                last.then_inc(ret_kv_done, 1)
                fill(4)
                pe.wait_ge(ret_s_ready, t + 2)
                pe.wait_ge(q_start_ready, t + 2)
                pe.wait_ge(ret_normed, t + 1)
                for h in range(HEADS):
                    mm(aux[:, 2, h * P:(h + 1) * P], ret_s[:, h], v[:, h], start=True, stop=False)
                    last = mm(aux[:, 2, h * P:(h + 1) * P], q_start_t[:, h], ret_state[:, h], start=False, stop=True)
                last.then_inc(ret_o_done, 1)
                fill(8)
                pe.wait_ge(ret_normed, t + 2)
                pe.wait_ge(ret_out_ready, t + 2)
                turn(aux[:, 3], ret_norm, ident[:]).then_inc(ret_o_turned, 1)

            pe.wait_ge(turned_freed, 4 * 6 + 4)
            pe.wait_ge(g_const, 16 * 5)
            pe.wait_ge(prep_dve, PREP_LOG)
            for n in range(3):
                last = mm(aux[:, 0, n * 32:(n + 1) * 32], tri[:, n], g_log[:], start=True, stop=True)
            last.then_inc(prep_pe, 1)

            pe.sem_inc(ret_o_done, 2)
            pe.sem_inc(ret_kv_done, 1)
            pe.sem_inc(qk_turned, 2)
            pe.sem_inc(ret_o_turned, 1)
            pe.wait_ge(acc_freed, 4 * U_MERGE + 4)
            pe.wait_ge(prep_act, 5)
            with pe.Fori(0, NT // 4) as i:
                for q in range(4):
                    if q % 2 == 0:
                        filler = Filler(2 * i + U_MERGE + q // 2, q // 2, 8 * i + 4 * (U_MERGE + q // 2))
                    ret_tile(4 * i + q, q % 2, filler.fill)

            def gdn_tile(t, s, fill):
                pe.wait_ge(g_scaled, 3 * t + 6)
                pe.wait_ge(g_scaled_pool, 5 * t + 7)
                pe.wait_ge(v_ready, t + 1)
                pe.wait_ge(g_state_ready, t + 1)
                pe.wait_ge(g_o_ready, t + 1)
                for bank, src in ((acc[:, 2], k_n), (acc[:, 3], k_b), (aux[:, 2], q_n), (aux[:, 3], q_d)):
                    turn(bank, src, ident[:]).then_inc(g_turned, 1)
                fill(1)
                pe.wait_ge(g_t_act, 2 * t + 1)
                mm(acc[:, 2], tri[:, 1], g_up[:].rearrange("p h n -> p (h n)"), start=True, stop=True).then_inc(
                    g_decay_done, 1)
                pe.wait_ge(g_t_dve, 2 * t + 2)
                for h in range(HEADS):
                    last = mm(aux[:, h // 2, (h % 2) * 2 * P:(h % 2 + 1) * 2 * P], k_nt[:, h],
                              kq_t[:, h].rearrange("p c n -> p (c n)"), start=True, stop=True)
                last.then_inc(g_a_done, 1)
                fill(3)
                for l in range(LEVELS):
                    part = b_t[:, (l + s) % 2]
                    pe.wait_ge(b_ready, 7 * t + l + 1)
                    if l == 0:
                        for h in range(HEADS):
                            last = mm(acc[:, 3, h * P:(h + 1) * P], part[:, h], ident[:], start=True, stop=True)
                        last.then_inc(b_used, 1)
                        fill(2)
                        continue
                    pe.wait_ge(inv_steps, 13 * t + 2 * l)
                    for h in range(HEADS):
                        last = mm(aux[:, 2, h * P:(h + 1) * P], part[:, h], inv[:, h], start=True, stop=True)
                    last.then_inc(b_used, 1)
                    fill(2)
                    pe.wait_ge(bi_ready, 6 * t + l)
                    if l < LEVELS - 1:
                        for h in range(HEADS):
                            last = mm(aux[:, 0, h * P:(h + 1) * P], inv_t[:, h], bi[:, h], start=True, stop=True)
                        last.then_inc(u_done, 1)
                    if l == 2:
                        pe.wait_ge(g_normed, t + 1)
                        pe.wait_ge(g_decay_exp, t + 1)
                        turn(acc[:, 2], g_on, ident[:]).then_inc(g_o_turned, 1)
                    for h in range(HEADS):
                        last = mm(aux[:, 1, h * P:(h + 1) * P], bi[:, h], inv_t[:, h], start=True, stop=True)
                    last.then_inc(u_done, 1)
                    fill(1)
                pe.wait_ge(inv_steps, 13 * t + 13)
                pe.wait_ge(g_out_ready, t + 2)
                for h in range(HEADS):
                    last = mm(acc[:, 2, h * P:(h + 1) * P], kb_dec[:, h], inv_t[:, h], start=True, stop=True)
                last.then_inc(w_done, 1)
                fill(2)
                pe.wait_ge(w_ready, t + 1)
                pe.wait_ge(g_state_ready, t + 1)
                for h in range(HEADS):
                    mm(acc[:, 3, h * P:(h + 1) * P], inv_t[:, h], v_b[:, h], start=True, stop=False)
                    last = mm(acc[:, 3, h * P:(h + 1) * P], w_t[:, h], g_state[:, h], start=False, stop=True)
                last.then_inc(v_done, 1)
                fill(2)
                pe.wait_ge(v_ready, t + 2)
                for h in range(HEADS):
                    mm(aux[:, 3, h * P:(h + 1) * P], q_dt[:, h], g_state[:, h], start=True, stop=False)
                    last = mm(aux[:, 3, h * P:(h + 1) * P], a_t[:, h, 1], v_new[:, h], start=False, stop=True)
                last.then_inc(g_o_done, 1)
                for h in range(HEADS):
                    last = mm(aux[:, 2, h * P:(h + 1) * P], k_e[:, h], v_new[:, h], start=True, stop=True)
                last.then_inc(g_s_done, 1)
                fill(4)

            pe.sem_inc(g_decay_done, 1)
            pe.sem_inc(g_turned, 4)
            pe.sem_inc(g_s_done, 1)
            pe.sem_inc(b_used, 1)
            with pe.Fori(0, NT // 2) as i:
                for s in range(2):
                    u = U_MERGE + U_MERGE_RET + s
                    gdn_tile(2 * i + s, s, Filler(2 * i + u, u % 2, 8 * i + 4 * u).fill)

            def ple_gate_unit(u):
                pe.wait_ge(w_split, u + 1)
                for b in range(4):
                    pe.wait_ge(acc_freed, 4 * u + b + 3)
                    for j, k in ((j, k) for j in range(2) for k in range(KD)):
                        t = 2 * b + j
                        hi = w_hi[:, u % 2, k * UC:(k + 1) * UC]
                        lo = w_lo[:, u % 2, k * UC:(k + 1) * UC]
                        last = parts(acc[:, b % 2, j * UC:(j + 1) * UC], x_hi[:, k, t * P:(t + 1) * P],
                                     x_lo[:, k, t * P:(t + 1) * P], hi, lo, k == 0, k == KD - 1)
                        if j == 1 and k == KD - 1:
                            last.then_inc(acc_ready, 1)

            pe.wait_ge(g_normed, NT + 1)
            turn(acc[:, 2], g_on, ident[:]).then_inc(g_o_turned, 1)
            ple_gate_unit(U_PLE)
            pe.wait_ge(cmp_loaded, 16 * CMP_LOADS)
            pe.wait_ge(g_out_ready, NT + 2)
            for c in range(2):
                for l in range(CMP_LEN // 2):
                    mm(aux[:, c, 0:2 * (NC - 1)], w1[:, c, l], kv_c[:, c, :, 2 * l:2 * l + CMP_STRIDE * (NC - 2) + 1:CMP_STRIDE],
                       start=(l == 0), stop=(l == CMP_LEN // 2 - 1))
                for l in range(CMP_LEN // 2):
                    last = mm(acc[:, 2 + c, 0:1], w1[:, c, l], pe_t[:, c, l:l + 1],
                              start=(l == 0), stop=(l == CMP_LEN // 2 - 1))
                last.then_inc(cmp_hidden_done, 1)
            pe.wait_ge(cmp_hidden_ready, 2)
            for g in range(2):
                mm(acc[64 * g:64 * g + 64, 2, 0:NC - 1], w2[:, 0], hidden[:, 0, g, 0:NC - 1], start=True, stop=True)
                last = mm(acc[0:NC - 1, 3, g * DH:(g + 1) * DH], hidden[:, 1, g, 0:NC - 1], w2[:, 1], start=True, stop=True)
            last.then_inc(cmp_kv_done, 1)

            pe.wait_ge(acc_freed, 4 * (U_PLE + 1) + 4)

            def taken(group):
                if by_dve(group):
                    pe.wait_ge(pt_taken_dve, dve_before(group) + 1)
                else:
                    pe.wait_ge(pt_taken_act, act_before(group) + 1)

            def bank_of(group):
                if group >= 4:
                    taken(group - 4)
                return acc[:, group % 4]

            def scores_cmp(n):
                pe.wait_ge(n_q_loaded[n % 2], 16 * (n // 2 + 1))
                pe.wait_ge(cmp_kv_ready, 1)
                if n > 0:
                    pe.wait_ge(s_taken, S_AT_CMP[n])
                for g in range(2):
                    rows = slice(64 * g, 64 * g + 64)
                    for h in range(4):
                        last = mm(aux[:, g, h * NC:(h + 1) * NC], n_q[rows, n % 2, h], kc_t[rows, :], start=True, stop=True)
                last.then_inc(s_done, 1)

            def scores_of(e):
                n, g, h = place(e)
                rows = slice(64 * g, 64 * g + 64)
                q = n_q[rows, n % 2, h]
                if h == 0:
                    pe.wait_ge(n_q_loaded[n % 2], 16 * (n // 2 + 1))
                pe.wait_ge(s_taken, S_AT[e])
                sel, win = blocks(n)
                for at in range(0, sel * P, HALF):
                    end = min(at + HALF, sel * P)
                    mm(aux[:, at // HALF, 0:end - at], q, k_sw[rows, 0, at:end], start=True, stop=True)
                mm(aux[:, 2, 0:win * P], q, k_sw[rows, 1, (n + 1 - win) * P:(n + 1) * P], start=True,
                   stop=True).then_inc(s_done, 1)

            def turn_cmp(n):
                pe.wait_ge(cmp_scaled, n + 1)
                for g in range(2):
                    bank = bank_of(GROUP_AT_CMP[n] + g)
                    for h in range(4):
                        last = nc.tensor.transpose(bank[0:NC, h * P:(h + 1) * P], cmp_s[:, 4 * g + h], ident[:])
                    last.then_inc(pt_turned, 1)

            def turn_of(e):
                sel, win = blocks(e // NH)
                total = sel + win
                pe.wait_ge(scaled, 2 * (e + 1))
                for at in range(0, total, 4):
                    bank = bank_of(GROUP_AT[e] + at // 4)
                    for j in range(at, min(at + 4, total)):
                        col = j * P if j < sel else S + (j - sel) * P
                        last = nc.tensor.transpose(bank[:, (j - at) * P:(j - at + 1) * P], scores[:, e % AHEAD, col:col + P], ident[:])
                    last.then_inc(pt_turned, 1)

            def outputs_of(e):
                n, g, h = place(e)
                rows = slice(64 * g, 64 * g + 64)
                if e % NH == 0:
                    if n > 0:
                        pe.wait_ge(o_taken, n)
                    for c in range(2):
                        taken(GROUP_AT_CMP[n] + c)
                        mm(aux[64 * c:64 * c + 64, 3], vc[0:NC, c * DH:(c + 1) * DH],
                           cmp_pt[0:NC, 4 * c:4 * c + 4].rearrange("p h n -> p (h n)"), start=True, stop=False,
                           skip_group_check=True)
                sel, win = blocks(n)
                for j in range(sel + win):
                    if j % 4 == 0:
                        taken(GROUP_AT[e] + j // 4)
                    b, k = (0, j) if j < sel else (1, n + 1 - win + j - sel)
                    last = mm(aux[rows, 3, h * P:(h + 1) * P], vsw[:, k, b * P + g * DH:b * P + (g + 1) * DH],
                              p_t[:, e % 2, j], start=False, stop=(j == sel + win - 1), skip_group_check=True)
                last.then_inc(o_done, 1)

            scores_cmp(0)
            for e in range(AHEAD):
                scores_of(e)
            turn_cmp(0)
            for e in range(STEPS):
                n, h = e // NH, e % NH
                turn_of(e)
                if e + AHEAD < STEPS:
                    scores_of(e + AHEAD)
                outputs_of(e)
                if n < NT - 1 and h == 0:
                    scores_cmp(n + 1)
                if n < NT - 1 and h == 5:
                    turn_cmp(n + 1)
            pe.wait_ge(pt_taken_dve, dve_before(GROUP_END))
            pe.wait_ge(pt_taken_act, act_before(GROUP_END))
            ple_gate_unit(U_PLE + 1)

            bank = [acc[:, b] for b in range(4)] + [aux[:, b] for b in range(4)]
            pe.wait_ge(acc_freed, 4 * U_BR + 4)
            pe.wait_ge(s_taken, S_END)
            with pe.Fori(0, KD // 2) as i:
                for s in range(2):
                    ct = 2 * i + s
                    hi = w_hi[:, s].rearrange("p (k n) -> p k n", n=P)
                    lo = w_lo[:, s].rearrange("p (k n) -> p k n", n=P)
                    pe.wait_ge(w_split, ct + U_BR + 1)
                    for h in range(2):
                        cols = slice(h * HALF, (h + 1) * HALF)
                        for b in range(3):
                            pe.wait_ge(br_taken, 6 * ct + 3 * h + b + 1)
                            for k in range(HEADS):
                                j = HEADS * b + k
                                o_h, o_l = mixer_part(j, x_hi, oc_hi), mixer_part(j, x_lo, oc_lo)
                                if s == 0 and h == 0:
                                    pe.wait_ge(o_split, j + 1)
                                last = parts(bank[3 * h + b], hi[:, j], lo[:, j], o_h[:, cols], o_l[:, cols],
                                             k == 0, k == HEADS - 1)
                            last.then_inc(br_done, 1)

            pe.wait_ge(br_taken, 6 * KD + 6)
            pe.wait_ge(o_taken, NT)

            def out_product(n, t):
                part_hi, part_lo = (w_hi, w_lo) if n < 2 else (wo_hi, wo_lo)
                for k in range(KD):
                    last = parts(bank[t][:, (n % 2) * UC:(n % 2 + 1) * UC], x_hi[:, k, t * P:(t + 1) * P],
                                 x_lo[:, k, t * P:(t + 1) * P], part_hi[:, n % 2, k * UC:(k + 1) * UC],
                                 part_lo[:, n % 2, k * UC:(k + 1) * UC], k == 0, k == KD - 1)
                return last

            for n in range(2):
                pe.wait_ge(w_split, U_OUT + n + 1)
                for t in range(NT):
                    pe.wait_ge(mixed_split, t + 1)
                    last = out_product(n, t)
                    if n == 1:
                        last.then_inc(out_done, 1)
            pe.wait_ge(wo_split, 2)
            for t in range(NT):
                pe.wait_ge(out_taken, t + 1)
                out_product(2, t)
                out_product(3, t).then_inc(out_done, 1)

        @block.scalar
        def _(act):
            act.sem_inc(acc_freed, 4)
            act.sem_inc(turned_freed, 4)

            for n, dst in enumerate(first_parts(p_hi, ple_hi, x_hi)):
                act.wait_ge(raw_loaded[n % 2], 16 * (n // 2 + 1))
                act.activation(dst, w_raw[:, n % 2].rearrange("p (k n) -> p k n", n=dst.shape[2]),
                               ACT.Copy).then_inc(first_hi, 1)

            def to_stage(bank0, b, func, stores, dst):
                act.wait_ge(acc_ready, bank0 + b + 1)
                act.wait_ge(stored[b], stores)
                act.activation(stage[:, b], acc[:, b], func).then_inc(acc_freed, 1)
                act.wait_ge(acc_freed, bank0 + b + 5)
                act.dma_start(dst, stage[:, b].rearrange("p (j n) -> p j n", j=2)).then_inc(stored[b], 16)

            with act.Fori(0, 3) as i:
                for s in range(2):
                    for b in range(4):
                        cols = ret_dram[2 * b:2 * b + 2, :, bass.ds(2 * UC * i + UC * s, UC)]
                        to_stage(8 * i + 4 * s, b, ACT.Copy, 32 * i + 16 * (s + 4), cols.rearrange("t p n -> p t n"))
            for b in range(4):
                act.wait_ge(acc_ready, 4 * U_VSW + b + 1)
                act.activation(vsw[:, 2 * b:2 * b + 2, :], acc[:, b].rearrange("p (j n) -> p j n", j=2),
                               ACT.Copy).then_inc(acc_freed, 1)
            for b in range(4):
                act.wait_ge(acc_ready, 4 * U_SMALL + b + 1)
                act.wait_ge(stored[b], 16 * 10)
                act.activation(stage[0:NSMALL, b, 0:UC], acc[0:NSMALL, b, 0:UC], ACT.Copy).then_inc(acc_freed, 1)
            act.wait_ge(small_turned, 1)
            act.activation(small[:].rearrange("p t n -> p (t n)"), aux[:, 0, 0:NT * NSMALL], ACT.Copy).then_inc(small_ready, 1)
            with act.Fori(0, 2) as i:
                for s in range(2):
                    for b in range(4):
                        half = nsa_dram[bass.ds(4 * i + 2 * s + b // 2, 1), :, (b % 2) * HALF:(b % 2 + 1) * HALF]
                        to_stage(8 * i + 4 * (U_NSA + s), b, ACT.Copy, 32 * i + 16 * (10 + s),
                                 half.rearrange("o p (j n) -> (o p) j n", j=2))
            with act.Fori(0, 3) as i:
                for s in range(2):
                    for b in range(4):
                        half = zt_dram[bass.ds(4 * i + 2 * s + b // 2, 1), :, (b % 2) * HALF:(b % 2 + 1) * HALF]
                        to_stage(8 * i + 4 * (U_Z + s), b, ACT.Silu, 32 * i + 16 * (14 + s),
                                 half.rearrange("o p (j n) -> (o p) j n", j=2))

            act.wait_ge(zeroed, 1)

            def conv_unit(g):
                for b in range(4):
                    c, h = b // 2, b % 2
                    act.wait_ge(acc_ready, 4 * g + 4 * U_GDN + b + 1)
                    act.wait_ge(conv_done, 2 * g + c + 1)
                    act.activation(conv_in[:, c, CONV_K - 1 + h * HALF:CONV_K - 1 + (h + 1) * HALF],
                                   acc[:, b], ACT.Copy).then_inc(acc_freed, 1)

            def silu_unit(g):
                for c in range(2):
                    act.wait_ge(conv_done, 2 * g + c + 3)
                    act.activation(conv_y[:, c], conv_y[:, c], ACT.Silu).then_inc(silu_done, 1)

            def store_unit(g):
                act.wait_ge(gdn_staged, g + 1)
                act.dma_start(gdn_dram[:, :, bass.ds(UC * g, UC)].rearrange("t p n -> p t n"),
                              gdn_stage[:]).then_inc(gdn_stored, 16)

            act.sem_inc(conv_done, 2)
            act.sem_inc(gdn_stored, 16)
            conv_unit(0)
            silu_unit(0)
            with act.Fori(0, 5) as g:
                conv_unit(g + 1)
                silu_unit(g + 1)
                store_unit(g)

            def ple_unit(s):
                for b in range(4):
                    cols = pleg_dram[2 * b:2 * b + 2, :, UC * s:UC * (s + 1)]
                    to_stage(4 * (U_PLE0 + s), b, ACT.Copy, 16 * (20 + s), cols.rearrange("t p n -> p t n"))

            ple_unit(0)
            store_unit(5)

            act.wait_ge(small_ready, 1)
            act.activation(beta[:], small[:, :, 0:4], ACT.Sigmoid).then_inc(prep_act, 1)
            act.activation(gates[:], small[:, :, 8:32], ACT.Sigmoid).then_inc(prep_act, 1)
            act.wait_ge(prep_dve, PREP_ABS)
            act.activation(gy[:], gy[:], ACT.Exp, scale=-1.0).then_inc(prep_act, 1)
            act.wait_ge(g_const, 16 * 5)
            act.activation(ea[:], a_log[:], ACT.Exp).then_inc(prep_act, 1)

            ple_unit(1)
            act.wait_ge(prep_pe, 1)
            act.activation(decays[:].rearrange("p c n -> p (c n)"), aux[:, 0, 0:96], ACT.Exp).then_inc(prep_act, 1)
            act.wait_ge(prep_dve, PREP_SS)
            act.activation(rn_q[:], rn_q[:], ACT.Sqrt).then_inc(prep_act, 1)
            act.activation(rn_k[:], rn_k[:], ACT.Sqrt).then_inc(prep_act, 1)

            def merge_bank(u, b, bank0, stores):
                act.wait_ge(acc_ready, bank0 + b + 1)
                act.wait_ge(stored[b], stores)
                act.activation(stage[:, b], acc[:, b % 2], ACT.Copy).then_inc(acc_freed, 1)
                act.wait_ge(acc_freed, bank0 + b + 5)
                act.dma_start(merge_dram[bass.ds(2 * u + b // 2, 1), :, (b % 2) * HALF:(b % 2 + 1) * HALF]
                              .rearrange("o p n -> (o p) n"), stage[:, b]).then_inc(stored[b], 16)

            act.sem_inc(qk_t_ready, 2)
            with act.Fori(0, NT // 4) as i:
                for q in range(4):
                    s = q % 2
                    t = 4 * i + q
                    for n, dst in enumerate((q_t, k_t)):
                        act.wait_ge(qk_turned, 2 * t + n + 3)
                        act.wait_ge(ret_s_done, t + 1)
                        act.wait_ge(q_start_ready, t + 1)
                        act.activation(dst[:].rearrange("p h n -> p (h n)"), acc[:, 2 + n],
                                       ACT.Copy).then_inc(qk_t_ready, 1)
                    merge_bank(2 * i + q // 2, 2 * s, 8 * i + 4 * (U_MERGE + q // 2), 32 * i + 16 * (22 + q // 2))
                    act.wait_ge(ret_stats_done, t + 1)
                    act.activation(ret_std[:], ret_mv[:, :, 1], ACT.Sqrt).then_inc(ret_std_ready, 1)
                    merge_bank(2 * i + q // 2, 2 * s + 1, 8 * i + 4 * (U_MERGE + q // 2), 32 * i + 16 * (22 + q // 2))
                    act.wait_ge(ret_out_ready, t + 3)
                    act.dma_start(oa_dram[:, :, bass.ds(P * t, P)].rearrange("h p n -> p h n"),
                                  ret_out[:, s]).then_inc(ret_stored[s], 16)
            for s in range(2):
                act.wait_ge(ret_stored[s], 16 * 5)

            act.sem_inc(v_ready, 1)
            act.sem_inc(g_o_ready, 1)
            with act.Fori(0, NT // 2) as i:
                for s in range(2):
                    t = 2 * i + s
                    u = U_MERGE_RET + s

                    def merge(b):
                        merge_bank(2 * i + u, b, 8 * i + 4 * (U_MERGE + u), 32 * i + 16 * (22 + u))

                    def flat(x):
                        return x.rearrange("p h n -> p (h n)")

                    act.wait_ge(g_turned, 4 * t + 5)
                    act.activation(flat(k_nt[:]), acc[:, 2], ACT.Copy).then_inc(g_t_act, 1)
                    act.wait_ge(g_turned, 4 * t + 8)
                    act.activation(flat(q_dt[:]), aux[:, 3], ACT.Copy).then_inc(g_t_act, 1)
                    act.wait_ge(g_decay_done, t + 2)
                    act.activation(flat(decay_t[:]), acc[:, 2], ACT.Exp).then_inc(g_decay_exp, 1)
                    act.wait_ge(g_ss_ready, t + 1)
                    act.activation(g_std[:], g_ss[:], ACT.Sqrt).then_inc(g_std_ready, 1)
                    for l in range(1, LEVELS):
                        act.wait_ge(b_used, 7 * t + l + 2)
                        if l > 1:
                            act.wait_ge(u_done, 11 * t + 2 * l - 2)
                        act.activation(flat(bi[:]), aux[:, 2], ACT.Copy).then_inc(bi_ready, 1)
                        if l in (1, 3, 6):
                            merge((1, 3, 6).index(l))
                    act.wait_ge(w_done, t + 1)
                    act.activation(flat(w_t[:]), acc[:, 2], ACT.Copy, scale=-1.0).then_inc(w_ready, 1)
                    act.wait_ge(v_done, t + 1)
                    act.activation(flat(v_new[:]), acc[:, 3], ACT.Copy).then_inc(v_ready, 1)
                    act.wait_ge(g_o_done, t + 1)
                    act.wait_ge(g_normed, t + 1)
                    act.activation(flat(g_o[:]), aux[:, 3], ACT.Copy).then_inc(g_o_ready, 1)
                    merge(3)
                    act.wait_ge(g_out_ready, t + 2)
                    act.dma_start(ob_dram[:, :, bass.ds(P * t, P)].rearrange("h p n -> p h n"),
                                  g_out[:, s]).then_inc(g_stored[s], 16)
            act.wait_ge(g_ss_ready, NT + 1)
            act.activation(g_std[:], g_ss[:], ACT.Sqrt).then_inc(g_std_ready, 1)
            act.wait_ge(g_out_ready, NT + 2)
            act.dma_start(ob_dram[:, :, S:].rearrange("h p n -> p h n"), g_out[:, 0]).then_inc(g_stored[0], 16)

            def ple_bank(u, b):
                act.wait_ge(acc_ready, 4 * u + b + 1)
                act.wait_ge(stored[b], 16 * (20 + u - U_PLE0))
                act.activation(stage[:, b], acc[:, b % 2], ACT.Copy).then_inc(acc_freed, 1)
                act.wait_ge(acc_freed, 4 * u + b + 5)
                cols = pleg_dram[2 * b:2 * b + 2, :, (u - U_PLE + 2) * UC:(u - U_PLE + 3) * UC]
                act.dma_start(cols.rearrange("t p n -> p t n"),
                              stage[:, b].rearrange("p (j n) -> p j n", j=2)).then_inc(stored[b], 16)

            for b in range(4):
                ple_bank(U_PLE, b)
            act.wait_ge(prep_act, 7)
            for c in range(2):
                act.wait_ge(cmp_hidden_done, c + 1)
                act.activation(cmp_bias[:, c:c + 1], acc[:, 2 + c, 0:1], ACT.Copy).then_inc(cmp_bias_ready, 1)
            act.wait_ge(cmp_bias_ready, 2)
            for c in range(2):
                act.activation(hidden[:, c, :, 0:NC - 1], aux[:, c, 0:2 * (NC - 1)].rearrange("p (g n) -> p g n", g=2),
                               ACT.Gelu_apprx_tanh, bias=cmp_bias[:, c:c + 1]).then_inc(cmp_hidden_ready, 1)

            def exp_of(e):
                act.wait_ge(max_ready, e + 1)
                for b, (at, width) in enumerate(zip((0, S), (w * P for w in blocks(e // NH)))):
                    part = scores[:, e % AHEAD, at:at + width]
                    act.activation(part, part, ACT.Exp, bias=n_nmax[:, e % AHEAD, b:b + 1], scale=SCALE,
                                   accum_out=n_sum[:, e % AHEAD, b:b + 1]).then_inc(exp_done, 1)

            def exp_cmp(n):
                act.wait_ge(cmp_shifted, n + 1)
                act.activation(cmp_s[:], cmp_s[:], ACT.Exp, scale=SCALE).then_inc(cmp_exp_done, 1)

            def take_groups_cmp(n):
                for g in range(2):
                    group = GROUP_AT_CMP[n] + g
                    if not by_dve(group):
                        act.wait_ge(pt_turned, group + 1)
                        if n > 0:
                            act.wait_ge(o_done, NH * (n - 1) + 1)
                        act.activation(cmp_pt[0:NC, 4 * g:4 * g + 4].rearrange("p h n -> p (h n)"),
                                       acc[0:NC, group % 4], ACT.Copy).then_inc(pt_taken_act, 1)

            def take_groups(e):
                total = sum(blocks(e // NH))
                for at in range(0, total, 4):
                    group = GROUP_AT[e] + at // 4
                    if not by_dve(group):
                        width = min(4, total - at) * P
                        act.wait_ge(pt_turned, group + 1)
                        if e >= 2:
                            act.wait_ge(o_done, e - 1)
                        act.activation(p_t[:, e % 2, at:at + width // P].rearrange("p j n -> p (j n)"),
                                       acc[:, group % 4, 0:width], ACT.Copy).then_inc(pt_taken_act, 1)

            def store_tile(n):
                act.wait_ge(o_taken, n + 1)
                act.dma_start(oc_dram[:, :, n * P:(n + 1) * P].rearrange("h p n -> p h n"),
                              n_out[:, n % 2]).then_inc(n_stored[n % 2], 16)

            exp_cmp(0)
            for e in range(AHEAD):
                exp_of(e)
            take_groups_cmp(0)
            for e in range(STEPS):
                n, h = e // NH, e % NH
                take_groups(e)
                if n < NT - 1 and h == 1:
                    exp_cmp(n + 1)
                if e + AHEAD < STEPS:
                    exp_of(e + AHEAD)
                if n < NT - 1 and h == 5:
                    take_groups_cmp(n + 1)
                if h == 0 and n > 0:
                    store_tile(n - 1)
            store_tile(NT - 1)

            for j in range(KB):
                if j % HEADS == 0:
                    act.wait_ge(o_loaded[j // HEADS], 16)
                if j == HEADS:
                    act.wait_ge(acc_ready, 4 * U_BR)
                act.activation(mixer_part(j, x_hi, oc_hi), mixed[:, j % (2 * HEADS)], ACT.Copy).then_inc(o_hi, 1)
                if j == 0 or j == HEADS - 1:
                    for b in range(2):
                        ple_bank(U_PLE + 1, 2 * (j > 0) + b)
            with act.Fori(0, KD) as ct:
                for h in range(2):
                    act.wait_ge(gate_loaded[h], 16 * (ct + 1))
                    act.activation(m_gate[:, h], m_gate[:, h], ACT.Sigmoid).then_inc(gate_ready, 1)
            act.wait_ge(br_done, 6 * KD)
            act.wait_ge(mixed_ready, 2 * KD + 2)
            with act.Fori(0, NT) as t:
                act.activation(x_hi[:, :, bass.ds(P * t, P)], mixed[:, :, bass.ds(P * t, P)], ACT.Copy).then_inc(mixed_hi, 1)
            for n in range(2):
                act.wait_ge(raw_loaded[n], 8 * (U_OUT + 2 + 8))
                act.activation(wo_hi[:, n], w_raw[:, n], ACT.Copy).then_inc(wo_part, 1)
            for h in range(2):
                with act.Fori(0, NT // 4) as i:
                    for s in range(4):
                        act.wait_ge(f_loaded[s], 32 * i + 32 * (h * NT // 4 + 1))
                        act.activation(f_gate[:, s], f_gate[:, s], ACT.Sigmoid).then_inc(f_sigmoid, 1)
            with act.Fori(0, NT // 2) as i:
                for s in range(2):
                    act.wait_ge(ln_var_ready, 2 * i + s + 1)
                    act.activation(ln_std[:, s:s + 1], ln_var[:, s:s + 1], ACT.Sqrt).then_inc(ln_std_ready, 1)

            for b in range(4):
                act.wait_ge(stored[b], 16 * 36)
            for s in range(2):
                act.wait_ge(n_stored[s], 16 * 4)

        @block.vector
        def _(dve):
            his = first_parts(p_hi, ple_hi, x_hi)
            for n, lo in enumerate(first_parts(p_lo, ple_lo, x_lo)):
                dve.wait_ge(first_hi, n + 1)
                dve.tensor_tensor(lo, w_raw[:, n % 2].rearrange("p (k n) -> p k n", n=lo.shape[2]),
                                  his[n].bitcast(F32), ALU.subtract).then_inc(first_split, 1)
                for m in range(4 * (n - 2), 4 * (n - 1)) if n >= 2 else ():
                    dve.wait_ge(ple_ready, m + 1)
                    if m >= 4:
                        dve.wait_ge(stored[m % 4], 16 * (m // 4))
                    dve.tensor_copy(stage[:, m % 4], aux[:, m % 4]).then_inc(ple_out, 1)
            dve.memset(conv_in[:, :, 0:CONV_K - 1], 0.0).then_inc(zeroed, 1)
            dve.wait_ge(zeroed, 1)
            dve.wait_ge(const_loaded, 32)
            st = Steps(dve, dve_steps)

            def conv(g, c):
                dve.wait_ge(acc_freed, 4 * g + 4 * U_GDN + 4 + 2 * (c + 1))
                dve.wait_ge(turned, 4 * g + 2 * (c + 1))
                w = conv_w[:, bass.ds(2 * g + c, 1), :]
                for k in range(CONV_K):
                    src, tap = conv_in[:, c, k:k + S], w[:, 0, k:k + 1]
                    if k == 0:
                        st.step(dve.tensor_scalar(conv_y[:, c], src, tap, None, ALU.mult))
                    else:
                        st.wait()
                        ins = dve.scalar_tensor_tensor(conv_y[:, c], src, tap, conv_y[:, c], ALU.mult, ALU.add)
                        if k < CONV_K - 1:
                            st.step(ins)
                        else:
                            ins.then_inc(conv_done, 1)

            def stage_unit(g):
                dve.wait_ge(gdn_stored, 16 * g + 16)
                for b in range(4):
                    c, h = b // 2, b % 2
                    dve.wait_ge(turned, 4 * g + b + 5)
                    dve.tensor_copy(gdn_stage[:, 4 * h:4 * h + 4, c * P:(c + 1) * P],
                                    aux[:, b].rearrange("p (j n) -> p j n", j=4)).then_inc(turned_freed, 1)
                dve.wait_ge(turned_freed, 4 * g + 8)
                dve.tensor_tensor(gdn_sq[:], gdn_stage[:], gdn_stage[:], ALU.mult).then_inc(gdn_staged, 1)
                dve.wait_ge(gdn_staged, g + 1)
                st.step(dve.tensor_reduce(gdn_ss[:, :, bass.ds(2 * g, 2)],
                                  gdn_sq[:].rearrange("p t (h n) -> p t h n", h=2), AX_X, ALU.add))
                st.wait()

            dve.sem_inc(turned, 4)
            for c in range(2):
                conv(0, c)
            with dve.Fori(0, 5) as g:
                st.enter(g, 7)
                for c in range(2):
                    conv(g + 1, c)
                stage_unit(g)
                st.leave(5, 7)
            stage_unit(5)

            st.wait()
            prep = Steps(dve, prep_dve)

            def small_step(ins):
                prep.step(ins)
                prep.wait()

            def tiles(x):
                return x.rearrange("p (t h) -> p t h", h=HEADS)

            def over_tiles(x):
                return x.rearrange("p (o h) -> p o h", o=1).broadcast_to([P, NT, HEADS])

            dve.wait_ge(g_const, 16 * 5)
            dve.wait_ge(small_ready, 1)
            small_step(dve.tensor_tensor(tiles(ga[:]), small[:, :, 4:8], over_tiles(dt_bias[:]), ALU.add))
            small_step(dve.tensor_scalar(gs[:], ga[:], -1.0, None, ALU.mult))
            small_step(dve.tensor_tensor(gy[:], ga[:], gs[:], ALU.max))
            assert prep.here == PREP_ABS
            dve.wait_ge(prep_act, 3)
            small_step(dve.tensor_scalar(gs[:], gy[:], 2.0, None, ALU.add))
            small_step(dve.reciprocal(gs[:], gs[:]))
            small_step(dve.tensor_tensor(gs[:], gs[:], gy[:], ALU.mult))
            small_step(dve.tensor_tensor(gs2[:], gs[:], gs[:], ALU.mult))
            small_step(dve.tensor_scalar(gpoly[:], gs2[:], 1.0 / ATANH[0], 1.0 / ATANH[1], ALU.mult, ALU.add))
            for n in ATANH[2:]:
                small_step(dve.tensor_tensor(gpoly[:], gpoly[:], gs2[:], ALU.mult))
                small_step(dve.tensor_scalar(gpoly[:], gpoly[:], 1.0 / n, None, ALU.add))
            small_step(dve.scalar_tensor_tensor(gpoly[:], gpoly[:], 2.0, gs[:], ALU.mult, ALU.mult))
            small_step(dve.scalar_tensor_tensor(gpoly[:], ga[:], 0.0, gpoly[:], ALU.max, ALU.add))
            dve.wait_ge(prep_act, 4)
            small_step(dve.tensor_scalar(ea[:], ea[:], -1.0, None, ALU.mult))
            small_step(dve.tensor_tensor(tiles(g_log[:]), tiles(gpoly[:]), over_tiles(ea[:]), ALU.mult))
            assert prep.here == PREP_LOG, prep.here
            small_step(dve.tensor_scalar(tiles(rn_q[:]), gdn_ss[:, :, 0:4], 1e-6, None, ALU.add))
            small_step(dve.tensor_scalar(tiles(rn_k[:]), gdn_ss[:, :, 4:8], 1e-6, None, ALU.add))
            assert prep.here == PREP_SS, prep.here
            dve.memset(ret_state[:], 0.0).then_inc(ret_state_ready, 1)
            dve.sem_inc(rotated, 1)
            dve.sem_inc(q_start_ready, 1)
            dve.sem_inc(k_end_ready, 1)
            dve.sem_inc(ret_s_ready, 1)
            dve.sem_inc(ret_normed, 1)
            dve.sem_inc(ret_out_ready, 2)
            dve.sem_inc(ret_s_done, 1)
            for q in ret_stored:
                dve.sem_inc(q, 16)
            dve.wait_ge(ret_const, 16 * 4)
            with dve.Fori(0, NT // 4) as i:
                st.enter(i, 4 * 12)
                for q in range(4):
                    s = q % 2
                    t = 4 * i + q
                    dve.wait_ge(rot_parts, 4 * t + 4)
                    dve.wait_ge(qk_turned, 2 * t + 2)
                    dve.wait_ge(k_end_ready, t + 1)
                    out_qk = rot[:].rearrange("p c h e n -> p (c h) e n")
                    st.step(dve.tensor_tensor(out_qk[:, :, 0], rot_tmp[:, 0], rot_tmp[:, 1], ALU.subtract))
                    st.wait()
                    dve.tensor_tensor(out_qk[:, :, 1], rot_tmp[:, 2], rot_tmp[:, 3], ALU.add).then_inc(rotated, 1)
                    dve.wait_ge(qk_t_ready, 2 * t + 3)
                    dve.wait_ge(ret_o_done, t + 2)
                    dve.tensor_tensor(q_start_t[:], q_t[:], q_decay[:], ALU.mult).then_inc(q_start_ready, 1)
                    dve.wait_ge(ret_s_done, t + 2)
                    dve.tensor_tensor(ret_s[:].rearrange("p h n -> p (h n)"), aux[:, 0],
                                      ret_decay[:].rearrange("p h n -> p (h n)"), ALU.mult).then_inc(ret_s_ready, 1)
                    dve.wait_ge(ret_o_done, t + 3)
                    for h in range(HEADS):
                        st.step(dve.bn_stats(ret_stats[:, h], aux[:, 2, h * P:(h + 1) * P]))
                    st.wait()
                    mean, var = ret_mv[:, :, 0], ret_mv[:, :, 1]
                    st.step(dve.tensor_tensor(mean, ret_stats[:, :, 1], ret_stats[:, :, 4], ALU.add))
                    st.step(dve.tensor_tensor(ret_dm[:], ret_stats[:, :, 1], ret_stats[:, :, 4], ALU.subtract))
                    st.step(dve.tensor_tensor(var, ret_stats[:, :, 2], ret_stats[:, :, 5], ALU.add))
                    st.wait()
                    st.step(dve.tensor_scalar(mean, mean, 0.5, None, ALU.mult))
                    st.step(dve.scalar_tensor_tensor(ret_dm[:], ret_dm[:], P / 4, ret_dm[:], ALU.mult, ALU.mult))
                    st.wait()
                    st.step(dve.tensor_tensor(var, var, ret_dm[:], ALU.add))
                    st.wait()
                    dve.tensor_scalar(var, var, 1.0 / P, 1e-5, ALU.mult, ALU.add).then_inc(ret_stats_done, 1)
                    dve.wait_ge(ret_kv_done, t + 2)
                    for h in range(HEADS):
                        ins = dve.scalar_tensor_tensor(ret_state[:, h], ret_state[:, h], chunk_decay(h),
                                                       aux[:, 1, h * P:(h + 1) * P], ALU.mult, ALU.add)
                    ins.then_inc(ret_state_ready, 1)
                    dve.wait_ge(ret_std_ready, t + 1)
                    st.step(dve.reciprocal(ret_rstd[:], ret_std[:]))
                    st.wait()
                    dve.wait_ge(ret_o_turned, t + 1)
                    for h in range(HEADS):
                        ins = dve.tensor_scalar(ret_norm[:, h], aux[:, 2, h * P:(h + 1) * P], ret_mv[:, h, 0:1],
                                                ret_rstd[:, h:h + 1], ALU.subtract, ALU.mult)
                    ins.then_inc(ret_normed, 1)
                    dve.wait_ge(ret_o_turned, t + 2)
                    dve.wait_ge(ret_z_loaded[s], 32 * i + 16 * (q // 2 + 1))
                    dve.wait_ge(ret_stored[s], 32 * i + 16 * (q // 2 + 1))
                    dve.tensor_tensor(ret_out[:, s].rearrange("p h n -> p (h n)"), aux[:, 3],
                                      ret_z[:, s].rearrange("p h n -> p (h n)"), ALU.mult).then_inc(ret_out_ready, 1)
                st.leave(NT // 4, 4 * 12)

            for q in range(2):
                dve.wait_ge(ret_stored[q], 16 * 5)
            dve.sem_inc(g_scaled, 3)
            dve.sem_inc(g_scaled_pool, 5)
            dve.wait_ge(prep_act, 7)
            small_step(dve.reciprocal(rn_q[:], rn_q[:]))
            small_step(dve.reciprocal(rn_k[:], rn_k[:]))
            small_step(dve.tensor_scalar(s_q[:], rn_q[:], float(P) ** -0.5, None, ALU.mult))
            small_step(dve.tensor_tensor(s_q_dec[:], s_q[:], decays[:, 0], ALU.mult))
            small_step(dve.tensor_tensor(s_k_beta[:], rn_k[:], beta_flat, ALU.mult))
            small_step(dve.tensor_tensor(s_k_beta_dec[:], s_k_beta[:], decays[:, 0], ALU.mult))
            small_step(dve.tensor_tensor(s_k_end[:], rn_k[:], decays[:, 1], ALU.mult))
            assert prep.here == PREP_DVE, prep.here

            dve.sem_inc(g_out_ready, 1)
            dve.sem_inc(g_z_loaded, 16)
            for q in g_stored:
                dve.sem_inc(q, 16)

            def by_head(scalars, t):
                return scalars[:, bass.ds(HEADS * t, HEADS)].rearrange("p (h o) -> p h o", o=1).broadcast_to([P, HEADS, P])

            def heads(bank):
                return bank.rearrange("p (h n) -> p h n", h=HEADS)

            def square(t):
                dve.wait_ge(g_o_ready, t + 1)
                st.step(dve.tensor_tensor(g_sq[:], g_o[:], g_o[:], ALU.mult))
                st.wait()
                st.step(dve.tensor_reduce(g_ss[:], g_sq[:], AX_X, ALU.add))
                st.wait()
                dve.tensor_scalar(g_ss[:], g_ss[:], 1.0 / P, 1e-6, ALU.mult, ALU.add).then_inc(g_ss_ready, 1)

            def normalize(t):
                dve.wait_ge(g_std_ready, t + 1)
                st.step(dve.reciprocal(g_rstd[:], g_std[:]))
                st.wait()
                dve.tensor_tensor(g_on[:], g_o[:], g_rstd[:].rearrange("p (h o) -> p h o", o=1).broadcast_to([P, HEADS, P]),
                                  ALU.mult).then_inc(g_normed, 1)

            def gate_deltanet(t, s, stores):
                dve.wait_ge(g_o_turned, t + 1)
                dve.wait_ge(g_z_loaded, 16 * (t + 1))
                dve.wait_ge(g_stored[s], stores)
                dve.scalar_tensor_tensor(g_out[:, s].rearrange("p h n -> p (h n)"), acc[:, 2], norm_w[:, 0:1],
                                         g_z[:].rearrange("p h n -> p (h n)"), ALU.mult, ALU.mult).then_inc(g_out_ready, 1)

            eye = ident[:].rearrange("p (o n) -> p o n", o=1).broadcast_to([P, HEADS, P])
            dve.wait_ge(prep_dve, PREP_DVE)
            dve.wait_ge(g_zeroed, 2)
            dve.wait_ge(g_state_ready, 1)
            with dve.Fori(0, NT // 2) as i:
                st.enter(i, 2 * 3)
                for s in range(2):
                    t = 2 * i + s
                    dve.wait_ge(g_loaded, 16 * (t + 1))
                    dve.wait_ge(g_turned, 4 * t + 4)
                    for dst, c, scalars in ((k_n, 1, rn_k), (k_b, 1, s_k_beta), (q_n, 0, s_q)):
                        dve.tensor_tensor(dst[:], g_in[:, c], by_head(scalars, t), ALU.mult).then_inc(g_scaled, 1)
                    square(t)
                    dve.wait_ge(g_turned, 4 * t + 7)
                    dve.tensor_copy(kq_t[:, :, 0], heads(acc[:, 3])).then_inc(g_t_dve, 1)
                    dve.tensor_copy(kq_t[:, :, 1], heads(aux[:, 2])).then_inc(g_t_dve, 1)
                    dve.wait_ge(g_a_done, t + 1)
                    dve.wait_ge(g_decay_ready, t + 1)
                    for h in range(HEADS):
                        ins = dve.tensor_tensor(
                            a_t[:, h], aux[:, h // 2, (h % 2) * 2 * P:(h % 2 + 1) * 2 * P].rearrange("p (c n) -> p c n", c=2),
                            decay_t[:, h:h + 1].broadcast_to([P, 2, P]), ALU.mult)
                    ins.then_inc(g_a_ready, 1)
                    normalize(t)
                    dve.wait_ge(b_used, 7 * t + 2)
                    dve.tensor_tensor(inv[:], eye, heads(acc[:, 3]), ALU.subtract).then_inc(inv_steps, 1)
                    dve.tensor_tensor(inv_t[:], eye, b_t[:, s], ALU.subtract).then_inc(inv_steps, 1)
                    for l in range(1, LEVELS):
                        if l == 3:
                            gate_deltanet(t, s, 16 * i + 16)
                        dve.wait_ge(inv_steps, 13 * t + 2 * l)
                        if l < LEVELS - 1:
                            dve.wait_ge(u_done, 11 * t + 2 * l - 1)
                            dve.tensor_tensor(inv[:], inv[:], heads(aux[:, 0]), ALU.subtract).then_inc(inv_steps, 1)
                            dve.wait_ge(u_done, 11 * t + 2 * l)
                            dve.tensor_tensor(inv_t[:], inv_t[:], heads(aux[:, 1]), ALU.subtract).then_inc(inv_steps, 1)
                        else:
                            dve.wait_ge(u_done, 11 * t + 11)
                            dve.tensor_tensor(inv_t[:], inv_t[:], heads(aux[:, 1]), ALU.subtract).then_inc(inv_steps, 1)
                    dve.wait_ge(g_s_done, t + 2)
                    for h in range(HEADS):
                        ins = dve.scalar_tensor_tensor(g_state[:, h], g_state[:, h], decays[:, 2, bass.ds(HEADS * t + h, 1)],
                                                       aux[:, 2, h * P:(h + 1) * P], ALU.mult, ALU.add)
                    ins.then_inc(g_state_ready, 1)
                st.leave(NT // 2, 2 * 3)
            square(NT)
            normalize(NT)
            gate_deltanet(NT, 0, 16 * 5)

            ns = Steps(dve, nsa_steps)

            def chained(ins):
                ns.step(ins)
                ns.wait()

            for q in range(2):
                dve.wait_ge(g_stored[q], 16 * (6 - q))
            ns.step(dve.memset(kc_t[:], 0.0))
            chained(dve.memset(vc[:], 0.0))
            dve.wait_ge(cmp_kv_done, 1)
            ns.step(dve.tensor_copy(kc_t[:, 0:NC - 1], acc[:, 2, 0:NC - 1]))
            chained(dve.tensor_copy(vc[0:NC - 1, :], acc[0:NC - 1, 3, 0:2 * DH]))
            dve.sem_inc(cmp_kv_ready, 1)
            dve.wait_ge(n_const, 16 * 7)

            def take_cmp(n):
                dve.wait_ge(s_done, S_AT_CMP[n] + 1)
                if n > 0:
                    dve.wait_ge(pt_turned, GROUP_AT_CMP[n - 1] + 2)
                mask = cmp_mask[:, n:n + 1, :].broadcast_to([P, 4, NC])
                for g in range(2):
                    ins = dve.tensor_tensor(cmp_s[:, 4 * g:4 * g + 4], aux[:, g, 0:4 * NC].rearrange("p (h c) -> p h c", h=4),
                                            mask, ALU.add)
                    ins.then_inc(s_taken, 1) if g else ns.step(ins)
                ns.wait()
                dve.wait_ge(s_taken, S_AT_CMP[n] + 1)
                chained(dve.tensor_reduce(cmp_max[:], cmp_s[:], AX_X, ALU.max))
                dve.tensor_tensor(cmp_s[:], cmp_s[:], cmp_max[:].rearrange("p (h o) -> p h o", o=1).broadcast_to([P, NH, NC]),
                                  ALU.subtract).then_inc(cmp_shifted, 1)

            def scale_cmp(n):
                dve.wait_ge(cmp_exp_done, n + 1)
                chained(dve.tensor_reduce(cmp_rsum[:], cmp_s[:], AX_X, ALU.add))
                chained(dve.reciprocal(cmp_rsum[:], cmp_rsum[:]))
                gate = gates[:, n].rearrange("p (h b) -> p h b", b=3)[:, :, 0]
                if n >= N_SEL * DH // P:
                    ns.step(dve.tensor_tensor(cmp_pn[:], cmp_s[:], cmp_rsum[:].rearrange("p (h o) -> p h o", o=1)
                                              .broadcast_to([P, NH, NC]), ALU.mult))
                chained(dve.tensor_tensor(cmp_coef[:], cmp_rsum[:], gate, ALU.mult))
                if n == 0:
                    chained(dve.tensor_scalar(cmp_coef[:], cmp_coef[:], row_valid[:, 0:1], None, ALU.mult))
                dve.tensor_tensor(cmp_s[:], cmp_s[:], cmp_coef[:].rearrange("p (h o) -> p h o", o=1).broadcast_to([P, NH, NC]),
                                  ALU.mult).then_inc(cmp_scaled, 1)

            def importance(n):
                chained(dve.tensor_reduce(cmp_pg[:], cmp_pn[:].rearrange("p (g h) c -> p g c h", g=2), AX_X, ALU.add))
                chained(dve.tensor_reduce(imp[:], cmp_pg[:].rearrange("p g (j c) -> p g j c", c=4), AX_X, ALU.add))
                chained(dve.tensor_tensor(imp[:, :, 1:16], imp[:, :, 1:16],
                                          cmp_pg[:].rearrange("p g (j c) -> p g j c", c=4)[:, :, 0:15, 3], ALU.add))
                chained(dve.tensor_tensor(imp[:], imp[:], rank_keep[:, n:n + 1, :].broadcast_to([P, 2, 16]), ALU.mult))
                chained(dve.tensor_tensor(imp[:], imp[:], rank_add[:, n:n + 1, :].broadcast_to([P, 2, 16]), ALU.add))

            def select(n, g):
                other = imp[:, g:g + 1, :].broadcast_to([P, 16, 16])
                own = imp[:, g].rearrange("p (j o) -> p j o", o=1).broadcast_to([P, 16, 16])
                ns.step(dve.tensor_tensor(beats[:, g], other, own, ALU.is_gt))
                chained(dve.tensor_tensor(ties[:, g], other, own, ALU.is_equal))
                chained(dve.tensor_tensor(ties[:, g], ties[:, g], earlier[:], ALU.mult))
                chained(dve.tensor_tensor(beats[:, g], beats[:, g], ties[:, g], ALU.add))
                chained(dve.tensor_reduce(n_beat[:, g], beats[:, g], AX_X, ALU.add))
                if n > N_SEL * DH // P:
                    dve.wait_ge(mask_ready, 2 * (n - N_SEL * DH // P) + g - 1)
                dve.tensor_scalar(sel_bias[:, g], n_beat[:, g], N_SEL - 0.5, NEG, ALU.is_ge, ALU.mult).then_inc(sel_ready, 1)

            def take(e):
                n, g, h = place(e)
                sel, win = blocks(n)
                dve.wait_ge(s_done, S_AT[e] + 1)
                if e >= AHEAD:
                    dve.wait_ge(pt_turned, GROUP_AT[e - AHEAD + 1])
                if n >= 4:
                    dve.wait_ge(mask_ready, 2 * (n - 4) + g + 1)
                    mask = sel_mask[:, g, 0:sel * P]
                else:
                    mask = causal_wide[:, S - sel * P:S]
                raw = aux[:, 0:2].rearrange("p b n -> p (b n)")[:, 0:sel * P]
                ns.step(dve.tensor_tensor_reduce(scores[:, e % AHEAD, 0:sel * P], raw, mask, 1.0, -3e38, ALU.add, ALU.max,
                                                 n_max[:, e % AHEAD, 0:1]))
                dve.tensor_tensor_reduce(scores[:, e % AHEAD, S:S + win * P], aux[:, 2, 0:win * P],
                                         win_mask[:, (3 - win) * P:3 * P], 1.0, -3e38, ALU.add, ALU.max,
                                         n_max[:, e % AHEAD, 1:2]).then_inc(s_taken, 1)
                ns.wait()
                dve.wait_ge(s_taken, S_AT[e] + 1)
                dve.tensor_scalar(n_nmax[:, e % AHEAD], n_max[:, e % AHEAD], -SCALE, None, ALU.mult).then_inc(max_ready, 1)

            def scale(e):
                n, g, h = place(e)
                head = 4 * g + h
                dve.wait_ge(exp_done, 2 * (e + 1))
                chained(dve.reciprocal(n_coef[:, e % AHEAD], n_sum[:, e % AHEAD]))
                chained(dve.tensor_tensor(n_coef[:, e % AHEAD], n_coef[:, e % AHEAD], gates[:, n, 3 * head + 1:3 * head + 3], ALU.mult))
                for b, (at, width) in enumerate(zip((0, S), (w * P for w in blocks(n)))):
                    part = scores[:, e % AHEAD, at:at + width]
                    dve.tensor_scalar(part, part, n_coef[:, e % AHEAD, b:b + 1], None, ALU.mult).then_inc(scaled, 1)

            def take_groups_cmp(n):
                for g in range(2):
                    group = GROUP_AT_CMP[n] + g
                    if by_dve(group):
                        dve.wait_ge(pt_turned, group + 1)
                        if n > 0:
                            dve.wait_ge(o_done, NH * (n - 1) + 1)
                        dve.tensor_copy(cmp_pt[0:NC, 4 * g:4 * g + 4].rearrange("p h n -> p (h n)"),
                                        acc[0:NC, group % 4]).then_inc(pt_taken_dve, 1)

            def take_groups(e):
                total = sum(blocks(e // NH))
                for at in range(0, total, 4):
                    group = GROUP_AT[e] + at // 4
                    if by_dve(group):
                        width = min(4, total - at) * P
                        dve.wait_ge(pt_turned, group + 1)
                        if e >= 2:
                            dve.wait_ge(o_done, e - 1)
                        dve.tensor_copy(p_t[:, e % 2, at:at + width // P].rearrange("p j n -> p (j n)"),
                                        acc[:, group % 4, 0:width]).then_inc(pt_taken_dve, 1)

            def gate_tile(n):
                dve.wait_ge(o_done, NH * (n + 1))
                dve.wait_ge(n_z_loaded[n % 2], 16 * (n // 2 + 1))
                if n >= 2:
                    dve.wait_ge(n_stored[n % 2], 16 * (n // 2))
                dve.tensor_tensor(n_out[:, n % 2].rearrange("p h n -> p (h n)"), aux[:, 3],
                                  n_z[:, n % 2].rearrange("p h n -> p (h n)"), ALU.mult).then_inc(o_taken, 1)

            take_cmp(0)
            for e in range(AHEAD):
                take(e)
            scale_cmp(0)
            take_groups_cmp(0)
            scale(0)
            for e in range(STEPS):
                n, h = e // NH, e % NH
                if e + 1 < STEPS:
                    scale(e + 1)
                take_groups(e)
                if h == 0 and n > 0:
                    gate_tile(n - 1)
                if e + AHEAD < STEPS:
                    take(e + AHEAD)
                if n < NT - 1 and h == 0:
                    take_cmp(n + 1)
                if n < NT - 1 and h == 1:
                    scale_cmp(n + 1)
                if N_SEL * DH // P <= n + 1 < NT and h == 2:
                    importance(n + 1)
                if N_SEL * DH // P <= n + 1 < NT and h in (3, 4):
                    select(n + 1, h - 3)
                if n < NT - 1 and h == 5:
                    take_groups_cmp(n + 1)
            gate_tile(NT - 1)

            dve.sem_inc(mixed_ready, 2)
            dve.sem_inc(br_taken, 6)
            for j in range(KB):
                dve.wait_ge(o_hi, j + 1)
                hi, lo = mixer_part(j, x_hi, oc_hi), mixer_part(j, x_lo, oc_lo)
                dve.tensor_tensor(lo, mixed[:, j % (2 * HEADS)], hi.bitcast(F32), ALU.subtract).then_inc(o_split, 1)
            dve.wait_ge(o_split, KB)
            fs = Steps(dve, fin_steps)
            with dve.Fori(0, KD) as ct:
                fs.enter(ct, 2)
                for h in range(2):
                    dve.wait_ge(gate_ready, 2 * ct + h + 1)
                    for b in range(3):
                        dve.wait_ge(br_done, 6 * ct + 3 * h + b + 1)
                        src = (acc if 3 * h + b < 4 else aux)[:, (3 * h + b) % 4]
                        dve.tensor_tensor(m_gate[:, h, 2 - b], m_gate[:, h, 2 - b], src, ALU.mult).then_inc(br_taken, 1)
                    dst = mixed[:, bass.ds(ct, 1), h * HALF:(h + 1) * HALF].rearrange("p o n -> p (o n)")
                    dve.wait_ge(br_taken, 6 * ct + 3 * h + 3 + 6)
                    fs.step(dve.tensor_tensor(dst, m_gate[:, h, 0], m_gate[:, h, 1], ALU.add))
                    fs.wait()
                    dve.tensor_tensor(dst, dst, m_gate[:, h, 2], ALU.add).then_inc(mixed_ready, 1)
                fs.leave(KD, 2)
            with dve.Fori(0, NT) as t:
                dve.wait_ge(mixed_hi, t + 1)
                tokens = bass.ds(P * t, P)
                dve.tensor_tensor(x_lo[:, :, tokens], mixed[:, :, tokens], x_hi[:, :, tokens].bitcast(F32),
                                  ALU.subtract).then_inc(mixed_split, 1)

            def half_tile(t, h):
                return resid[:, bass.ds(t, 1), h * HALF:(h + 1) * HALF].rearrange("p o n -> p (o n)")

            def residual(t, s, h):
                dve.wait_ge(f_prod, t + 1 + NT * h)
                dve.scalar_tensor_tensor(half_tile(t, h), half_tile(t, h), ALPHA, f_gate[:, s], ALU.mult,
                                         ALU.add).then_inc(f_used, 1)

            for n in range(2):
                dve.wait_ge(wo_part, n + 1)
                dve.tensor_tensor(wo_lo[:, n], w_raw[:, n], wo_hi[:, n].bitcast(F32), ALU.subtract).then_inc(wo_split, 1)
            dve.sem_inc(f_used, 4)
            dve.wait_ge(x_loaded[0], 16)
            with dve.Fori(0, NT // 4) as i:
                for s in range(4):
                    residual(4 * i + s, s, 0)
            dve.wait_ge(f_used, NT + 4)
            dve.wait_ge(x_loaded[1], 16)
            for t in range(NT):
                dve.wait_ge(out_done, t + 1)
                bank = (acc if t < 4 else aux)[:, t % 4]
                dve.tensor_tensor(half_tile(t, 0), half_tile(t, 0), bank, ALU.add).then_inc(out_taken, 1)
                dve.wait_ge(out_taken, t + 1)
                fs.step(dve.bn_stats(ln_stats[:, t, 0], half_tile(t, 0)))
                residual(t, t % 4, 1)
            dve.wait_ge(f_used, 2 * NT + 4)
            dve.wait_ge(ln_loaded, 16)
            for t in range(NT):
                s = t % 2
                dve.wait_ge(out_done, NT + t + 1)
                bank = (acc if t < 4 else aux)[:, t % 4]
                dve.tensor_tensor(half_tile(t, 1), half_tile(t, 1), bank, ALU.add).then_inc(out_taken, 1)
                dve.wait_ge(out_taken, NT + t + 1)
                fs.step(dve.bn_stats(ln_stats[:, t, 1], half_tile(t, 1)))
                fs.wait()
                fs.step(dve.bn_aggr(ln_mv[:, s], ln_stats[:, t]))
                fs.wait()
                if t >= 2:
                    dve.wait_ge(ln_std_ready, t - 1)
                dve.tensor_scalar(ln_var[:, s:s + 1], ln_mv[:, s, 1:2], 1e-5, None, ALU.add).then_inc(ln_var_ready, 1)
                tile = resid[:, t]
                fs.step(dve.scalar_tensor_tensor(tile, tile, ln_mv[:, s, 0:1], ln_gb[:, 0], ALU.subtract, ALU.mult))
                dve.wait_ge(ln_std_ready, t + 1)
                fs.step(dve.reciprocal(ln_rstd[:, s:s + 1], ln_std[:, s:s + 1]))
                fs.wait()
                dve.scalar_tensor_tensor(tile, tile, ln_rstd[:, s:s + 1], ln_gb[:, 1], ALU.mult, ALU.add).then_inc(ln_done, 1)


def nsa_tables():
    q, k = np.arange(P)[:, None], np.arange(P)[None, :]
    later = np.where(k > q, NEG, 0)
    causal_wide = np.concatenate([np.zeros((P, S - P)), later], 1)
    win_mask = np.concatenate([np.where(k > q, 0, NEG), np.zeros((P, P)), later], 1)
    t = np.arange(S).reshape(NT, P).T[:, :, None]
    c = np.arange(NC)[None, None, :]
    cmp_mask = np.where((c * CMP_STRIDE + CMP_LEN - 1 <= t) & (c < NC - 1), 0, NEG)
    j, cur = np.arange(S // DH)[None, None, :], t // DH
    forced, valid = (j == 0) | (j == cur) | (j == cur - 1), j <= cur
    i = np.arange(16)
    tables = {
        "causal_wide": causal_wide, "win_mask": win_mask, "cmp_mask": cmp_mask,
        "row_valid": (np.arange(P) >= CMP_LEN - 1)[:, None],
        "rank_keep": valid & ~forced, "rank_add": np.where(valid, np.where(forced, -NEG, 0), NEG),
        "earlier": np.broadcast_to(i[None, :] < i[:, None], (P, 16, 16)),
    }
    return {n: a.astype(np.float32) for n, a in tables.items()}


def gdn_tables():
    k, i = np.arange(P)[:, None], np.arange(P)[None, :]
    masks = [(k // (1 << l) == i // (1 << l) - 1) & (k // (2 << l) == i // (2 << l)) for l in range(LEVELS)]
    return {
        "tri": np.stack([k <= i, k > i, k == k + 0 * i], 1).astype(np.float32),
        "level_masks": np.stack(masks, 1).astype(np.float32),
    }


def log_decay(h):
    return np.log1p(-np.exp2(np.float32(-5.0 - h)), dtype=np.float32)


def chunk_decay(h):
    return float(np.exp(np.float32(P) * log_decay(h)))


def ret_tables():
    pos = np.arange(P, dtype=np.float32)
    lg = np.array([log_decay(h) for h in range(HEADS)], np.float32)
    scale = np.float32(P ** -0.5)
    diff = pos[None, :] - pos[:, None]
    decay = np.where(diff[:, None] >= 0, np.exp(np.maximum(diff, 0)[:, None] * lg[None, :, None]), 0) * scale
    inv = np.float32(10000.0) ** (-np.arange(0, P, 2, dtype=np.float32) / np.float32(P))
    ang = np.arange(S, dtype=np.float32)[:, None] * inv[None, :]
    cs = np.stack([np.cos(ang), np.sin(ang)], 1).reshape(NT, P, 2, P // 2).transpose(1, 0, 2, 3)
    return {
        "cos_sin": cs.astype(np.float32),
        "ret_decay": decay.astype(np.float32),
        "q_decay": np.broadcast_to(np.exp((pos + 1)[None, :] * lg[:, None]), (P, HEADS, P)).astype(np.float32),
        "k_decay": (np.exp((P - 1 - pos)[:, None] * lg[None, :]) * scale).astype(np.float32),
    }


def weight_units(w):
    n = w.shape[1] // UC
    return w.reshape(KD, P, n, UC).transpose(2, 1, 0, 3).reshape(n, P, UNIT)


def weight_rows(w):
    return w.reshape(2, P, S).transpose(1, 0, 2).reshape(1, P, UNIT)


def layout(x, p, w_in, gdn_conv_w, w_ple, gdn_a_log, gdn_dt_bias, gdn_norm_w, w_ple_gate,
           nsa_pe_k, nsa_pe_v, nsa_cmp_w1k, nsa_cmp_w2k, nsa_cmp_w1v, nsa_cmp_w2v,
           w_branch_a, w_branch_b, w_branch_c, w_out, ln_g, ln_b):
    w = w_in[0]
    sizes = (512, 512, 512, 512, 1536, 4, 4, 512, 512, 128, 128, 128, 128, 128, 128, 24, 512, 3072)
    names = "rq rk rv rz gqkv gb ga gz nq nkc nvc nks nvs nkw nvw ng nz merge".split()
    ends = np.cumsum(sizes)
    col = {n: w[:, e - z:e] for n, e, z in zip(names, ends, sizes)}
    halves = np.arange(W4).reshape(HEADS, P // 2, 2).transpose(0, 2, 1).reshape(-1)
    pairs = np.arange(W4).reshape(2, 4, 64).transpose(1, 0, 2).reshape(-1)
    small = np.zeros((D, UC), w.dtype)
    small[:, 0:4], small[:, 4:8], small[:, 8:32] = col["gb"], col["ga"], col["ng"]
    units = [
        col["rq"][:, halves], col["rk"][:, halves], col["rv"],
        col["nvs"], col["nvw"], small,
        col["nq"][:, pairs], col["nkc"], col["nvc"], col["nks"], col["nkw"],
        col["rz"], col["gz"], col["nz"][:, pairs],
        col["gqkv"], w_ple_gate[0][:, 0:2 * UC], col["merge"], w_ple_gate[0][:, 2 * UC:],
        w_out[0],
    ]
    weights = weight_units(np.concatenate(units, axis=1))
    w_branch = np.concatenate([w_branch_c[0][pairs], w_branch_b[0], w_branch_a[0]])
    first = np.concatenate([weight_rows(p[0, 0].T), weight_rows(w_ple[0]), weight_units(x[0].T)])
    return {
        "first": first, "weights": weights,
        "w_branch": w_branch.reshape(KB, P, KD, P).transpose(2, 1, 0, 3).reshape(KD, P, UNIT_BR),
        "x_tok": x[0].reshape(NT, P, D).transpose(1, 0, 2),
        "ln_gb": np.broadcast_to(np.stack([ln_g[0], ln_b[0]]), (P, 2, D)),
        "conv_w": gdn_conv_w[0].reshape(CONV_K, 12, P).transpose(2, 1, 0),
        "ident": np.eye(P, dtype=np.float32),
        **ret_tables(), **gdn_tables(), **nsa_tables(),
        "w1": np.stack([w[0].reshape(CMP_LEN // 2, P, P).transpose(1, 0, 2) for w in (nsa_cmp_w1k, nsa_cmp_w1v)], 1),
        "w2": np.stack([nsa_cmp_w2k[0], nsa_cmp_w2v[0]], 1),
        "pe_t": np.stack([pe[0].reshape(CMP_LEN // 2, P).T for pe in (nsa_pe_k, nsa_pe_v)], 1),
        "dt_bias": np.broadcast_to(gdn_dt_bias, (P, HEADS)), "a_log": np.broadcast_to(gdn_a_log, (P, HEADS)),
        "norm_w": gdn_norm_w.reshape(P, 1),
    }


def kernel(**inputs):
    import concourse.bacc as bacc
    from concourse.bass_utils import run_bass_kernel_spmd

    nc = bacc.Bacc("TRN2", target_bir_lowering=False, num_devices=1)
    arrays = {n: np.ascontiguousarray(a) for n, a in layout(**{n: np.asarray(a) for n, a in inputs.items()}).items()}
    io = {n: nc.dram_tensor(n, a.shape, mybir.dt.from_np(a.dtype), kind="ExternalInput").ap() for n, a in arrays.items()}
    out = nc.dram_tensor("out", (1, S, D), F32, kind="ExternalOutput").ap()
    build(nc, io, out)
    r = run_bass_kernel_spmd(nc, [arrays], core_ids=[0])
    return r.results[0]["out"]
```
